# Optimizing a Trainium2 kernel written in Bass

```python
import jax, jax.numpy as jnp
from jax import lax
import numpy as np

D_MODEL = 2048
BATCH = 1
SEQ = 512
DEPTH = 2
DEC_BATCH = 1
DEC_SEQ = 64
PAST_LEN = 256

CHUNK = 64
D_MIX = D_MODEL
HEAD_DIM = 128
D_LRU = D_MIX // 2
LRU_BLOCKS = 8
LRU_BLOCK = D_LRU // LRU_BLOCKS
CONV_W = 4
LRU_C = 8.0
D_BAND = D_MIX // 4
N_BAND_HEADS = D_BAND // HEAD_DIM
BAND_PAST_CHUNKS = 8
BAND_PAST = BAND_PAST_CHUNKS * CHUNK
REL_CLIP = 256
D_DSA = D_MIX - D_LRU - D_BAND
N_DSA_HEADS = D_DSA // HEAD_DIM
N_IDX_HEADS = 16
IDX_DIM = 64
TOPK_MAX = 256
Q_BLOCK = 128
ROPE_THETA = 500000.0
ROPE_FRAC = 4
EPS = 1e-6
NEG = -1e30
SPLITS = (D_LRU, D_LRU, D_BAND, D_BAND, D_BAND, D_BAND, D_DSA, D_DSA, D_DSA, D_DSA,
          N_IDX_HEADS * IDX_DIM, IDX_DIM, N_IDX_HEADS)
D_IN = sum(SPLITS)

kernel_name = 'hybrid_streaming_encoder_step'

def rmsnorm(x, g):
    xf = x.astype(jnp.float32)
    y = xf * lax.rsqrt(jnp.mean(xf * xf, axis=-1, keepdims=True) + EPS)
    return (y * g.astype(jnp.float32)).astype(x.dtype)

def modulate(x, c, g, w_ada, b_ada):
    mod = jnp.dot(jax.nn.silu(c), w_ada) + b_ada
    shift, scale, gate = jnp.split(mod, 3, axis=-1)
    h = rmsnorm(x, g) * (1 + scale[:, None]) + shift[:, None]
    return h, gate[:, None]

def project(h, w_in):
    u = jnp.dot(h, w_in)
    return jnp.split(u, np.cumsum(SPLITS)[:-1].tolist(), axis=-1)

def split_heads(t, n):
    return t.reshape(t.shape[:-1] + (n, t.shape[-1] // n))

def rope_partial(x, pos):
    d = x.shape[-1]
    r = d // ROPE_FRAC
    half = r // 2
    inv = ROPE_THETA ** (-jnp.arange(half, dtype=jnp.float32) / half)
    ang = pos.astype(jnp.float32)[:, None] * inv[None]
    cos = jnp.cos(ang)[:, None, :]
    sin = jnp.sin(ang)[:, None, :]
    xr = x[..., :r].astype(jnp.float32)
    x1, x2 = xr[..., :half], xr[..., half:]
    rot = jnp.concatenate([x1 * cos - x2 * sin, x2 * cos + x1 * sin], axis=-1).astype(x.dtype)
    return jnp.concatenate([rot, x[..., r:]], axis=-1)

def causal_conv(xp, w, b):
    T = xp.shape[1] - (CONV_W - 1)
    acc = xp[:, 0:T] * w[0]
    for j in range(1, CONV_W):
        acc = acc + xp[:, j:j + T] * w[j]
    return acc + b

def rglru(x, h0, w_rg, b_rg, w_ig, b_ig, lam):
    B, T, _ = x.shape
    xb = x.reshape(B, T, LRU_BLOCKS, LRU_BLOCK)
    r = jax.nn.sigmoid(jnp.einsum('btgi,gij->btgj', xb, w_rg).reshape(B, T, D_LRU) + b_rg)
    i = jax.nn.sigmoid(jnp.einsum('btgi,gij->btgj', xb, w_ig).reshape(B, T, D_LRU) + b_ig)
    log_a = -LRU_C * r.astype(jnp.float32) * jax.nn.softplus(-lam.astype(jnp.float32))
    a = jnp.exp(log_a)
    u = jnp.sqrt(-jnp.expm1(2.0 * log_a)) * (i * x).astype(jnp.float32)
    u = u.at[:, 0].add(a[:, 0] * h0)

    def comb(l, rr):
        return (l[0] * rr[0], rr[0] * l[1] + rr[1])

    _, h = lax.associative_scan(comb, (a, u), axis=1)
    return h

def band_attn_prompt(q, k, v, rel_bias):
    B, S, H, D = q.shape
    NC = S // CHUNK
    P = BAND_PAST_CHUNKS
    KB = (P + 1) * CHUNK
    qc = q.reshape(B, NC, CHUNK, H, D)
    pad = ((0, 0), (P * CHUNK, 0), (0, 0), (0, 0))
    kp = jnp.pad(k, pad).reshape(B, NC + P, CHUNK, H, D)
    vp = jnp.pad(v, pad).reshape(B, NC + P, CHUNK, H, D)
    kb = jnp.concatenate([kp[:, j:j + NC] for j in range(P + 1)], axis=2)
    vb = jnp.concatenate([vp[:, j:j + NC] for j in range(P + 1)], axis=2)
    qi = jnp.arange(CHUNK)
    kj = jnp.arange(KB)
    rel = qi[:, None] + P * CHUNK - kj[None]
    bias = rel_bias[:, jnp.clip(rel, -REL_CLIP, REL_CLIP) + REL_CLIP].astype(jnp.float32)
    valid = (jnp.arange(NC)[:, None] - P) * CHUNK + kj[None] >= 0
    s = jnp.einsum('bnqhd,bnkhd->bnhqk', qc, kb).astype(jnp.float32) * HEAD_DIM ** -0.5 + bias
    s = jnp.where(valid[None, :, None, None, :], s, NEG)
    p = jax.nn.softmax(s, axis=-1).astype(v.dtype)
    return jnp.einsum('bnhqk,bnkhd->bnqhd', p, vb).reshape(B, S, H * D)

def band_attn_sample(q, k, v, rel_bias, q_pos, k_pos):
    B, T = q.shape[:2]
    rel = q_pos[:, None] - k_pos[None]
    bias = rel_bias[:, jnp.clip(rel, -REL_CLIP, REL_CLIP) + REL_CLIP].astype(jnp.float32)
    s = jnp.einsum('bqhd,bkhd->bhqk', q, k).astype(jnp.float32) * HEAD_DIM ** -0.5 + bias
    p = jax.nn.softmax(s, axis=-1).astype(v.dtype)
    return jnp.einsum('bhqk,bkhd->bqhd', p, v).reshape(B, T, -1)

def dsa_attend(q, qi, w, k, v, ki, q_pos, k_pos, topk):
    sc = jnp.einsum('thd,sd->ths', qi, ki).astype(jnp.float32) * IDX_DIM ** -0.5
    score = jnp.einsum('ths,th->ts', jax.nn.relu(sc), w.astype(jnp.float32))
    adm = (k_pos[None, :] // CHUNK) <= (q_pos[:, None] // CHUNK)
    score = jnp.where(adm, score, NEG)
    vals, idx = lax.top_k(score, topk)
    sel = vals > NEG * 0.5
    ks = k[idx]
    vs = v[idx]
    s = jnp.einsum('thd,tkhd->htk', q, ks).astype(jnp.float32) * HEAD_DIM ** -0.5
    s = jnp.where(sel[None], s, NEG)
    p = jax.nn.softmax(s, axis=-1).astype(v.dtype)
    return jnp.einsum('htk,tkhd->thd', p, vs)

def dsa_prompt(q, qi, w, k, v, ki, topk):
    B, S = q.shape[:2]
    nb = S // Q_BLOCK
    pos = jnp.arange(S)

    def to_blocks(a):
        return jnp.moveaxis(a.reshape((B, nb, Q_BLOCK) + a.shape[2:]), 1, 0)

    def one_block(args):
        qb, qib, wb, pb = args
        f = lambda qq, qqi, ww, kk, vv, kki: dsa_attend(qq, qqi, ww, kk, vv, kki, pb, pos, topk)
        return jax.vmap(f)(qb, qib, wb, k, v, ki)

    o = lax.map(one_block, (to_blocks(q), to_blocks(qi), to_blocks(w), pos.reshape(nb, Q_BLOCK)))
    return jnp.moveaxis(o, 0, 1).reshape(B, S, -1)

def dsa_sample(q, qi, w, k, v, ki, q_pos, k_pos, topk):
    o = lax.map(lambda a: dsa_attend(a[0], a[1], a[2], a[3], a[4], a[5], q_pos, k_pos, topk),
                (q, qi, w, k, v, ki))
    return o.reshape(q.shape[0], q.shape[1], -1)

def merge(oa, ob, oc, za, zb, zc, g_branch, w_out):
    ga = g_branch[:D_LRU]
    gb = g_branch[D_LRU:D_LRU + D_BAND]
    gc = g_branch[D_LRU + D_BAND:]
    y = jnp.concatenate([rmsnorm(oa, ga) * jax.nn.silu(za),
                         rmsnorm(ob, gb) * jax.nn.silu(zb),
                         rmsnorm(oc, gc) * jax.nn.silu(zc)], axis=-1)
    return jnp.dot(y, w_out)

def prompt_layer(x, c, lp):
    (g_n, w_a, b_a, w_i, cw, cb, wrg, brg, wig, big, lam, relb, gbr, w_o) = lp
    B, S, _ = x.shape
    pos = jnp.arange(S)
    h, gate = modulate(x, c, g_n, w_a, b_a)
    xa, za, qb, kb, vb, zb, qc, kc, vc, zc, qi, ki, wi = project(h, w_i)
    xpad = jnp.concatenate([jnp.zeros((B, CONV_W - 1, D_LRU), xa.dtype), xa], axis=1)
    hs = rglru(causal_conv(xpad, cw, cb), jnp.zeros((B, D_LRU), jnp.float32), wrg, brg, wig, big, lam)
    qb = split_heads(qb, N_BAND_HEADS)
    kb = split_heads(kb, N_BAND_HEADS)
    vb = split_heads(vb, N_BAND_HEADS)
    ob = band_attn_prompt(qb, kb, vb, relb)
    qc = rope_partial(split_heads(qc, N_DSA_HEADS), pos)
    kc = rope_partial(split_heads(kc, N_DSA_HEADS), pos)
    vc = split_heads(vc, N_DSA_HEADS)
    qi = rope_partial(split_heads(qi, N_IDX_HEADS), pos)
    ki = rope_partial(ki[:, :, None], pos)[:, :, 0]
    oc = dsa_prompt(qc, qi, wi * N_IDX_HEADS ** -0.5, kc, vc, ki, min(TOPK_MAX, S // 4))
    out = merge(hs.astype(x.dtype), ob, oc, za, zb, zc, gbr, w_o)
    nbr = min(BAND_PAST, S)
    new = (xpad[:, -(CONV_W - 1):], hs[:, -1], kb[:, -nbr:], vb[:, -nbr:], kc, vc, ki)
    return x + gate * out, new

def sample_layer(x, c, st, lp):
    (g_n, w_a, b_a, w_i, cw, cb, wrg, brg, wig, big, lam, relb, gbr, w_o) = lp
    conv_s, lru_s, bk, bv, dk, dv, dik = st
    B, T, _ = x.shape
    P = dk.shape[1]
    W = bk.shape[1]
    pos = P + jnp.arange(T)
    h, gate = modulate(x, c, g_n, w_a, b_a)
    xa, za, qb, kb, vb, zb, qc, kc, vc, zc, qi, ki, wi = project(h, w_i)
    xpad = jnp.concatenate([conv_s.astype(xa.dtype), xa], axis=1)
    hs = rglru(causal_conv(xpad, cw, cb), lru_s.astype(jnp.float32), wrg, brg, wig, big, lam)
    qb = split_heads(qb, N_BAND_HEADS)
    kb = split_heads(kb, N_BAND_HEADS)
    vb = split_heads(vb, N_BAND_HEADS)
    kb_all = jnp.concatenate([bk.astype(kb.dtype), kb], axis=1)
    vb_all = jnp.concatenate([bv.astype(vb.dtype), vb], axis=1)
    ob = band_attn_sample(qb, kb_all, vb_all, relb, pos, P - W + jnp.arange(W + T))
    qc = rope_partial(split_heads(qc, N_DSA_HEADS), pos)
    kc = rope_partial(split_heads(kc, N_DSA_HEADS), pos)
    vc = split_heads(vc, N_DSA_HEADS)
    qi = rope_partial(split_heads(qi, N_IDX_HEADS), pos)
    ki = rope_partial(ki[:, :, None], pos)[:, :, 0]
    L = P + T
    kc_all = jnp.concatenate([dk.astype(kc.dtype), kc], axis=1)
    vc_all = jnp.concatenate([dv.astype(vc.dtype), vc], axis=1)
    ki_all = jnp.concatenate([dik.astype(ki.dtype), ki], axis=1)
    oc = dsa_sample(qc, qi, wi * N_IDX_HEADS ** -0.5, kc_all, vc_all, ki_all, pos, jnp.arange(L),
                    min(TOPK_MAX, L // 4))
    out = merge(hs.astype(x.dtype), ob, oc, za, zb, zc, gbr, w_o)
    new = (xpad[:, -(CONV_W - 1):], hs[:, -1], kb, vb, kc, vc, ki)
    return x + gate * out, new

def setup_inputs(seed: int = 0) -> dict:
    key = jax.random.key(seed)
    ks = jax.random.split(key, 32)
    f32 = jnp.float32

    def nrm(k, shape, s):
        return jax.random.normal(k, shape, f32) * s

    band_rows = min(BAND_PAST, PAST_LEN)
    return {
        'x_prompt': nrm(ks[0], (BATCH, SEQ, D_MODEL), 1.0),
        'x_sample': nrm(ks[1], (DEC_BATCH, DEC_SEQ, D_MODEL), 1.0),
        'c_prompt': nrm(ks[2], (BATCH, D_MODEL), 1.0),
        'c_sample': nrm(ks[3], (DEC_BATCH, D_MODEL), 1.0),
        'state_conv': nrm(ks[4], (DEPTH, DEC_BATCH, CONV_W - 1, D_LRU), 1.0),
        'state_lru': nrm(ks[5], (DEPTH, DEC_BATCH, D_LRU), 0.5),
        'cache_band_k': nrm(ks[6], (DEPTH, DEC_BATCH, band_rows, N_BAND_HEADS, HEAD_DIM), 1.0),
        'cache_band_v': nrm(ks[7], (DEPTH, DEC_BATCH, band_rows, N_BAND_HEADS, HEAD_DIM), 1.0),
        'cache_dsa_k': nrm(ks[8], (DEPTH, DEC_BATCH, PAST_LEN, N_DSA_HEADS, HEAD_DIM), 1.0),
        'cache_dsa_v': nrm(ks[9], (DEPTH, DEC_BATCH, PAST_LEN, N_DSA_HEADS, HEAD_DIM), 1.0),
        'cache_dsa_idx_k': nrm(ks[10], (DEPTH, DEC_BATCH, PAST_LEN, IDX_DIM), 1.0),
        'g_norm': 1.0 + nrm(ks[11], (DEPTH, D_MODEL), 0.02),
        'w_ada': nrm(ks[12], (DEPTH, D_MODEL, 3 * D_MODEL), 0.5 * D_MODEL ** -0.5),
        'b_ada': nrm(ks[13], (DEPTH, 3 * D_MODEL), 0.02),
        'w_in': nrm(ks[14], (DEPTH, D_MODEL, D_IN), D_MODEL ** -0.5),
        'conv_w': nrm(ks[15], (DEPTH, CONV_W, D_LRU), CONV_W ** -0.5),
        'conv_b': nrm(ks[16], (DEPTH, D_LRU), 0.02),
        'w_rg': nrm(ks[17], (DEPTH, LRU_BLOCKS, LRU_BLOCK, LRU_BLOCK), LRU_BLOCK ** -0.5),
        'b_rg': nrm(ks[18], (DEPTH, D_LRU), 0.02),
        'w_ig': nrm(ks[19], (DEPTH, LRU_BLOCKS, LRU_BLOCK, LRU_BLOCK), LRU_BLOCK ** -0.5),
        'b_ig': nrm(ks[20], (DEPTH, D_LRU), 0.02),
        'lru_lambda': jax.random.uniform(ks[21], (DEPTH, D_LRU), f32, 4.3, 9.0),
        'rel_bias': nrm(ks[22], (DEPTH, N_BAND_HEADS, 2 * REL_CLIP + 1), 0.5),
        'g_branch': 1.0 + nrm(ks[23], (DEPTH, D_MIX), 0.02),
        'w_out': nrm(ks[24], (DEPTH, D_MIX, D_MODEL), D_MIX ** -0.5),
        'g_final': 1.0 + nrm(ks[25], (D_MODEL,), 0.02),
    }

def reference(x_prompt, x_sample, c_prompt, c_sample, state_conv, state_lru, cache_band_k, cache_band_v,
              cache_dsa_k, cache_dsa_v, cache_dsa_idx_k, g_norm, w_ada, b_ada, w_in, conv_w, conv_b,
              w_rg, b_rg, w_ig, b_ig, lru_lambda, rel_bias, g_branch, w_out, g_final):
    xp = x_prompt
    xs = x_sample
    p_new = []
    s_new = []
    for l in range(DEPTH):
        lp = (g_norm[l], w_ada[l], b_ada[l], w_in[l], conv_w[l], conv_b[l], w_rg[l], b_rg[l],
              w_ig[l], b_ig[l], lru_lambda[l], rel_bias[l], g_branch[l], w_out[l])
        xp, pn = prompt_layer(xp, c_prompt, lp)
        st = (state_conv[l], state_lru[l], cache_band_k[l], cache_band_v[l],
              cache_dsa_k[l], cache_dsa_v[l], cache_dsa_idx_k[l])
        xs, sn = sample_layer(xs, c_sample, st, lp)
        p_new.append(pn)
        s_new.append(sn)
    y_prompt = rmsnorm(xp, g_final)
    y_sample = rmsnorm(xs, g_final)
    p_conv, p_lru, p_band_k, p_band_v, p_dsa_k, p_dsa_v, p_dsa_idx_k = [
        jnp.stack([t[j] for t in p_new], axis=0) for j in range(7)]
    s_conv, s_lru, s_band_k, s_band_v, s_dsa_k, s_dsa_v, s_dsa_idx_k = [
        jnp.stack([t[j] for t in s_new], axis=0) for j in range(7)]
    return (y_prompt, y_sample, p_conv, p_lru, p_band_k, p_band_v, p_dsa_k, p_dsa_v, p_dsa_idx_k,
            s_conv, s_lru, s_band_k, s_band_v, s_dsa_k, s_dsa_v, s_dsa_idx_k)


_drawn_inputs = setup_inputs


def setup_inputs(seed=0):
    import zlib

    import numpy as np

    out = dict(_drawn_inputs(seed))
    spreads = {}
    factors = {'b_rg': 8.0, 'b_ig': 7.882, 'g_branch': 6.601, 'g_final': 2.725}
    for name, (base, spread) in spreads.items():
        noise = np.random.default_rng([zlib.crc32(name.encode()), seed]).standard_normal(out[name].shape)
        drawn = base * np.exp(spread * noise) if base else spread * noise
        out[name] = __import__('jax').numpy.asarray(drawn.astype(out[name].dtype))
    for name, factor in factors.items():
        out[name] = (out[name] * factor).astype(out[name].dtype)
    return out
```

```python
from contextlib import ExitStack

import concourse.bass as bass
import numpy as np
from concourse import mybir

F32 = mybir.dt.float32
F32R = mybir.dt.float32r
BF16 = mybir.dt.bfloat16
ALU = mybir.AluOpType
ACT = mybir.ActivationFunctionType
AX = mybir.AxisListType

P = 128
D_MODEL, SEQ, DEC, PAST, DEPTH = 2048, 512, 64, 256, 2
KT = D_MODEL // P
T = SEQ + DEC
HALF = T // 2
D_LRU, HEADS, HD = 1024, 4, 128
G = D_LRU // P
IDX_HEADS, IDX_DIM, TOPK, TOPK_S = 16, 64, 128, 80
CHUNK, CONV_W, EPS, NEG, TAKEN = 64, 4, 1e-6, -1e30, -3e38
REL = 256
D_IN = 7248
SCALE = float(HD) ** -0.5
IDX_SCALE = float(IDX_DIM) ** -0.5 * float(IDX_HEADS) ** -0.5
ROPE_THETA = 500000.0

KI = 0
QI = 1
LRU = QI + 8
HEAD = LRU + 2 * G
OUT = HEAD + 8 * 4
TILES = OUT + KT
RING = 4
KC = 4
CHUNKS = TILES * 4
USES = ((TILES + 1) // 2, TILES // 2)
COL_KI = 7168
COLS = {"qi": 6144, "xa": 0, "za": 1024}
ADA = 3 * KT
AB = 512
ADA_BLOCKS = ADA * P // AB
NEW_K = SEQ + PAST
KEYS = NEW_K + DEC
NS = PAST + DEC
W = SEQ + 3 + DEC + 1
S0 = SEQ + 3
WH = W // 2
ACC = {1: 0, 2: 256, 3: 640, 4: 1152}
SEL = {0: 0, 1: 128, 2: 384, 3: 768, 4: 1280}
NK = {0: 128, 1: 256, 2: 384, 3: 512, 4: NS}
NQ = {0: P, 1: P, 2: P, 3: P, 4: DEC}

V1 = {"b_ada": 0, "g_norm": 48, "conv_w": 64, "conv_b": 96, "b_rg": 104, "b_ig": 112, "lam": 120}
V2 = {"g_branch": 0, "state_lru": 16, "state_conv": 24}
V0 = {"c_prompt": 0, "c_sample": 16, "g_final": 32}


def head_col(h, part):
    return 2048 + (h // HEADS) * 2048 + part * 512 + (h % HEADS) * P


def build(nc, inp, out, scratch):
    with ExitStack() as ctx:
        def sb(name, shape, dt=F32):
            return ctx.enter_context(nc.sbuf_tensor(name, shape, dt))

        started = []
        start = {}

        def sem(name, at=0):
            start[name] = at
            s = ctx.enter_context(nc.semaphore(name))
            if at:
                started.append((s, at))
            return s

        xy = sb("xy", [P, KT, T])
        act_hi = sb("act_hi", [P, KT, T], F32R)
        act_lo = sb("act_lo", [P, KT, T], F32R)
        raw = sb("raw", [P, RING, KC, P])
        w_hi = sb("w_hi", [P, RING, KC, P], F32R)
        w_lo = sb("w_lo", [P, RING, KC, P], F32R)
        work = sb("work", [P, 8192])
        lbf = sb("lb", [P, 3 * 584])
        rope = sb("rope", [P, 2, T])
        ki_t = sb("ki_t", [P, KEYS])
        qi_raw = sb("qi_raw", [P, T])
        acc = sb("acc", [P, 1472])
        selm = sb("selm", [P, 1600], BF16)
        kw_tok = sb("kw_tok", [P, 5, 80])
        ci = sb("ci", [P, 2, IDX_DIM])
        top8 = sb("top8", [P, 3, 8])
        w_rg = sb("w_rg", [P, P])
        w_ig = sb("w_ig", [P, P])
        sq = sb("sq", [P, T])
        sqb = sb("sqb", [P, 3, T])
        sqx = sqb[:, 0, :]
        ident = sb("ident", [P, P])
        ones = sb("ones", [P, P])
        swap_i = sb("swap_i", [P, P])
        swap_d = sb("swap_d", [32, 32])
        vec1 = sb("vec1", [P, P])
        vec2 = sb("vec2", [P, 48])
        vec0 = sb("vec0", [P, 48])
        sc = sb("sc", [P, KT, 2])
        mod = sb("mod", [P, ADA, 2])
        hg = sb("hg", [P, KT])
        hb = sb("hb", [P, 2, G])
        sp_ = sb("sp", [P, 6, G])
        stat = sb("stat", [P, 8, G])
        stat_r = sb("stat_r", [64, P])
        nmx = sb("nmx", [P, 2])
        rsum = sb("rsum", [P, 2])
        rinv = sb("rinv", [P, 2])

        at = 0

        def cut(n):
            nonlocal at
            at += n
            return work[:, at - n:at]

        q_t = [cut(T) for _ in range(2)]
        k_t = [cut(KEYS) for _ in range(2)]
        s_sb = [cut(512) for _ in range(2)]
        v_t = cut(T)
        qi_rot = v_t
        ck = cut(2 * P).rearrange("p (b n) -> p b n", b=2)
        cv = cut(2 * P).rearrange("p (b n) -> p b n", b=2)
        bias = cut(512)
        first = at
        p_t = [cut(512) for _ in range(2)]
        v_tok = cut(5 * P).rearrange("p (b n) -> p b n", b=5)
        k_tok = cut(5 * P).rearrange("p (b n) -> p b n", b=5)
        lb = [work[:, first + n * 584:first + (n + 1) * 584] for n in range(2)] \
            + [lbf[:, n * 584:(n + 1) * 584] for n in range(3)] \
            + [work[:, first + 2 * 584:first + 3 * 584]]
        vrow = lb[4][:, 0:2 * P].rearrange("p (a n) -> p a n", a=2)
        d_rot = lb[3]
        ada_w = work[:, :].rearrange("p (s k n) -> p s k n", s=4, k=KC)
        ada_row = [sqb[0:2, n, 0:AB] for n in (1, 2)]
        x_row = work[:, :].rearrange("p (s n) -> p s n", s=4)
        x_old = [work[:, n * T:(n + 1) * T] for n in range(4)]
        y_row = [work[:, 2048 + 2048 * j:4096 + 2048 * j] for j in range(2)]
        h_f = [lb[0][:, 0:T], lb[1][:, 0:T]]
        r_x = lb[2][:, 0:T]
        r_b = [lb[2 + j][:, 0:T] for j in range(3)]
        z_t = qi_raw

        proj = [ctx.enter_context(nc.psum_tensor(f"proj{b}", [P, 2, 512], F32)) for b in range(2)]
        misc = ctx.enter_context(nc.psum_tensor("misc", [P, 4, 512], F32))
        s_ps = [misc[:, 0, :], misc[:, 1, :]]
        t_ps = misc[:, 2, :]
        o_ps = misc[:, 3, :]

        const_in = sem("const_in")
        x_in = [sem(f"x_in{s}") for s in range(4)]
        xt_made = sem("xt_made")
        xt_read = sem("xt_read")
        x_kept = sem("x_kept")
        x_whole = sem("x_whole")
        c_row_made = sem("c_row_made")
        c_ready = sem("c_ready")
        vec_in = sem("vec_in")
        vec_made = sem("vec_made")
        vec_ready = sem("vec_ready")
        ada_in = [sem(f"ada_in{s}") for s in range(4)]
        ada_used = sem("ada_used")
        ada_read = sem("ada_read", 2)
        ada_turned = sem("ada_turned", 2)
        mod_ready = sem("mod_ready")
        ss_made = sem("ss_made")
        ms_ready = sem("ms_ready")
        r_ready = sem("r_ready")
        norm_x = sem("norm_x")
        pad_ready = sem("pad_ready")
        h_split = sem("h_split")
        h_ready = sem("h_ready")
        raw_in = [sem(f"raw_in{s}") for s in range(RING)]
        hi_ready = sem("hi_ready")
        lo_ready = sem("lo_ready", RING)
        chunks_used = sem("chunks_used", RING)
        bank_free = [sem(f"bank_free{b}", 1) for b in range(2)]
        evac = sem("evac")
        swapped = sem("swapped")
        roped = sem("roped")
        rope_in = sem("rope_in")
        ci_in = sem("ci_in")
        ki_ready = sem("ki_ready")
        s_made = sem("s_made")
        s_read = sem("s_read", 1)
        idx_made = sem("idx_made", 1)
        idx_read = sem("idx_read", 1)
        relu_made = sem("relu_made")
        relu_used = sem("relu_used", 1)
        sel_ready = sem("sel_ready")
        t_made = sem("t_made", 1)
        t_read = sem("t_read", 1)
        exp_made = sem("exp_made")
        y_neg = sem("y_neg", 1)
        p_ready = sem("p_ready")
        o_made = sem("o_made", 1)
        o_read_a = sem("o_read_a", 1)
        o_read_v = sem("o_read_v", 1)
        zs_ready = sem("zs_ready", 1)
        gate_w_in = sem("gate_w_in")
        conv_ready = sem("conv_ready", 1)
        gates_made = sem("gates_made", 1)
        gates_read = sem("gates_read", 1)
        root_made = sem("root_made")
        hs_ready = sem("hs_ready", 1)
        hs_sq = sem("hs_sq")
        sq_made = sem("sq_made")
        sq_used = sem("sq_used", 1)
        bias_in = sem("bias_in")
        bias_ready = sem("bias_ready")
        ck_in = sem("ck_in")
        cv_in = sem("cv_in")
        ki_out = sem("ki_out", 16)
        tok_out = sem("tok_out", 16)
        sqc_ready = sem("sqc_ready")
        stat_ready = sem("stat_ready")
        stat_out = sem("stat_out", 16)
        old_in = [sem(f"old_in{s}") for s in range(4)]
        rel_rows = sem("rel_rows")
        rel_out = sem("rel_out")
        lam_exp = sem("lam_exp")
        x_new = sem("x_new")
        yn_made = sem("yn_made")
        yt_made = sem("yt_made")
        yt_read = sem("yt_read")
        y_out = [sem(f"y_out{s}") for s in range(2)]
        ticks = sem("ticks")

        def hold(eng, s, value):
            eng.wait_ge(s, value + start[s.name])
            eng.sem_inc(ticks, 1)

        def chunk_no(l, t, c):
            return l * CHUNKS + t * 4 + c

        def tile_made(eng, l, t):
            hold(eng, chunks_used, chunk_no(l, t, 4))

        block = ctx.enter_context(nc.Block())

        def wide(ps, n=HALF):
            return ps[:, :, 0:n]

        def halves(ap):
            return ap.rearrange("p (a n) -> p a n", a=2)

        def q_cols(b):
            return slice(b * P, b * P + NQ[b])

        def key_cols(b):
            return slice(0, NK[b]) if b < 4 else slice(SEQ, KEYS)

        PARTS = ((0, SEQ, 0), (SEQ, T, 1))
        T_EV = 3 + 8 * 8
        SQ_U = 32
        TOK = 32 * 16
        CONSTS = 8

        @block.sync
        def _(sp):
            for s, n in started:
                sp.sem_inc(s, n)
            for dst, src in (
                (ident[:, :], inp["ident"]), (swap_i[:, :], inp["swap_i"]), (swap_d[:, :], inp["swap_d"]),
                (ones[:, :], inp["ones"]),
                (vrow[0:16, 0, :], inp["c_prompt"].rearrange("a (r p) -> (a r) p", p=P)),
                (vrow[16:32, 0, :], inp["c_sample"].rearrange("a (r p) -> (a r) p", p=P)),
                (vrow[32:48, 0, :], inp["g_final"].rearrange("(r p) -> r p", p=P)),
                (lbf[0:8, 0:384], inp["rel_bias"].rearrange("l h n -> (l h) n")[:, 129:513]),
            ):
                sp.dma_start(dst, src).then_inc(const_in, 16)
            for b in range(5):
                if b == 4:
                    sp.wait_ge(xt_read, 4)
                src = inp["x_prompt"][0, b * P:(b + 1) * P, :] if b < 4 else inp["x_sample"][0]
                sp.dma_start(x_row[0:src.shape[0], b % 4, :], src).then_inc(x_in[b % 4], 16)
            sp.wait_ge(rel_rows, 1)
            sp.dma_start(scratch["rows"], lbf[0:8, 0:640]).then_inc(rel_out, 16)
            sp.wait_ge(rel_out, 16)
            sp.dma_start(scratch["windows"], bass.AP(scratch["rows"].tensor, 0, [[640, 8], [1, P], [1, 512]]))\
                .then_inc(rel_out, 16)
            sp.wait_ge(rel_out, 32)
            sp.dma_start(scratch["windows"][:, 0:CHUNK, 0:CHUNK], inp["blocked"]).then_inc(rel_out, 16)
            sp.wait_ge(x_whole, 1)
            sp.dma_start(scratch["x_keep"][0], xy[:, :, :]).then_inc(x_kept, 16)
            sp.wait_ge(rel_out, 48)

            with sp.Fori(0, DEPTH) as l:
                hold(sp, vec_made, l + 1)
                hold(sp, x_whole, l + 1)
                for n, (name, row, rows) in enumerate((
                    ("b_ada", V1["b_ada"], ADA), ("g_norm", V1["g_norm"], KT),
                    ("conv_w", V1["conv_w"], 4 * G), ("conv_b", V1["conv_b"], G),
                    ("b_rg", V1["b_rg"], G), ("b_ig", V1["b_ig"], G), ("lru_lambda", V1["lam"], G),
                    ("g_branch", V2["g_branch"], KT), ("state_lru", V2["state_lru"], G),
                    ("state_conv", V2["state_conv"], 3 * G),
                )):
                    src = inp[name][l]
                    src = {1: lambda a: a.rearrange("(r p) -> r p", p=P),
                           2: lambda a: a.rearrange("a (r p) -> (a r) p", p=P),
                           3: lambda a: a.rearrange("a b (r p) -> (a b r) p", p=P)}[len(src.shape)](src)
                    sp.dma_start(vrow[row:row + rows, int(n > 6), :], src).then_inc(vec_in, 16)
                hold(sp, tok_out, l * TOK)
                w_ada = inp["w_ada"][l].rearrange("(k p) n -> p k n", p=P)

                def load_ada(s, col):
                    sp.dma_start(ada_w[:, s], w_ada[:, s * KC:(s + 1) * KC, bass.ds(col, AB)])\
                        .then_inc(ada_in[s], 16)

                for s in range(4):
                    load_ada(s, 0)
                with sp.Fori(1, ADA_BLOCKS) as j:
                    for s in range(4):
                        hold(sp, ada_used, (l * ADA_BLOCKS + j) * 4 + (s - 3))
                        load_ada(s, j * AB)
                sp.dma_start(rope[:, :, :], inp["rope_i"]).then_inc(rope_in, 16)
                sp.dma_start(ci[:, :, :], inp["cache_dsa_idx_k"][l, 0].rearrange("(b p) n -> p b n", p=P))\
                    .then_inc(ci_in, 16)

                w_in = inp["w_in"][l].rearrange("(k p) n -> p k n", p=P)
                w_out = inp["w_out"][l].rearrange("(k p) n -> p k n", p=P)

                def load(w, t, col, width=P):
                    for c in range(4):
                        hold(sp, lo_ready, chunk_no(l, t, c) + 1 - RING)
                        sp.dma_start(raw[:, c, :, 0:width],
                                     w[:, c * KC:(c + 1) * KC, bass.ds(col, width)]).then_inc(raw_in[c], 16)

                load(w_in, KI, COL_KI, 80)
                with sp.Fori(0, 8) as q:
                    load(w_in, QI + q, COLS["qi"] + q * P)
                with sp.Fori(0, G) as g:
                    load(w_in, LRU + 2 * g, COLS["xa"] + g * P)
                    hold(sp, gates_made, l * G + g)
                    sp.dma_start(w_rg[:, :], inp["w_rg"][l, g]).then_inc(gate_w_in, 16)
                    sp.dma_start(w_ig[:, :], inp["w_ig"][l, g]).then_inc(gate_w_in, 16)
                    load(w_in, LRU + 1 + 2 * g, COLS["za"] + g * P)

                def load_head_extras(h, values):
                    kind = "band" if h < HEADS else "dsa"
                    if values:
                        hold(sp, o_made, (l * 8 + h) * 5)
                    else:
                        hold(sp, y_neg, (l * 8 + h) * 5)
                        if h < HEADS:
                            sp.dma_start(bias, scratch["windows"][l * HEADS + h]).then_inc(bias_in, 16)
                    src = inp[f"cache_{kind}_{'v' if values else 'k'}"][l, 0, :, h % HEADS, :]
                    sp.dma_start(cv if values else ck, src.rearrange("(b p) n -> p b n", p=P))\
                        .then_inc(cv_in if values else ck_in, 16)

                for h in range(8):
                    load(w_in, HEAD + 4 * h, head_col(h, 0))
                    if h > 0:
                        load_head_extras(h - 1, False)
                    if h == HEADS - 1:
                        sp.dma_start(rope[0:32, :, :], inp["rope_d"]).then_inc(rope_in, 16)
                    load(w_in, HEAD + 4 * h + 1, head_col(h, 1))
                    load(w_in, HEAD + 4 * h + 2, head_col(h, 2))
                    if h > 0:
                        load_head_extras(h - 1, True)
                    load(w_in, HEAD + 4 * h + 3, head_col(h, 3))
                load_head_extras(7, False)
                load(w_out, OUT, 0)
                load_head_extras(7, True)
                hold(sp, o_made, (l + 1) * 40)
                for s in range(4):
                    sp.dma_start(x_old[s], scratch["x_keep"][l, :, s]).then_inc(old_in[s], 16)
                for j in range(1, 4):
                    load(w_out, OUT + j, j * P)
                with sp.Fori(1, 4) as jj:
                    for s in range(4):
                        hold(sp, x_new, l * KT + 4 * jj + (s - 3))
                        sp.dma_start(x_old[s], scratch["x_keep"][l, :, 4 * jj + s]).then_inc(old_in[s], 16)
                        load(w_out, OUT + s + 4 * jj, jj * 512 + s * P)

            for b in range(5):
                sp.wait_ge(yt_read, 4 * (b + 1))
                n = P if b < 4 else DEC
                dst = out["y_prompt"][0, b * P:(b + 1) * P, :] if b < 4 else out["y_sample"][0]
                sp.dma_start(dst, y_row[b % 2][0:n, :]).then_inc(y_out[b % 2], 16)
            sp.wait_ge(y_out[0], 48)
            sp.wait_ge(y_out[1], 32)
            hold(sp, tok_out, DEPTH * TOK)
            hold(sp, ki_out, DEPTH * 32)
            hold(sp, stat_out, DEPTH * 64)
            sp.wait_ge(x_kept, 16 + DEPTH * KT * 16)

        @block.gpsimd
        def _(pool):
            def split(l, t, width=P):
                for c in range(4):
                    pool.wait_ge(hi_ready, chunk_no(l, t, c) + 1)
                    pool.tensor_tensor(w_lo[:, c, :, 0:width], raw[:, c, :, 0:width],
                                       w_hi[:, c, :, 0:width].bitcast(F32), ALU.subtract)\
                        .then_inc(lo_ready, 1)

            with pool.Fori(0, DEPTH) as l:
                split(l, KI, 80)
                with pool.Fori(1, TILES) as t:
                    split(l, t)

        @block.tensor
        def _(pe):
            pe.wait_ge(const_in, CONSTS * 16)
            pe.transpose(proj[0][:, 0, 0:48], vrow[0:48, 0, :], ident[0:48, 0:48]).then_inc(vec_made, 1)
            for b in range(5):
                n = P if b < 4 else DEC
                pe.wait_ge(x_in[b % 4], 16 * (b // 4 + 1))
                for k4 in range(4):
                    e = 4 * b + k4
                    if e >= 4:
                        pe.wait_ge(xt_read, e - 3)
                    for k in range(4):
                        m = pe.transpose(misc[:, e % 4, k * P:k * P + n],
                                         x_row[0:n, b % 4, (4 * k4 + k) * P:(4 * k4 + k + 1) * P],
                                         ident[0:n, 0:n])
                    m.then_inc(xt_made, 1)

            def sum_squares(ps, src):
                for half in range(2):
                    m = pe.matmul(ps[:, half, 0:HALF], ones[:, :], src[:, half * HALF:(half + 1) * HALF],
                                  start=True, stop=True)
                m.then_inc(ss_made, 1)

            with pe.Fori(0, DEPTH) as l:
                hold(pe, vec_in, (l + 1) * 160)
                hold(pe, x_whole, l + 1)
                pe.transpose(t_ps[:, 0:P], vrow[:, 0, :], ident[:, :])
                pe.transpose(o_ps[:, 0:48], vrow[0:48, 1, :], ident[0:48, 0:48]).then_inc(vec_made, 1)
                hold(pe, bank_free[0], l * USES[0])
                sum_squares(proj[0], sqx)
                pe.wait_ge(c_ready, 1)

                def modulate(j, n):
                    hold(pe, ada_read, l * ADA_BLOCKS + j - 1)
                    for s in range(4):
                        hold(pe, ada_in[s], (l * ADA_BLOCKS + j + 1) * 16)
                        for kk in range(KC):
                            k = s * KC + kk
                            m = pe.matmul(s_ps[n][0:2, :], sc[:, k, :], ada_w[:, s, kk, :],
                                          start=(k == 0), stop=(k == KT - 1))
                        m.then_inc(ada_used, 1)

                def turn_modulation(j, n):
                    hold(pe, ada_read, l * ADA_BLOCKS + j + 1)
                    for i in range(AB // P):
                        m = pe.matmul(t_ps[:, bass.ds(j * 8 + 2 * i, 2)], ada_row[n][:, i * P:(i + 1) * P],
                                      ident[0:2, 0:2], start=True, stop=True)
                    m.then_inc(ada_turned, 1)

                modulate(0, 0)
                hold(pe, vec_ready, l + 1)
                with pe.Fori(0, ADA_BLOCKS // 2 - 1) as i:
                    modulate(2 * i + 1, 1)
                    turn_modulation(2 * i, 0)
                    modulate(2 * i + 2, 0)
                    turn_modulation(2 * i + 1, 1)
                modulate(ADA_BLOCKS - 1, 1)
                turn_modulation(ADA_BLOCKS - 2, 0)
                turn_modulation(ADA_BLOCKS - 1, 1)

                def chunks(t, b, use, cs, width=P, acts=None):
                    for c in cs:
                        if c == 0:
                            pe.wait_ge(bank_free[b], l * USES[b] + use + 1)
                        if acts is not None:
                            pe.wait_ge(h_ready, l * 2 * KT + acts + (c + 1) * KC)
                        pe.wait_ge(lo_ready, chunk_no(l, t, c) + 1 + RING)
                        for kk in range(KC):
                            k = c * KC + kk
                            for half in range(2):
                                cols = slice(half * HALF, (half + 1) * HALF)
                                dst = proj[b][0:width, half, 0:HALF]
                                pe.matmul(dst, w_hi[:, c, kk, 0:width], act_hi[:, k, cols],
                                          start=(k == 0), stop=False)
                                pe.matmul(dst, w_hi[:, c, kk, 0:width], act_lo[:, k, cols],
                                          start=False, stop=False)
                            for half in range(2):
                                cols = slice(half * HALF, (half + 1) * HALF)
                                m = pe.matmul(proj[b][0:width, half, 0:HALF], w_lo[:, c, kk, 0:width],
                                              act_hi[:, k, cols], start=False, stop=(k == KT - 1))
                        m.then_inc(chunks_used, 1)

                def swap(t_evac, b, perm, src, n, keys=None):
                    hold(pe, evac, l * OUT + t_evac + 1)
                    for half in range(2):
                        if src is not None:
                            m = pe.matmul(proj[b][0:n, half, 0:HALF], perm,
                                          src[0:n, half * HALF:(half + 1) * HALF], start=True, stop=True)
                        else:
                            a, z = ((0, HALF), (HALF, SEQ))[half]
                            m = pe.matmul(proj[b][0:n, half, 0:z - a], perm, keys[0:n, a:z],
                                          start=True, stop=True)
                    if src is None:
                        m = pe.matmul(proj[b][0:n, 1, SEQ - HALF:HALF], perm, keys[0:n, NEW_K:KEYS],
                                      start=True, stop=True, skip_group_check=True)
                    m.then_inc(swapped, 1)

                def t_event(e):
                    hold(pe, t_read, l * T_EV + e)

                def scores(q, first=False):
                    hold(pe, roped, l * 17 + q + 2)
                    for e, (b, hh) in enumerate((b, hh) for b in (1, 2, 3, 4) for hh in range(2)):
                        hold(pe, idx_read, l * 64 + (8 * q + e - 1 if not first or e > 1 else 0))
                        rows = slice(64 * hh, 64 * hh + 64)
                        pe.matmul(s_ps[e % 2][0:NQ[b], 0:NK[b]], qi_rot[rows, q_cols(b)],
                                  ki_t[rows, key_cols(b)], start=True, stop=True).then_inc(idx_made, 1)

                chunks(KI, 0, 0, range(4), 80, acts=0)
                chunks(QI, 1, 0, (0, 1))
                swap(KI, 0, swap_i[0:64, 0:64], qi_raw, 64)
                hold(pe, ci_in, (l + 1) * 16)
                t_event(0)
                for b in range(2):
                    m = pe.transpose(t_ps[0:64, b * P:(b + 1) * P], ci[:, b, :], ident[:, :])
                m.then_inc(t_made, 1)
                chunks(QI, 1, 0, (2, 3))
                hold(pe, roped, l * 17 + 1)
                t_event(1)
                for b in range(5):
                    m = pe.transpose(t_ps[0:NQ[b], b * 80:b * 80 + 80], qi_raw[0:80, q_cols(b)],
                                     ident[0:80, 0:80])
                m.then_inc(t_made, 1)

                def query_tile(q, b, use, first=False):
                    chunks(QI + q, b, use, (0, 1))
                    swap(QI - 1 + q, 1 - b, swap_i[:, :], qi_raw, P)
                    chunks(QI + q, b, use, (2, 3))
                    if first:
                        hold(pe, ki_ready, l + 1)
                    scores(q - 1, first)

                query_tile(1, 0, 1, True)
                with pe.Fori(0, 3) as it:
                    query_tile(2 * it + 2, 1, it + 1)
                    query_tile(2 * it + 3, 0, it + 2)

                def recurrent_block(g, first=False):
                    chunks(LRU + 2 * g, 1, g + 4, (0, 1))
                    if first:
                        swap(QI + 7, 0, swap_i[:, :], qi_raw, P)
                    chunks(LRU + 2 * g, 1, g + 4, (2, 3))
                    if first:
                        scores(7)
                        hold(pe, idx_read, (l + 1) * 64)
                        t_event(2)
                    chunks(LRU + 1 + 2 * g, 0, g + 5, range(4))
                    hold(pe, gates_read, l * G + g)
                    hold(pe, conv_ready, l * G + g + 1)
                    hold(pe, gate_w_in, (l * G + g + 1) * 32)
                    for n, w in enumerate((w_rg, w_ig)):
                        for half in range(2):
                            m = pe.matmul(misc[:, 2 * n + half, 0:WH], w[:, :],
                                          lb[1][:, half * WH:(half + 1) * WH], start=True, stop=True)
                    m.then_inc(gates_made, 1)

                recurrent_block(0, True)
                with pe.Fori(1, G) as g:
                    recurrent_block(g)

                def head_side(h, s):
                    q, k, e0 = q_t[h % 2], k_t[h % 2], 3 + 8 * h

                    def score(b):
                        if b < 2:
                            hold(pe, s_read, l * 40 + 5 * h)
                        else:
                            hold(pe, s_read, l * 40 + 5 * h + b - 1)
                        pe.matmul(s_ps[b % 2][0:NQ[b], 0:NK[b]], q[:, q_cols(b)], k[:, key_cols(b)],
                                  start=True, stop=True).then_inc(s_made, 1)

                    def turn(b, e):
                        t_event(e0 + e)
                        hold(pe, p_ready, l * 40 + 5 * h + b + 1)
                        for j in range(0, NK[b], P):
                            n = min(P, NK[b] - j)
                            m = pe.transpose(t_ps[0:n, j:j + NQ[b]], s_sb[b % 2][0:NQ[b], j:j + n],
                                             ident[0:NQ[b], 0:NQ[b]])
                        m.then_inc(t_made, 1)

                    def mix(b, e):
                        hold(pe, t_read, l * T_EV + e0 + e + 1)
                        if b in (0, 4):
                            hold(pe, o_read_v, l * 16 + 2 * h + (b == 4))
                            hold(pe, o_read_a, l * 16 + 2 * h + (b == 4))
                        if b == 4:
                            hold(pe, cv_in, (l * 8 + h + 1) * 16)
                            vs = [cv[:, 0, :], cv[:, 1, :], v_tok[0:DEC, 4, :]]
                        else:
                            vs = [v_tok[:, j, :] for j in range(b + 1)]
                        for j, v in enumerate(vs):
                            c = (b % 4) * P
                            m = pe.matmul(o_ps[:, c:c + NQ[b]], v,
                                          p_t[b % 2][0:v.shape[0], j * P:j * P + NQ[b]],
                                          start=(j == 0), stop=(j == len(vs) - 1), skip_group_check=True)
                        m.then_inc(o_made, 1)

                    if s == 0:
                        hold(pe, evac, l * OUT + HEAD + 4 * h + 3)
                        t_event(e0)
                        for b in range(4):
                            m = pe.transpose(t_ps[:, b * P:(b + 1) * P], k[:, q_cols(b)], ident[:, :])
                        m.then_inc(t_made, 1)
                        score(0)
                        score(1)
                    elif s == 1:
                        t_event(e0 + 1)
                        for b in range(4):
                            m = pe.transpose(t_ps[:, b * P:(b + 1) * P], v_t[:, q_cols(b)], ident[:, :])
                        m.then_inc(t_made, 1)
                    elif s == 2:
                        turn(0, 2)
                        score(2)
                    elif s == 3:
                        turn(1, 3)
                        score(3)
                        mix(0, 2)
                    elif s == 4:
                        t_event(e0 + 4)
                        hold(pe, ck_in, (l * 8 + h + 1) * 16)
                        pe.transpose(t_ps[0:DEC, 0:P], k[:, NEW_K:KEYS], ident[:, :])
                        pe.transpose(t_ps[0:DEC, P:2 * P], v_t[:, SEQ:T], ident[:, :])
                        for b in range(2):
                            m = pe.transpose(t_ps[:, (2 + b) * P:(3 + b) * P], ck[:, b, :], ident[:, :])
                        m.then_inc(t_made, 1)
                        mix(1, 3)
                    elif s == 5:
                        turn(2, 5)
                        hold(pe, t_read, l * T_EV + e0 + 5)
                        score(4)
                    elif s == 6:
                        turn(3, 6)
                        mix(2, 5)
                    elif s == 7:
                        turn(4, 7)
                        mix(3, 6)
                    elif s == 8:
                        mix(4, 7)

                for h in range(9):
                    for s in range(8):
                        t, c = HEAD + 4 * h + s // 2, 2 * (s % 2)
                        if h < 8:
                            chunks(t, t % 2, t // 2, (c, c + 1))
                        if h == 8 and s == 0:
                            for n in range(2):
                                hold(pe, bank_free[1 - n], (l + 1) * USES[1 - n] - 8)
                                sum_squares(proj[1 - n], sqb[:, n, :])
                        if h > 1 and s == 0:
                            head_side(h - 2, 8)
                        if h > 0:
                            head_side(h - 1, s)
                        elif s == 6:
                            hold(pe, stat_ready, l + 1)
                            pe.transpose(t_ps[0:64, 0:P], stat[:, :, :].rearrange("p a g -> p (a g)"),
                                         ident[:, :]).then_inc(t_made, 1)
                        if HEADS <= h < 8 and s in (2, 4):
                            part = s // 2 - 1
                            src = q_t[h % 2] if part == 0 else None
                            swap(HEAD + 4 * h + part, (t - 1) % 2, swap_d[:, :], src, 32,
                                 k_t[h % 2])
                head_side(7, 8)
                hold(pe, sqc_ready, l + 1)
                sum_squares(misc[:, 0:2], sqb[:, 2, :])

                def out_tile(j, b, use, first=False):
                    chunks(OUT + j, b, use, range(4), acts=KT if first else None)

                out_tile(0, 1, OUT // 2, True)
                out_tile(1, 0, OUT // 2 + 1)
                with pe.Fori(1, KT // 2) as jj:
                    out_tile(2 * jj, 1, jj + OUT // 2)
                    out_tile(2 * jj + 1, 0, jj + OUT // 2 + 1)

            pe.wait_ge(x_whole, DEPTH + 1)
            hold(pe, bank_free[0], DEPTH * USES[0])
            sum_squares(proj[0], sqx)
            pe.wait_ge(yn_made, KT)
            for b in range(5):
                n = P if b < 4 else DEC
                for k4 in range(4):
                    e = 4 * b + k4
                    if e >= 4:
                        pe.wait_ge(yt_read, e - 3)
                    for k in range(4):
                        m = pe.transpose(misc[0:n, e % 4, k * P:(k + 1) * P], xy[:, 4 * k4 + k, b * P:b * P + n],
                                         ident[:, :])
                    m.then_inc(yt_made, 1)

        @block.scalar
        def _(act):
            act.wait_ge(c_row_made, 1)
            act.activation(sq[:, 0:32], vec0[:, 0:32], ACT.Tanh, scale=0.5).then_inc(c_row_made, 1)

            def square(u, src, ready, value):
                hold(act, ready, value)
                hold(act, sq_used, u)
                act.activation(sq[:, :], src, ACT.Square).then_inc(sq_made, 1)

            act.wait_ge(c_ready, 1)
            for k in range(KT):
                square(k, xy[:, k, :], xt_read, 20)

            with act.Fori(0, DEPTH) as l:
                hold(act, vec_ready, l + 1)
                act.activation(sp_[:, 0, :], vec1[:, V1["lam"]:], ACT.Abs)
                act.drain()
                act.activation(sp_[:, 0, :], sp_[:, 0, :], ACT.Exp, scale=-1.0)
                act.drain().then_inc(lam_exp, 1)

                def root(r, n):
                    hold(act, ms_ready, l * 4 + n + 1)
                    act.activation(r, r, ACT.Sqrt).then_inc(r_ready, 1)

                def upper(t, cs, width=P):
                    for c in cs:
                        hold(act, raw_in[c], (l * TILES + t + 1) * 16)
                        hold(act, chunks_used, chunk_no(l, t, c) + 1 - RING)
                        act.activation(w_hi[:, c, :, 0:width], raw[:, c, :, 0:width], ACT.Copy)\
                            .then_inc(hi_ready, 1)

                root(r_x, 0)
                hold(act, mod_ready, l + 1)
                for k in range(KT):
                    hold(act, norm_x, l * 2 * KT + k + 1)
                    if k > 1:
                        hold(act, h_ready, l * 2 * KT + k - 1)
                    for a, z, w in PARTS:
                        act.activation(h_f[k % 2][:, a:z], xy[:, k, a:z], ACT.Identity,
                                       scale=mod[:, KT + k, w:w + 1], bias=mod[:, k, w:w + 1])
                    act.drain()
                    act.activation(act_hi[:, k, :], h_f[k % 2], ACT.Copy).then_inc(h_split, 1)
                    if k == 3:
                        upper(KI, range(4), 80)

                def take(t, b, pairs, free):
                    for dst, src in pairs:
                        act.activation(dst, src, ACT.Copy)
                    act.drain().then_inc(evac, 1)
                    if free:
                        act.drain().then_inc(bank_free[b], 1)

                def t_take(e, pairs):
                    hold(act, t_made, l * T_EV + e + 1)
                    for dst, src in pairs:
                        act.activation(dst, src, ACT.Copy)
                    act.drain().then_inc(t_read, 1)

                upper(QI, range(4))
                tile_made(act, l, KI)
                hold(act, zs_ready, l * 16)
                take(KI, 0, [(halves(qi_raw[0:80, :]), wide(proj[0])[0:80])], False)
                upper(QI + 1, (0, 1))
                t_take(0, [(ki_t[64 * n:64 * n + 64, SEQ:NEW_K], t_ps[0:64, 0:2 * P]) for n in range(2)])
                upper(QI + 1, (2, 3))
                hold(act, roped, l * 17 + 1)
                for n in range(2):
                    act.activation(ki_t[64 * n:64 * n + 64, 0:SEQ], qi_raw[0:64, 0:SEQ], ACT.Copy)
                    act.activation(ki_t[64 * n:64 * n + 64, NEW_K:KEYS], qi_raw[0:64, SEQ:T], ACT.Copy)
                act.drain().then_inc(ki_ready, 1)
                hold(act, ki_out, l * 32)
                t_take(1, [(kw_tok[:, 0:4, :], t_ps[:, 0:320].rearrange("p (b n) -> p b n", b=4)),
                           (kw_tok[0:DEC, 4, :], t_ps[0:DEC, 320:400])])
                act.dma_start(out["p_dsa_idx_k"][l, 0].rearrange("(b p) n -> p b n", p=P),
                              kw_tok[:, 0:4, 0:IDX_DIM]).then_inc(ki_out, 16)
                act.dma_start(out["s_dsa_idx_k"][l, 0], kw_tok[0:DEC, 4, 0:IDX_DIM]).then_inc(ki_out, 16)

                def take_query(q, b):
                    tile_made(act, l, QI + q)
                    hold(act, roped, l * 17 + q + 1)
                    take(QI + q, b, [(halves(qi_raw[:, :]), wide(proj[b]))], False)

                take_query(0, 1)

                def relus(q, first=False):
                    for e, (b, hh) in enumerate((b, hh) for b in (1, 2, 3, 4) for hh in range(2)):
                        hold(act, idx_made, l * 64 + 8 * q + e + 1)
                        hold(act, relu_used, l * 64 + (8 * q + e - 1 if not first or e > 1 else 0))
                        act.activation(s_sb[e % 2][0:NQ[b], 0:NK[b]], s_ps[e % 2][0:NQ[b], 0:NK[b]],
                                       ACT.Relu, scale=IDX_SCALE).then_inc(idx_read, 1)

                def query_tile(q, b, first=False):
                    upper(QI + 1 + q, range(4))
                    take_query(q, b)
                    relus(q - 1, first)

                query_tile(1, 0, True)
                with act.Fori(0, 3) as it:
                    query_tile(2 * it + 2, 1)
                    query_tile(2 * it + 3, 0)

                def take_input(g):
                    tile_made(act, l, LRU + 2 * g)
                    hold(act, conv_ready, l * G + g)
                    hold(act, pad_ready, l + 1)
                    take(LRU, 1, [(lb[0][:, 3:3 + HALF], proj[1][:, 0, 0:HALF]),
                                  (lb[0][:, 3 + HALF:3 + SEQ], proj[1][:, 1, 0:SEQ - HALF]),
                                  (lb[0][:, S0 + 3:S0 + 3 + DEC], proj[1][:, 1, SEQ - HALF:HALF])], True)

                def take_gate_path(t, b, n):
                    tile_made(act, l, t)
                    hold(act, zs_ready, l * 16 + n)
                    act.activation(halves(z_t[:, :]), wide(proj[b]), ACT.Tanh, scale=0.5)
                    act.drain().then_inc(evac, 1)

                def gates(g):
                    hold(act, gates_made, l * G + g + 1)
                    hold(act, hs_ready, l * G + g)
                    for n in range(2):
                        act.activation(lb[2 + n][:, 0:W].rearrange("p (a n) -> p a n", a=2),
                                       misc[:, 2 * n:2 * n + 2, 0:WH], ACT.Tanh, scale=0.5,
                                       bias=hb[:, n, bass.ds(g, 1)])
                    act.drain().then_inc(gates_read, 1)
                    act.activation(lb[4][:, 0:W], lb[2][:, 0:W], ACT.Tanh,
                                   scale=sp_[:, 4, bass.ds(g, 1)], bias=sp_[:, 4, bass.ds(g, 1)])
                    act.activation(lb[5][:, 0:W], lb[2][:, 0:W], ACT.Exp,
                                   scale=sp_[:, 5, bass.ds(g, 1)], bias=sp_[:, 5, bass.ds(g, 1)])
                    act.drain()
                    act.activation(lb[2][:, 0:W], lb[4][:, 0:W], ACT.Sqrt)
                    act.drain().then_inc(root_made, 1)

                def square_states(g):
                    hold(act, hs_ready, l * G + g + 1)
                    hold(act, sq_used, KT + l * SQ_U + g)
                    act.activation(sq[:, 0:SEQ], lb[4][:, 0:SEQ], ACT.Square)
                    act.activation(sq[:, SEQ:T], lb[4][:, S0:S0 + DEC], ACT.Square)
                    act.drain().then_inc(sq_made, 1)

                def recurrent_block(g, first=False):
                    upper(LRU + 1 + 2 * g, (0, 1))
                    if not first:
                        gates(g - 1)
                    upper(LRU + 1 + 2 * g, (2, 3))
                    take_input(g)
                    if first:
                        relus(7)
                    upper(LRU + 2 + 2 * g, (0, 1))
                    if not first:
                        square_states(g - 1)
                    upper(LRU + 2 + 2 * g, (2, 3))
                    take_gate_path(LRU + 1 + 2 * g, 0, g)

                recurrent_block(0, True)
                with act.Fori(1, G) as g:
                    recurrent_block(g)

                def head_side(h, s):
                    q, k, e0 = q_t[h % 2], k_t[h % 2], 3 + 8 * h
                    kind = "band" if h < HEADS else "dsa"

                    def exp(b):
                        hold(act, y_neg, l * 40 + 5 * h + b + 1)
                        x = s_sb[b % 2][0:NQ[b], 0:NK[b]]
                        act.activation(x, x, ACT.Exp, scale=-1.0, bias=nmx[0:NQ[b], b % 2:b % 2 + 1],
                                       accum_out=rsum[0:NQ[b], b % 2:b % 2 + 1])
                        act.drain().then_inc(exp_made, 1)

                    def take_turned(b, e):
                        hold(act, o_made, l * 40 + 5 * h + max(b - 1, 0))
                        if b < 4:
                            t_take(e0 + e, [(p_t[b % 2][:, 0:NK[b]], t_ps[:, 0:NK[b]])])
                        else:
                            t_take(e0 + e, [
                                (p_t[0][:, 0:2 * P].rearrange("p (b n) -> p b n", b=2)[:, :, 0:DEC],
                                 t_ps[:, 0:2 * P].rearrange("p (b n) -> p b n", b=2)[:, :, 0:DEC]),
                                (p_t[0][0:DEC, 2 * P:2 * P + DEC], t_ps[0:DEC, 2 * P:2 * P + DEC])])

                    def give(name, dst, tile):
                        act.dma_start(dst, tile).then_inc(tok_out, 16)

                    if s == 0:
                        hold(act, tok_out, l * TOK + 64 * h)
                        t_take(e0, [(k_tok[:, 0:4, :], t_ps.rearrange("p (b n) -> p b n", b=4))])
                        give("k", out[f"p_{kind}_k"][l, 0, :, h % HEADS, :]
                             .rearrange("(b p) n -> p b n", p=P), k_tok[:, 0:4, :])
                        exp(0)
                        exp(1)
                    elif s == 1:
                        t_take(e0 + 1, [(v_tok[:, 0:4, :], t_ps.rearrange("p (b n) -> p b n", b=4))])
                        give("v", out[f"p_{kind}_v"][l, 0, :, h % HEADS, :]
                             .rearrange("(b p) n -> p b n", p=P), v_tok[:, 0:4, :])
                    elif s == 2:
                        take_turned(0, 2)
                        exp(2)
                    elif s == 3:
                        take_turned(1, 3)
                        exp(3)
                    elif s == 4:
                        t_take(e0 + 4, [(k_tok[0:DEC, 4, :], t_ps[0:DEC, 0:P]),
                                        (v_tok[0:DEC, 4, :], t_ps[0:DEC, P:2 * P]),
                                        (k[:, SEQ:NEW_K], t_ps[:, 2 * P:4 * P])])
                        give("k", out[f"s_{kind}_k"][l, 0, :, h % HEADS, :], k_tok[0:DEC, 4, :])
                        give("v", out[f"s_{kind}_v"][l, 0, :, h % HEADS, :], v_tok[0:DEC, 4, :])
                    elif s == 5:
                        take_turned(2, 5)
                        exp(4)
                    elif s == 6:
                        take_turned(3, 6)
                    elif s == 7:
                        take_turned(4, 7)
                        hold(act, o_read_v, l * 16 + 2 * h + 1)
                        hold(act, sq_used, KT + l * SQ_U + G + h)
                        act.activation(sq[:, 0:SEQ], o_ps[:, 0:SEQ], ACT.Square).then_inc(o_read_a, 1)
                    elif s == 8:
                        hold(act, o_read_v, l * 16 + 2 * h + 2)
                        act.activation(sq[:, SEQ:T], o_ps[:, 0:DEC], ACT.Square)
                        act.drain().then_inc(o_read_a, 1)
                        act.drain().then_inc(sq_made, 1)

                def take_head(h, part):
                    t = HEAD + 4 * h + part
                    b = t % 2
                    if part == 3:
                        take_gate_path(t, b, G + h)
                        return
                    tile_made(act, l, t)
                    if part == 2 and h > 0:
                        hold(act, t_made, l * T_EV + 3 + 8 * (h - 1) + 5)
                    if part == 1:
                        pairs = [(k_t[h % 2][:, 0:HALF], proj[b][:, 0, 0:HALF]),
                                 (k_t[h % 2][:, HALF:SEQ], proj[b][:, 1, 0:SEQ - HALF]),
                                 (k_t[h % 2][:, NEW_K:KEYS], proj[b][:, 1, SEQ - HALF:HALF])]
                    else:
                        pairs = [(halves(q_t[h % 2] if part == 0 else v_t), wide(proj[b]))]
                    take(t, b, pairs, h < HEADS or part == 2)

                for h in range(9):
                    for s in range(8):
                        t = HEAD + 4 * h + s // 2
                        if h < 8:
                            upper(t + 1, (0, 1) if s % 2 == 0 else (2, 3))
                            if s % 2:
                                take_head(h, s // 2)
                        if h == 0 and s == 0:
                            gates(G - 1)
                        if h == 0 and s == 4:
                            square_states(G - 1)
                        if h > 1 and s == 0:
                            head_side(h - 2, 8)
                        if h > 0:
                            head_side(h - 1, s)
                        elif s == 6:
                            hold(act, stat_out, l * 64)
                            t_take(2, [(stat_r[:, :], t_ps[0:64, 0:P])])
                            for n, name in enumerate(("p_conv", "p_lru", "s_conv", "s_lru")):
                                rows = slice((0, 24, 32, 56)[n], (24, 32, 56, 64)[n])
                                dst = out[name][l]
                                dst = dst.rearrange("a (g p) -> (a g) p", p=P) if n % 2 else \
                                    dst.rearrange("a j (g p) -> (a j g) p", p=P)
                                act.dma_start(dst, stat_r[rows, :]).then_inc(stat_out, 16)
                        if h == 8 and s in (0, 3):
                            root(r_b[s // 3], 1 + s // 3)
                head_side(7, 8)
                root(r_b[2], 3)
                tile_made(act, l, OUT - 1)
                for j in range(KT):
                    hold(act, norm_x, l * 2 * KT + KT + j + 1)
                    act.activation(act_hi[:, j, :], xy[:, j, :], ACT.Copy).then_inc(h_split, 1)

                def out_tile(j, last=False):
                    if not last:
                        upper(OUT + 1 + j, range(4))
                    square(KT + l * SQ_U + KT + j, xy[:, j, :] if isinstance(j, int)
                           else xy[:, bass.ds(j, 1), :].rearrange("p a n -> p (a n)"),
                           x_new, l * KT + j + 1)
                    act.dma_start(scratch["x_keep"][l + 1, :, j], xy[:, j, :] if isinstance(j, int)
                                  else xy[:, bass.ds(j, 1), :].rearrange("p a n -> p (a n)"))\
                        .then_inc(x_kept, 16)

                with act.Fori(0, KT - 1) as j:
                    out_tile(j)
                out_tile(KT - 1, True)

            act.wait_ge(ms_ready, DEPTH * 4 + 1)
            act.activation(r_x, r_x, ACT.Sqrt).then_inc(r_ready, 1)
            for b in range(5):
                n = P if b < 4 else DEC
                if b > 1:
                    act.wait_ge(y_out[b % 2], 16 * (b // 2))
                for k4 in range(4):
                    e = 4 * b + k4
                    act.wait_ge(yt_made, e + 1)
                    act.activation(y_row[b % 2][0:n, 512 * k4:512 * k4 + 512], misc[0:n, e % 4, :], ACT.Copy)\
                        .then_inc(yt_read, 1)

        @block.vector
        def _(dve):
            def tt(o, a, b, op):
                return dve.tensor_tensor(o, a, b, op)

            def stt(o, a, s, b, op0, op1):
                return dve.scalar_tensor_tensor(out=o, in0=a, scalar=s, in1=b, op0=op0, op1=op1)

            dve.memset(sqx, 0.0)
            dve.memset(selm[:, 0:P], 0.0)
            dve.drain()
            dve.memset(selm[0:CHUNK, CHUNK:P], NEG)
            dve.wait_ge(const_in, CONSTS * 16)
            for n in range(2):
                dve.tensor_scalar(lbf[0:8, 384 + n * P:384 + (n + 1) * P], ones[0:8, :], lbf[0:8, 383:384],
                                  None, ALU.mult)
            dve.drain().then_inc(rel_rows, 1)
            dve.wait_ge(vec_made, 1)
            dve.tensor_copy(vec0[:, :], proj[0][:, 0, 0:48]).then_inc(c_row_made, 1)
            dve.wait_ge(c_row_made, 2)
            for a in range(2):
                c = slice(KT * a, KT * a + KT)
                stt(sc[:, :, a], sq[:, c], 1.0, vec0[:, c], ALU.add, ALU.mult)
            dve.drain()
            dve.tensor_scalar(sc[:, :, :], sc[:, :, :], 0.5, None, ALU.mult).then_inc(c_ready, 1)
            for b in range(5):
                n = P if b < 4 else DEC
                for k4 in range(4):
                    e = 4 * b + k4
                    dve.wait_ge(xt_made, e + 1)
                    dve.tensor_copy(xy[:, 4 * k4:4 * k4 + 4, b * P:b * P + n],
                                    misc[:, e % 4, :].rearrange("p (k n) -> p k n", k=4)[:, :, 0:n])\
                        .then_inc(xt_read, 1)

            def add_squares(dst, u):
                hold(dve, sq_made, u + 1)
                tt(dst, dst, sq[:, :], ALU.add)
                dve.drain().then_inc(sq_used, 1)

            for k in range(KT):
                add_squares(sqx, k)
            dve.drain().then_inc(x_whole, 1)

            def mean_square(ps, dst, n, value):
                hold(dve, ss_made, value)
                dve.tensor_scalar(halves(dst), wide(ps), 1.0 / n, EPS, ALU.mult, ALU.add)
                dve.drain()
                dve.reciprocal(dst, dst)
                dve.drain().then_inc(ms_ready, 1)

            with dve.Fori(0, DEPTH) as l:
                hold(dve, vec_made, l + 2)
                dve.tensor_copy(vec1[:, :], t_ps[:, 0:P])
                dve.tensor_copy(vec2[:, :], o_ps[:, 0:48])
                dve.drain().then_inc(vec_ready, 1)
                dve.tensor_scalar(hg[:, :], vec2[:, 0:KT], 0.5, None, ALU.mult)
                dve.tensor_scalar(hb[:, :, :], vec1[:, V1["b_rg"]:V1["lam"]]
                                  .rearrange("p (a g) -> p a g", a=2), 0.5, None, ALU.mult)
                mean_square(proj[0], r_x, D_MODEL, l * 4 + 1)
                e_, z_, z2, p_, m_ = (sp_[:, n, :] for n in range(5))
                hold(dve, lam_exp, l + 1)
                dve.tensor_scalar(z_, e_, 2.0, None, ALU.add)
                dve.tensor_scalar(m_, vec1[:, V1["lam"]:], -1.0, 0.0, ALU.mult, ALU.max)
                dve.drain()
                dve.reciprocal(z_, z_)
                dve.drain()
                tt(z_, z_, e_, ALU.mult)
                dve.drain()
                tt(z2, z_, z_, ALU.mult)
                dve.drain()
                dve.tensor_scalar(p_, z2, 1.0 / 17, 1.0 / 15, ALU.mult, ALU.add)
                dve.drain()
                for n in (13, 11, 9, 7, 5, 3, 1):
                    tt(p_, p_, z2, ALU.mult)
                    dve.drain()
                    dve.tensor_scalar(p_, p_, 1.0 / n, None, ALU.add)
                    dve.drain()
                stt(p_, z_, 2.0, p_, ALU.mult, ALU.mult)
                dve.drain()
                tt(p_, p_, m_, ALU.add)
                dve.drain()
                dve.tensor_scalar(sp_[:, 4, :], p_, 2.0, None, ALU.mult)
                dve.tensor_scalar(sp_[:, 5, :], p_, -4.0, None, ALU.mult)
                with dve.Fori(0, ADA_BLOCKS // 2) as i:
                    for n in range(2):
                        hold(dve, ada_used, (l * ADA_BLOCKS + 2 * i + n + 1) * 4)
                        hold(dve, ada_turned, l * ADA_BLOCKS + 2 * i + n - 1)
                        dve.tensor_copy(ada_row[n], s_ps[n][0:2, :]).then_inc(ada_read, 1)
                hold(dve, ada_turned, (l + 1) * ADA_BLOCKS)
                made = t_ps[:, 0:2 * ADA].rearrange("p (j a) -> p j a", a=2)
                for a in range(2):
                    tt(mod[:, :, a], made[:, :, a], vec1[:, 0:ADA], ALU.add)
                dve.drain()
                for a in range(2):
                    stt(mod[:, KT:2 * KT, a], mod[:, KT:2 * KT, a], 1.0,
                        vec1[:, V1["g_norm"]:V1["g_norm"] + KT], ALU.add, ALU.mult)
                dve.drain().then_inc(mod_ready, 1)

                def lower(k, src, base):
                    hold(dve, h_split, l * 2 * KT + base + k + 1)
                    tt(act_lo[:, k, :], src, act_hi[:, k, :].bitcast(F32), ALU.subtract)\
                        .then_inc(h_ready, 1)

                hold(dve, x_kept, 16 + l * KT * 16)
                hold(dve, r_ready, l * 4 + 1)
                for k in range(KT + 1):
                    if k < KT:
                        tt(xy[:, k, :], xy[:, k, :], r_x, ALU.mult).then_inc(norm_x, 1)
                    if k > 0:
                        lower(k - 1, h_f[(k - 1) % 2], 0)
                dve.drain()
                dve.memset(lb[0][:, 0:3], 0.0)
                dve.memset(lb[0][:, S0 + 3 + DEC:W + 4], 0.0)
                dve.memset(lb[0][:, S0:S0 + 3], 0.0)
                dve.drain().then_inc(pad_ready, 1)
                dve.memset(sqb[:, :, :], 0.0)
                dve.memset(acc[:, :], 0.0)

                def rotate(n, raw_parts, rot, b, table):
                    hold(dve, swapped, l * 17 + n + 1)
                    rows = rot.shape[0]
                    tt(halves(rot), wide(proj[b])[0:rows], halves(rope[0:rows, 1, :]), ALU.mult)
                    dve.drain().then_inc(bank_free[b], 1)
                    for x, a, z in raw_parts:
                        tt(x, x, rope[0:rows, 0, a:z], ALU.mult)
                    dve.drain()

                hold(dve, rope_in, (2 * l + 1) * 16)
                rotate(0, [(qi_raw[0:64, :], 0, T)], qi_rot[0:64, :], 0, 0)
                tt(qi_raw[0:64, :], qi_raw[0:64, :], qi_rot[0:64, :], ALU.add)
                dve.drain().then_inc(roped, 1)

                def query(q, b, first=False):
                    if not first:
                        hold(dve, idx_made, l * 64 + 8 * q)
                    rotate(q + 1, [(qi_raw[:, :], 0, T)], qi_rot[:, :], b, 0)
                    tt(qi_rot[:, :], qi_rot[:, :], qi_raw[:, :], ALU.add)
                    dve.drain().then_inc(roped, 1)

                def add_scores(q):
                    for e, (b, hh) in enumerate((b, hh) for b in (1, 2, 3, 4) for hh in range(2)):
                        hold(dve, idx_read, l * 64 + 8 * q + e + 1)
                        a = acc[0:NQ[b], ACC[b]:ACC[b] + NK[b]]
                        stt(a, s_sb[e % 2][0:NQ[b], 0:NK[b]],
                            kw_tok[0:NQ[b], b, bass.ds(IDX_DIM + 2 * q + hh, 1)], a, ALU.mult, ALU.add)\
                            .then_inc(relu_used, 1)
                        if hh == 0:
                            dve.drain()

                hold(dve, t_read, l * T_EV + 2)
                query(0, 1, True)
                add_scores(0)
                with dve.Fori(0, 3) as it:
                    query(2 * it + 1, 0)
                    add_scores(2 * it + 1)
                    query(2 * it + 2, 1)
                    add_scores(2 * it + 2)
                query(7, 0)
                add_scores(7)
                dve.drain()
                for b in (1, 2, 3):
                    end = ACC[b] + NK[b]
                    dve.memset(acc[0:CHUNK, end - CHUNK:end], NEG)
                dve.drain()

                def best(blocks, rows):
                    for n, b in enumerate(blocks):
                        dve.max(top8[0:rows, n, :], acc[0:rows, ACC[b]:ACC[b] + NK[b]])
                    dve.drain()
                    for n, b in enumerate(blocks):
                        a = acc[0:rows, ACC[b]:ACC[b] + NK[b]]
                        dve.match_replace(a, top8[0:rows, n, :], a, TAKEN)
                    dve.drain()

                def col(v, base, g):
                    return v[:, bass.ds(base + g, 1)]

                def convolve(g):
                    state = vec2[:, V2["state_conv"]:V2["state_conv"] + 3 * G]\
                        .rearrange("p (j g) -> p j g", g=G)
                    dve.tensor_copy(lb[0][:, S0:S0 + 3], state[:, :, bass.ds(g, 1)]
                                    .rearrange("p j a -> p (j a)"))
                    hold(dve, evac, l * OUT + LRU + 2 * g + 1)
                    dve.drain()
                    x, y = lb[0], lb[1][:, 0:W]
                    dve.tensor_copy(stat[:, 0:3, bass.ds(g, 1)].rearrange("p j a -> p (j a)"),
                                    x[:, SEQ:SEQ + 3])
                    dve.tensor_copy(stat[:, 4:7, bass.ds(g, 1)].rearrange("p j a -> p (j a)"),
                                    x[:, S0 + DEC:S0 + DEC + 3])
                    dve.tensor_scalar(y, x[:, 0:W], col(vec1, V1["conv_w"], g), col(vec1, V1["conv_b"], g),
                                      ALU.mult, ALU.add)
                    for j in range(1, CONV_W):
                        dve.drain()
                        stt(y, x[:, j:j + W], col(vec1, V1["conv_w"] + j * G, g), y, ALU.mult, ALU.add)
                    dve.drain().then_inc(conv_ready, 1)

                def gate_path(t, b, dst):
                    hold(dve, evac, l * OUT + t + 1)
                    stt(halves(dst), halves(z_t[:, :]), 1.0, wide(proj[b]), ALU.add, ALU.mult)
                    dve.drain().then_inc(bank_free[b], 1)
                    dve.drain().then_inc(zs_ready, 1)

                def tile(v, j):
                    return v[:, bass.ds(j, 1), :].rearrange("p a n -> p (a n)")

                def recur(g):
                    hold(dve, root_made, l * G + g + 1)
                    x, s, ti, t, a = (lb[n][:, 0:W] for n in (1, 2, 3, 4, 5))
                    stt(s, a, 1.0, s, ALU.add, ALU.mult)
                    stt(t, a, 1.0, t, ALU.add, ALU.mult)
                    stt(ti, ti, 1.0, x, ALU.add, ALU.mult)
                    dve.drain()
                    dve.tensor_scalar(a, t, -1.0, 1.0, ALU.mult, ALU.add)
                    stt(s, s, 0.5, ti, ALU.mult, ALU.mult)
                    dve.drain()
                    dve.tensor_tensor_scan(t[:, 0:SEQ], a[:, 0:SEQ], s[:, 0:SEQ], 0.0, ALU.mult, ALU.add)
                    dve.tensor_tensor_scan(t[:, S0:S0 + DEC], a[:, S0:S0 + DEC], s[:, S0:S0 + DEC],
                                           col(vec2, V2["state_lru"], g), ALU.mult, ALU.add)
                    dve.drain().then_inc(hs_ready, 1)
                    dve.tensor_copy(stat[:, 3, bass.ds(g, 1)], t[:, SEQ - 1:SEQ])
                    dve.tensor_copy(stat[:, 7, bass.ds(g, 1)], t[:, S0 + DEC - 1:S0 + DEC])
                    y = tile(xy, g)
                    for a_, z_, at_ in ((0, SEQ, 0), (SEQ, T, S0)):
                        stt(y[:, a_:z_], t[:, at_:at_ + z_ - a_], col(hg, 0, g), y[:, a_:z_],
                            ALU.mult, ALU.mult)
                    add_squares(sqb[:, 0, :], KT + l * SQ_U + g)

                def recurrent_block(g, first=False):
                    if not first:
                        recur(g - 1)
                    convolve(g)
                    for _ in range(2):
                        best((1, 2, 3), P)
                    gate_path(LRU + 1 + 2 * g, 0, tile(xy, g))

                recurrent_block(0, True)
                with dve.Fori(1, G) as g:
                    recurrent_block(g)

                def head_side(h, s):
                    def logits(b):
                        e = {0: 0, 1: 0, 2: 3, 3: 4, 4: 6}[b]
                        hold(dve, t_made, l * T_EV + 3 + 8 * h + e)
                        hold(dve, s_made, l * 40 + 5 * h + b + 1)
                        if h >= HEADS:
                            mask = selm[0:NQ[b], SEL[b]:SEL[b] + NK[b]]
                        elif b < 4:
                            mask = bias[:, 0:NK[b]][:, ::-1]
                        else:
                            mask = bias[0:DEC, CHUNK:CHUNK + NS][:, ::-1]
                        x = s_sb[b % 2][0:NQ[b], 0:NK[b]]
                        stt(x, s_ps[b % 2][0:NQ[b], 0:NK[b]], -SCALE, mask, ALU.mult, ALU.subtract)
                        dve.drain().then_inc(s_read, 1)
                        dve.tensor_reduce(nmx[0:NQ[b], b % 2:b % 2 + 1], x, AX.X, ALU.min)
                        dve.drain().then_inc(y_neg, 1)

                    def normalise(b):
                        hold(dve, exp_made, l * 40 + 5 * h + b + 1)
                        r = rinv[0:NQ[b], b % 2:b % 2 + 1]
                        dve.reciprocal(r, rsum[0:NQ[b], b % 2:b % 2 + 1])
                        dve.drain()
                        x = s_sb[b % 2][0:NQ[b], 0:NK[b]]
                        dve.tensor_scalar(x, x, r, None, ALU.mult)
                        dve.drain().then_inc(p_ready, 1)

                    if s == 0:
                        if h < HEADS:
                            hold(dve, bias_in, (l * HEADS + h + 1) * 16)
                        logits(0)
                        logits(1)
                        normalise(0)
                        normalise(1)
                    elif s in (2, 3, 5):
                        b = {2: 2, 3: 3, 5: 4}[s]
                        logits(b)
                        normalise(b)
                    elif s in (7, 8):
                        a, z = (0, SEQ) if s == 7 else (SEQ, T)
                        hold(dve, o_made, l * 40 + 5 * h + s - 3)
                        y = xy[:, G + h, a:z]
                        stt(y, o_ps[:, 0:z - a], hg[:, G + h:G + h + 1], y, ALU.mult, ALU.mult)
                        dve.drain().then_inc(o_read_v, 1)
                        if s == 8:
                            add_squares(sqb[:, 1 + h // HEADS, :], KT + l * SQ_U + G + h)

                for h in range(9):
                    for s in range(8):
                        t = HEAD + 4 * h + s // 2
                        if h == 0 and s == 1:
                            recur(G - 1)
                            dve.drain().then_inc(stat_ready, 1)
                        if h == 0 and s == 3:
                            for _ in range(TOPK_S // 8):
                                best((4,), DEC)
                            for b in (1, 2, 3, 4):
                                dve.tensor_scalar(selm[0:NQ[b], SEL[b]:SEL[b] + NK[b]],
                                                  acc[0:NQ[b], ACC[b]:ACC[b] + NK[b]],
                                                  0.5 * TAKEN, NEG, ALU.is_gt, ALU.mult)
                            dve.drain()
                        if HEADS <= h < 8 and s in (2, 4):
                            part = s // 2 - 1
                            x = (q_t if part == 0 else k_t)[h % 2][0:32]
                            parts = [(x, 0, T)] if part == 0 else \
                                [(x[:, 0:SEQ], 0, SEQ), (x[:, NEW_K:KEYS], SEQ, T)]
                            hold(dve, rope_in, (2 * l + 2) * 16)
                            rotate(9 + 2 * (h - HEADS) + part, parts, d_rot[0:32, 0:T], (t - 1) % 2, 1)
                            for y, a, z in parts:
                                tt(y, y, d_rot[0:32, a:z], ALU.add)
                            dve.drain().then_inc(roped, 1)
                        if h > 1 and s == 0:
                            head_side(h - 2, 8)
                        if h > 0:
                            head_side(h - 1, s)
                        if h < 8 and s == 7:
                            gate_path(t, t % 2, xy[:, G + h, :])
                        if h == 8 and s in (0, 3):
                            mean_square(proj[1 - s // 3], r_b[s // 3], (D_LRU, D_LRU // 2)[s // 3],
                                        l * 4 + 2 + s // 3)
                head_side(7, 8)
                dve.drain().then_inc(sqc_ready, 1)
                dve.memset(sqx, 0.0)
                mean_square(misc[:, 0:2], r_b[2], D_LRU // 2, l * 4 + 4)
                for j in range(KT + 1):
                    if j < KT:
                        n = 0 if j < G else 1 if j < G + HEADS else 2
                        if j in (0, G, G + HEADS):
                            hold(dve, r_ready, l * 4 + 2 + n)
                        tt(xy[:, j, :], xy[:, j, :], r_b[n], ALU.mult).then_inc(norm_x, 1)
                    if j > 0:
                        lower(j - 1, xy[:, j - 1, :], KT)

                def out_tile(j, jj, s):
                    b = (OUT + s) % 2
                    tile_made(dve, l, OUT + j)
                    hold(dve, old_in[s], (l * 4 + jj + 1) * 16)
                    x = tile(xy, j)
                    for half, a, z, w in ((0, 0, HALF, 0), (1, HALF, SEQ, 0), (1, SEQ, T, 1)):
                        gate = mod[:, bass.ds(2 * KT + j, 1), w:w + 1].rearrange("p a n -> p (a n)")
                        stt(x[:, a:z], proj[b][:, half, a - half * HALF:z - half * HALF], gate,
                            x_old[s][:, a:z], ALU.mult, ALU.add)
                    dve.drain().then_inc(bank_free[b], 1)
                    dve.drain().then_inc(x_new, 1)
                    add_squares(sqx, KT + l * SQ_U + KT + j)

                with dve.Fori(0, 4) as jj:
                    for s in range(4):
                        out_tile(4 * jj + s, jj, s)
                dve.drain().then_inc(x_whole, 1)

            mean_square(proj[0], r_x, D_MODEL, DEPTH * 4 + 1)
            dve.wait_ge(x_kept, 16 + DEPTH * KT * 16)
            dve.wait_ge(r_ready, DEPTH * 4 + 1)
            for k in range(KT):
                stt(xy[:, k, :], xy[:, k, :], vec0[:, 32 + k:33 + k], r_x, ALU.mult, ALU.mult)\
                    .then_inc(yn_made, 1)


_INS = ["x_prompt", "x_sample", "c_prompt", "c_sample", "state_conv", "state_lru", "cache_band_k",
        "cache_band_v", "cache_dsa_k", "cache_dsa_v", "cache_dsa_idx_k", "g_norm", "w_ada", "b_ada",
        "w_in", "conv_w", "conv_b", "w_rg", "b_rg", "w_ig", "b_ig", "lru_lambda", "rel_bias",
        "g_branch", "w_out", "g_final"]
_OUTS = {
    "y_prompt": (1, SEQ, D_MODEL), "y_sample": (1, DEC, D_MODEL),
    "p_conv": (DEPTH, 1, CONV_W - 1, D_LRU), "p_lru": (DEPTH, 1, D_LRU),
    "p_band_k": (DEPTH, 1, SEQ, HEADS, HD), "p_band_v": (DEPTH, 1, SEQ, HEADS, HD),
    "p_dsa_k": (DEPTH, 1, SEQ, HEADS, HD), "p_dsa_v": (DEPTH, 1, SEQ, HEADS, HD),
    "p_dsa_idx_k": (DEPTH, 1, SEQ, IDX_DIM),
    "s_conv": (DEPTH, 1, CONV_W - 1, D_LRU), "s_lru": (DEPTH, 1, D_LRU),
    "s_band_k": (DEPTH, 1, DEC, HEADS, HD), "s_band_v": (DEPTH, 1, DEC, HEADS, HD),
    "s_dsa_k": (DEPTH, 1, DEC, HEADS, HD), "s_dsa_v": (DEPTH, 1, DEC, HEADS, HD),
    "s_dsa_idx_k": (DEPTH, 1, DEC, IDX_DIM),
}


def _rotary(rows, group, width):
    pos = np.concatenate([np.arange(SEQ), PAST + np.arange(DEC)]).astype(np.float32)
    half = width // 2
    inv = np.float32(ROPE_THETA) ** (-np.arange(half, dtype=np.float32) / np.float32(half))
    ang = pos[None] * inv[:, None].astype(np.float32)
    table = np.zeros((rows, 2, T), np.float32)
    table[:, 0] = 1
    for r in range(0, rows, group):
        table[r:r + half, 0] = table[r + half:r + width, 0] = np.cos(ang)
        table[r:r + half, 1] = -np.sin(ang)
        table[r + half:r + width, 1] = np.sin(ang)
    return table


def _swaps(rows, group, width):
    m = np.zeros((rows, rows), np.float32)
    for r in range(0, rows, group):
        for n in range(width):
            m[r + n, r + (n + width // 2) % width] = 1
    return m


def _constants():
    return {
        "ident": np.eye(P, dtype=np.float32), "ones": np.ones((P, P), np.float32),
        "swap_i": _swaps(P, 64, 16), "swap_d": _swaps(32, 32, 32),
        "blocked": np.full((8, CHUNK, CHUNK), NEG, np.float32),
        "rope_i": _rotary(P, 64, 16), "rope_d": _rotary(32, 32, 32),
    }


def kernel(**inputs):
    import concourse.bacc as bacc
    from concourse.bass_utils import run_bass_kernel_spmd

    nc = bacc.Bacc("TRN2", target_bir_lowering=False, num_devices=1)
    arrays, ins, outs = {}, {}, {}
    for name in _INS:
        arrays[f"in_{name}"] = np.ascontiguousarray(inputs[name])
    for name, a in _constants().items():
        arrays[f"in_{name}"] = a
    for name, a in arrays.items():
        ins[name[3:]] = nc.dram_tensor(name, a.shape, mybir.dt.from_np(a.dtype), kind="ExternalInput").ap()
    for name, shape in _OUTS.items():
        outs[name] = nc.dram_tensor(f"out_{name}", shape, F32, kind="ExternalOutput").ap()
    scratch = {
        "rows": nc.dram_tensor("rel_rows", (8, 640), F32, kind="Internal").ap(),
        "windows": nc.dram_tensor("rel_windows", (8, P, 512), F32, kind="Internal").ap(),
        "x_keep": nc.dram_tensor("x_keep", (DEPTH + 1, P, KT, T), F32, kind="Internal").ap(),
    }
    build(nc, ins, outs, scratch)
    r = run_bass_kernel_spmd(nc, [arrays], core_ids=[0])
    return tuple(r.results[0][f"out_{name}"] for name in _OUTS)
```

```python
from contextlib import ExitStack

import concourse.bass as bass
import numpy as np
from concourse import mybir

F32 = mybir.dt.float32
F32R = mybir.dt.float32r
BF16 = mybir.dt.bfloat16
ALU = mybir.AluOpType
ACT = mybir.ActivationFunctionType
AX = mybir.AxisListType

P = 128
D_MODEL, SEQ, DEC, PAST, DEPTH = 2048, 512, 64, 256, 2
KT = D_MODEL // P
T = SEQ + DEC
HALF = T // 2
D_LRU, HEADS, HD = 1024, 4, 128
G = D_LRU // P
IDX_HEADS, IDX_DIM, TOPK, TOPK_S = 16, 64, 128, 80
CHUNK, CONV_W, EPS, NEG, TAKEN = 64, 4, 1e-6, -1e30, -3e38
REL = 256
D_IN = 7248
SCALE = float(HD) ** -0.5
IDX_SCALE = float(IDX_DIM) ** -0.5 * float(IDX_HEADS) ** -0.5
ROPE_THETA = 500000.0

KI = 0
QI = 1
LRU = QI + 8
HEAD = LRU + 2 * G
OUT = HEAD + 8 * 4
TILES = OUT + KT
RING = 4
KC = 4
CHUNKS = TILES * 4
USES = ((TILES + 1) // 2, TILES // 2)
COL_KI = 7168
COLS = {"qi": 6144, "xa": 0, "za": 1024}
ADA = 3 * KT
AB = 512
ADA_BLOCKS = ADA * P // AB
NEW_K = SEQ + PAST
KEYS = NEW_K + DEC
NS = PAST + DEC
W = SEQ + 3 + DEC + 1
S0 = SEQ + 3
WH = W // 2
ACC = {1: 0, 2: 256, 3: 640, 4: 1152}
SEL = {0: 0, 1: 128, 2: 384, 3: 768, 4: 1280}
NK = {0: 128, 1: 256, 2: 384, 3: 512, 4: NS}
NQ = {0: P, 1: P, 2: P, 3: P, 4: DEC}

V1 = {"b_ada": 0, "g_norm": 48, "conv_w": 64, "conv_b": 96, "b_rg": 104, "b_ig": 112, "lam": 120}
V2 = {"g_branch": 0, "state_lru": 16, "state_conv": 24}
V0 = {"c_prompt": 0, "c_sample": 16, "g_final": 32}


def head_col(h, part):
    return 2048 + (h // HEADS) * 2048 + part * 512 + (h % HEADS) * P


def build(nc, inp, out, scratch):
    with ExitStack() as ctx:
        def sb(name, shape, dt=F32):
            return ctx.enter_context(nc.sbuf_tensor(name, shape, dt))

        started = []
        start = {}

        def sem(name, at=0):
            start[name] = at
            s = ctx.enter_context(nc.semaphore(name))
            if at:
                started.append((s, at))
            return s

        xy = sb("xy", [P, KT, T])
        act_hi = sb("act_hi", [P, KT, T], F32R)
        act_lo = sb("act_lo", [P, KT, T], F32R)
        raw = sb("raw", [P, RING, KC, P])
        w_hi = sb("w_hi", [P, RING, KC, P], F32R)
        w_lo = sb("w_lo", [P, RING, KC, P], F32R)
        work = sb("work", [P, 8192])
        lbf = sb("lb", [P, 3 * 584])
        rope = sb("rope", [P, 2, T])
        ki_t = sb("ki_t", [P, KEYS])
        qi_raw = sb("qi_raw", [P, T])
        acc = sb("acc", [P, 1472])
        selm = sb("selm", [P, 1600], BF16)
        kw_tok = sb("kw_tok", [P, 5, 80])
        ci = sb("ci", [P, 2, IDX_DIM])
        top8 = sb("top8", [P, 3, 8])
        w_rg = sb("w_rg", [P, P])
        w_ig = sb("w_ig", [P, P])
        sq = sb("sq", [P, T])
        sqb = sb("sqb", [P, 3, T])
        sqx = sqb[:, 0, :]
        ident = sb("ident", [P, P])
        ones = sb("ones", [P, P])
        swap_i = sb("swap_i", [P, P])
        swap_d = sb("swap_d", [32, 32])
        vec1 = sb("vec1", [P, P])
        vec2 = sb("vec2", [P, 48])
        vec0 = sb("vec0", [P, 48])
        sc = sb("sc", [P, KT, 2])
        mod = sb("mod", [P, ADA, 2])
        hg = sb("hg", [P, KT])
        hb = sb("hb", [P, 2, G])
        sp_ = sb("sp", [P, 6, G])
        stat = sb("stat", [P, 8, G])
        stat_r = sb("stat_r", [64, P])
        nmx = sb("nmx", [P, 2])
        rsum = sb("rsum", [P, 2])
        rinv = sb("rinv", [P, 2])

        at = 0

        def cut(n):
            nonlocal at
            at += n
            return work[:, at - n:at]

        q_t = [cut(T) for _ in range(2)]
        k_t = [cut(KEYS) for _ in range(2)]
        s_sb = [cut(512) for _ in range(2)]
        v_t = cut(T)
        qi_rot = v_t
        ck = cut(2 * P).rearrange("p (b n) -> p b n", b=2)
        cv = cut(2 * P).rearrange("p (b n) -> p b n", b=2)
        bias = cut(512)
        first = at
        p_t = [cut(512) for _ in range(2)]
        v_tok = cut(5 * P).rearrange("p (b n) -> p b n", b=5)
        k_tok = cut(5 * P).rearrange("p (b n) -> p b n", b=5)
        lb = [work[:, first + n * 584:first + (n + 1) * 584] for n in range(2)] \
            + [lbf[:, n * 584:(n + 1) * 584] for n in range(3)] \
            + [work[:, first + 2 * 584:first + 3 * 584]]
        vrow = acc[:, 0:2 * P].rearrange("p (a n) -> p a n", a=2)
        d_rot = lb[3]
        ada_w = work[:, :].rearrange("p (s k n) -> p s k n", s=4, k=KC)
        ada_row = [sqb[0:2, n, 0:AB] for n in (1, 2)]
        raw_flat = raw[:, :, :, :].rearrange("p c k n -> p (c k n)")
        XC = D_MODEL // 2
        x_row = [raw_flat[:, 0:XC], raw_flat[:, XC:2 * XC], lbf[:, 640:640 + XC],
                 rope[:, :, :].rearrange("p a n -> p (a n)")[:, 0:XC], acc[:, 2 * P:2 * P + XC]]
        y_row = [work[:, 2048 + 2048 * j:4096 + 2048 * j] for j in range(2)]
        r_x = lb[2][:, 0:T]
        r_b = [lb[n][:, 0:T] for n in (2, 4, 3)]
        z_t = qi_raw
        x_old = [lb[n][:, 0:T] for n in (2, 3, 4)] + [qi_raw[:, :]]

        proj = [ctx.enter_context(nc.psum_tensor(f"proj{b}", [P, 2, 512], F32)) for b in range(2)]
        misc = ctx.enter_context(nc.psum_tensor("misc", [P, 4, 512], F32))
        s_ps = [misc[:, 0, :], misc[:, 1, :]]
        t_ps = misc[:, 2, :]
        o_ps = misc[:, 3, :]

        const_in = sem("const_in")
        x_in = [sem(f"x_in{s}") for s in range(5)]
        xt_made = sem("xt_made")
        xt_read = sem("xt_read")
        x_kept = sem("x_kept")
        x_whole = sem("x_whole")
        c_row_made = sem("c_row_made")
        c_ready = sem("c_ready")
        vec_in = sem("vec_in")
        vec_made = sem("vec_made")
        vec_ready = sem("vec_ready")
        ada_in = [sem(f"ada_in{s}") for s in range(4)]
        ada_used = sem("ada_used")
        ada_read = sem("ada_read", 2)
        ada_turned = sem("ada_turned", 2)
        ss_made = sem("ss_made")
        ms_ready = sem("ms_ready")
        r_ready = sem("r_ready")
        norm_x = sem("norm_x", 1)
        pad_ready = sem("pad_ready")
        h_split = sem("h_split")
        h_low_g = sem("h_low_g")
        h_low_v = sem("h_low_v")
        raw_in = [sem(f"raw_in{s}") for s in range(RING)]
        hi_ready = sem("hi_ready")
        lo_ready = sem("lo_ready", RING)
        chunks_used = sem("chunks_used", RING)
        bank_free = [sem(f"bank_free{b}", 1) for b in range(2)]
        evac = sem("evac")
        swapped = sem("swapped")
        roped = sem("roped")
        rope_in = sem("rope_in")
        ci_in = sem("ci_in")
        ki_ready = sem("ki_ready")
        s_made = sem("s_made")
        s_read = sem("s_read", 1)
        idx_made = sem("idx_made", 1)
        idx_read = sem("idx_read", 1)
        relu_made = sem("relu_made")
        relu_used = sem("relu_used", 1)
        sel_ready = sem("sel_ready")
        t_made = sem("t_made", 1)
        t_read = sem("t_read", 1)
        exp_made = sem("exp_made")
        y_neg = sem("y_neg", 1)
        p_ready = sem("p_ready")
        o_made = sem("o_made", 1)
        o_read_a = sem("o_read_a", 1)
        o_read_v = sem("o_read_v", 1)
        zs_ready = sem("zs_ready", 1)
        gate_w_in = sem("gate_w_in")
        conv_ready = sem("conv_ready", 1)
        gates_made = sem("gates_made", 1)
        gates_read = sem("gates_read", 1)
        root_made = sem("root_made")
        hs_ready = sem("hs_ready", 1)
        hs_sq = sem("hs_sq")
        sq_made = sem("sq_made")
        sq_used = sem("sq_used", 1)
        bias_in = sem("bias_in")
        bias_ready = sem("bias_ready")
        ck_in = sem("ck_in")
        cv_in = sem("cv_in")
        ki_out = sem("ki_out", 16)
        tok_out = sem("tok_out", 16)
        sqc_ready = sem("sqc_ready")
        stat_ready = sem("stat_ready")
        stat_out = sem("stat_out", 16)
        old_in = [sem(f"old_in{s}") for s in range(4)]
        rel_rows = sem("rel_rows")
        rel_out = sem("rel_out")
        lam_exp = sem("lam_exp")
        x_new = sem("x_new", 1)
        yn_made = sem("yn_made")
        yt_made = sem("yt_made")
        yt_read = sem("yt_read")
        y_out = [sem(f"y_out{s}") for s in range(2)]
        ticks = sem("ticks")

        def hold(eng, s, value):
            eng.wait_ge(s, value + start[s.name])
            eng.sem_inc(ticks, 1)

        def chunk_no(l, t, c):
            return l * CHUNKS + t * 4 + c

        def t_no(h, e):
            return 3 + 8 * h + e + (0 if h < 5 else min(e + 1, 4) if h == 5 else 4)

        def tile_made(eng, l, t):
            hold(eng, chunks_used, chunk_no(l, t, 4))

        block = ctx.enter_context(nc.Block())

        def wide(ps, n=HALF):
            return ps[:, :, 0:n]

        def halves(ap):
            return ap.rearrange("p (a n) -> p a n", a=2)

        def q_cols(b):
            return slice(b * P, b * P + NQ[b])

        def key_cols(b):
            return slice(0, NK[b]) if b < 4 else slice(SEQ, KEYS)

        PARTS = ((0, SEQ, 0), (SEQ, T, 1))
        T_EV = 3 + 8 * 8 + 4
        SQ_U = 32
        TOK = 32 * 16
        CONSTS = 8

        @block.sync
        def _(sp):
            for s, n in started:
                sp.sem_inc(s, n)
            for dst, src in (
                (ident[:, :], inp["ident"]), (swap_i[:, :], inp["swap_i"]), (swap_d[:, :], inp["swap_d"]),
                (ones[:, :], inp["ones"]),
                (vrow[0:16, 0, :], inp["c_prompt"].rearrange("a (r p) -> (a r) p", p=P)),
                (vrow[16:32, 0, :], inp["c_sample"].rearrange("a (r p) -> (a r) p", p=P)),
                (vrow[32:48, 0, :], inp["g_final"].rearrange("(r p) -> r p", p=P)),
                (lbf[0:8, 0:384], inp["rel_bias"].rearrange("l h n -> (l h) n")[:, 129:513]),
            ):
                sp.dma_start(dst, src).then_inc(const_in, 16)
            for i in range(10):
                b, slot, cols = i // 2, i % 5, slice(i % 2 * XC, (i % 2 + 1) * XC)
                if i >= 5:
                    sp.wait_ge(xt_read, 2 * (i - 4))
                src = inp["x_prompt"][0, b * P:(b + 1) * P, cols] if b < 4 else inp["x_sample"][0][:, cols]
                sp.dma_start(x_row[slot][0:src.shape[0], :], src).then_inc(x_in[slot], 16)

            with sp.Fori(0, DEPTH) as l:
                hold(sp, vec_made, l + 1)
                hold(sp, norm_x, l * 2 * KT)
                for n, (name, row, rows) in enumerate((
                    ("b_ada", V1["b_ada"], ADA), ("g_norm", V1["g_norm"], KT),
                    ("conv_w", V1["conv_w"], 4 * G), ("conv_b", V1["conv_b"], G),
                    ("b_rg", V1["b_rg"], G), ("b_ig", V1["b_ig"], G), ("lru_lambda", V1["lam"], G),
                    ("g_branch", V2["g_branch"], KT), ("state_lru", V2["state_lru"], G),
                    ("state_conv", V2["state_conv"], 3 * G),
                )):
                    src = inp[name][l]
                    src = {1: lambda a: a.rearrange("(r p) -> r p", p=P),
                           2: lambda a: a.rearrange("a (r p) -> (a r) p", p=P),
                           3: lambda a: a.rearrange("a b (r p) -> (a b r) p", p=P)}[len(src.shape)](src)
                    sp.dma_start(vrow[row:row + rows, int(n > 6), :], src).then_inc(vec_in, 16)
                hold(sp, o_made, l * 40)
                hold(sp, tok_out, l * TOK)
                w_ada = inp["w_ada"][l].rearrange("(k p) n -> p k n", p=P)

                def load_ada(s, col):
                    sp.dma_start(ada_w[:, s], w_ada[:, s * KC:(s + 1) * KC, bass.ds(col, AB)])\
                        .then_inc(ada_in[s], 16)

                for s in range(4):
                    load_ada(s, 0)
                with sp.Fori(1, ADA_BLOCKS) as j:
                    for s in range(4):
                        hold(sp, ada_used, (l * ADA_BLOCKS + j) * 4 + (s - 3))
                        load_ada(s, j * AB)
                sp.dma_start(rope[:, :, :], inp["rope_i"]).then_inc(rope_in, 16)
                sp.dma_start(ci[:, :, :], inp["cache_dsa_idx_k"][l, 0].rearrange("(b p) n -> p b n", p=P))\
                    .then_inc(ci_in, 16)

                w_in = inp["w_in"][l].rearrange("(k p) n -> p k n", p=P)
                w_out = inp["w_out"][l].rearrange("(k p) n -> p k n", p=P)

                def load(w, t, col, width=P):
                    for c in range(4):
                        hold(sp, lo_ready, chunk_no(l, t, c) + 1 - RING)
                        sp.dma_start(raw[:, c, :, 0:width],
                                     w[:, c * KC:(c + 1) * KC, bass.ds(col, width)]).then_inc(raw_in[c], 16)

                load(w_in, KI, COL_KI, 80)
                with sp.Fori(0, 8) as q:
                    load(w_in, QI + q, COLS["qi"] + q * P)
                with sp.Fori(0, G) as g:
                    load(w_in, LRU + 2 * g, COLS["xa"] + g * P)
                    hold(sp, gates_made, l * G + g)
                    sp.dma_start(w_rg[:, :], inp["w_rg"][l, g]).then_inc(gate_w_in, 16)
                    sp.dma_start(w_ig[:, :], inp["w_ig"][l, g]).then_inc(gate_w_in, 16)
                    load(w_in, LRU + 1 + 2 * g, COLS["za"] + g * P)

                def load_head_extras(h, values):
                    kind = "band" if h < HEADS else "dsa"
                    if values:
                        hold(sp, o_made, (l * 8 + h) * 5)
                    else:
                        hold(sp, y_neg, (l * 8 + h) * 5)
                        if h < HEADS:
                            sp.dma_start(bias, scratch["windows"][l * HEADS + h]).then_inc(bias_in, 16)
                    src = inp[f"cache_{kind}_{'v' if values else 'k'}"][l, 0, :, h % HEADS, :]
                    sp.dma_start(cv if values else ck, src.rearrange("(b p) n -> p b n", p=P))\
                        .then_inc(cv_in if values else ck_in, 16)

                for h in range(8):
                    load(w_in, HEAD + 4 * h, head_col(h, 0))
                    if h > 0:
                        load_head_extras(h - 1, False)
                    if h == HEADS - 1:
                        sp.dma_start(rope[0:32, :, :], inp["rope_d"]).then_inc(rope_in, 16)
                    load(w_in, HEAD + 4 * h + 1, head_col(h, 1))
                    load(w_in, HEAD + 4 * h + 2, head_col(h, 2))
                    if h > 0:
                        load_head_extras(h - 1, True)
                    load(w_in, HEAD + 4 * h + 3, head_col(h, 3))
                load_head_extras(7, False)
                load(w_out, OUT, 0)
                load_head_extras(7, True)
                load(w_out, OUT + 1, P)
                hold(sp, norm_x, (l + 1) * 2 * KT)
                for s in range(4):
                    sp.dma_start(x_old[s], scratch["x_keep"][l, :, s]).then_inc(old_in[s], 16)
                for j in range(2, 4):
                    load(w_out, OUT + j, j * P)
                with sp.Fori(1, 4) as jj:
                    for s in range(4):
                        hold(sp, x_new, l * KT + 4 * jj + (s - 3))
                        sp.dma_start(x_old[s], scratch["x_keep"][l, :, 4 * jj + s]).then_inc(old_in[s], 16)
                        load(w_out, OUT + s + 4 * jj, jj * 512 + s * P)

            for b in range(5):
                sp.wait_ge(yt_read, 4 * (b + 1))
                n = P if b < 4 else DEC
                dst = out["y_prompt"][0, b * P:(b + 1) * P, :] if b < 4 else out["y_sample"][0]
                sp.dma_start(dst, y_row[b % 2][0:n, :]).then_inc(y_out[b % 2], 16)
            sp.wait_ge(y_out[0], 48)
            sp.wait_ge(y_out[1], 32)
            hold(sp, tok_out, DEPTH * TOK)
            hold(sp, ki_out, DEPTH * 32)
            hold(sp, stat_out, DEPTH * 64)
            sp.wait_ge(x_kept, 16 + DEPTH * KT * 16)

        @block.gpsimd
        def _(pool):
            pool.wait_ge(c_ready, 1)
            pool.wait_ge(xt_read, 20)
            pool.tensor_tensor(sqx, xy[:, 0, :], xy[:, 0, :], ALU.mult)
            for k in range(1, KT):
                pool.tensor_tensor(sq[:, :], xy[:, k, :], xy[:, k, :], ALU.mult)
                pool.drain()
                pool.tensor_tensor(sqx, sqx, sq[:, :], ALU.add)
                pool.drain()
            pool.drain().then_inc(x_whole, 1)

            def lower(l, base, k0=0, k1=KT):
                for k in range(k0, k1):
                    if k % 4 < 3:
                        pool.wait_ge(h_split, l * 2 * KT + base + k + 1)
                        pool.tensor_tensor(act_lo[:, k, :], xy[:, k, :], act_hi[:, k, :].bitcast(F32),
                                           ALU.subtract).then_inc(h_low_g, 1)

            def split(l, t, width=P, cs=range(4)):
                for c in cs:
                    pool.wait_ge(hi_ready, chunk_no(l, t, c) + 1)
                    pool.tensor_tensor(w_lo[:, c, :, 0:width], raw[:, c, :, 0:width],
                                       w_hi[:, c, :, 0:width].bitcast(F32), ALU.subtract)\
                        .then_inc(lo_ready, 1)

            with pool.Fori(0, DEPTH) as l:
                split(l, KI, 80)
                lower(l, 0)
                with pool.Fori(1, OUT + 1) as t:
                    split(l, t)
                lower(l, KT, 0, G + HEADS)
                split(l, OUT + 1, cs=(0, 1, 2))
                lower(l, KT, G + HEADS, KT)
                split(l, OUT + 1, cs=(3,))
                with pool.Fori(OUT + 2, TILES) as t:
                    split(l, t)

        @block.tensor
        def _(pe):
            pe.wait_ge(const_in, CONSTS * 16)
            pe.transpose(proj[0][:, 0, 0:48], vrow[0:48, 0, :], ident[0:48, 0:48]).then_inc(vec_made, 1)
            for b in range(5):
                n = P if b < 4 else DEC
                for k4 in range(4):
                    e = 4 * b + k4
                    slot = e // 2 % 5
                    pe.wait_ge(x_in[slot], 16 * (e // 10 + 1))
                    if e >= 4:
                        pe.wait_ge(xt_read, e - 3)
                    for k in range(4):
                        c = (e % 2 * 4 + k) * P
                        m = pe.transpose(misc[:, e % 4, k * P:k * P + n], x_row[slot][0:n, c:c + P],
                                         ident[0:n, 0:n])
                    m.then_inc(xt_made, 1)

            def sum_squares(ps, src):
                for half in range(2):
                    m = pe.matmul(ps[:, half, 0:HALF], ones[:, :], src[:, half * HALF:(half + 1) * HALF],
                                  start=True, stop=True)
                m.then_inc(ss_made, 1)

            pe.wait_ge(xt_read, 20)
            pe.wait_ge(c_ready, 1)

            with pe.Fori(0, DEPTH) as l:

                def modulate(j, n):
                    hold(pe, ada_read, l * ADA_BLOCKS + j - 1)
                    for s in range(4):
                        hold(pe, ada_in[s], (l * ADA_BLOCKS + j + 1) * 16)
                        for kk in range(KC):
                            k = s * KC + kk
                            m = pe.matmul(s_ps[n][0:2, :], sc[:, k, :], ada_w[:, s, kk, :],
                                          start=(k == 0), stop=(k == KT - 1))
                        m.then_inc(ada_used, 1)

                def turn_modulation(j, n):
                    hold(pe, ada_read, l * ADA_BLOCKS + j + 1)
                    for i in range(AB // P):
                        m = pe.matmul(t_ps[:, bass.ds(j * 8 + 2 * i, 2)], ada_row[n][:, i * P:(i + 1) * P],
                                      ident[0:2, 0:2], start=True, stop=True)
                    m.then_inc(ada_turned, 1)

                modulate(0, 0)
                hold(pe, vec_in, (l + 1) * 160)
                pe.transpose(t_ps[:, 0:P], vrow[:, 0, :], ident[:, :])
                pe.transpose(o_ps[:, 0:48], vrow[0:48, 1, :], ident[0:48, 0:48]).then_inc(vec_made, 1)
                hold(pe, vec_ready, l + 1)

                def two_blocks(i):
                    modulate(2 * i + 1, 1)
                    turn_modulation(2 * i, 0)
                    modulate(2 * i + 2, 0)
                    turn_modulation(2 * i + 1, 1)

                with pe.Fori(0, ADA_BLOCKS // 2 - 2) as i:
                    two_blocks(i)
                hold(pe, x_whole, l + 1)
                hold(pe, bank_free[0], l * USES[0])
                sum_squares(proj[0], sqx)
                two_blocks(ADA_BLOCKS // 2 - 2)
                modulate(ADA_BLOCKS - 1, 1)
                turn_modulation(ADA_BLOCKS - 2, 0)
                turn_modulation(ADA_BLOCKS - 1, 1)

                def chunks(t, b, use, cs, width=P, acts=None):
                    for c in cs:
                        if c == 0:
                            pe.wait_ge(bank_free[b], l * USES[b] + use + 1)
                        if acts is not None:
                            pe.wait_ge(h_low_g, (l * 2 * KT + acts + (c + 1) * KC) // KC * 3)
                            pe.wait_ge(h_low_v, (l * 2 * KT + acts + (c + 1) * KC) // KC)
                        pe.wait_ge(lo_ready, chunk_no(l, t, c) + 1 + RING)
                        for kk in range(KC):
                            k = c * KC + kk
                            for half in range(2):
                                cols = slice(half * HALF, (half + 1) * HALF)
                                dst = proj[b][0:width, half, 0:HALF]
                                pe.matmul(dst, w_hi[:, c, kk, 0:width], act_hi[:, k, cols],
                                          start=(k == 0), stop=False)
                                pe.matmul(dst, w_hi[:, c, kk, 0:width], act_lo[:, k, cols],
                                          start=False, stop=False)
                            for half in range(2):
                                cols = slice(half * HALF, (half + 1) * HALF)
                                m = pe.matmul(proj[b][0:width, half, 0:HALF], w_lo[:, c, kk, 0:width],
                                              act_hi[:, k, cols], start=False, stop=(k == KT - 1))
                        m.then_inc(chunks_used, 1)

                def swap(t_evac, b, perm, src, n, keys=None):
                    hold(pe, evac, l * OUT + t_evac + 1)
                    for half in range(2):
                        if src is not None:
                            m = pe.matmul(proj[b][0:n, half, 0:HALF], perm,
                                          src[0:n, half * HALF:(half + 1) * HALF], start=True, stop=True)
                        else:
                            a, z = ((0, HALF), (HALF, SEQ))[half]
                            m = pe.matmul(proj[b][0:n, half, 0:z - a], perm, keys[0:n, a:z],
                                          start=True, stop=True)
                    if src is None:
                        m = pe.matmul(proj[b][0:n, 1, SEQ - HALF:HALF], perm, keys[0:n, NEW_K:KEYS],
                                      start=True, stop=True, skip_group_check=True)
                    m.then_inc(swapped, 1)

                def t_event(e):
                    hold(pe, t_read, l * T_EV + e)

                def scores(q, first=False):
                    hold(pe, roped, l * 17 + q + 2)
                    for e, (b, hh) in enumerate((b, hh) for b in (1, 2, 3, 4) for hh in range(2)):
                        hold(pe, idx_read, l * 64 + (8 * q + e - 1 if not first or e > 1 else 0))
                        rows = slice(64 * hh, 64 * hh + 64)
                        pe.matmul(s_ps[e % 2][0:NQ[b], 0:NK[b]], qi_rot[rows, q_cols(b)],
                                  ki_t[rows, key_cols(b)], start=True, stop=True).then_inc(idx_made, 1)

                chunks(KI, 0, 0, range(4), 80, acts=0)
                chunks(QI, 1, 0, (0, 1))
                swap(KI, 0, swap_i[0:64, 0:64], qi_raw, 64)
                hold(pe, ci_in, (l + 1) * 16)
                t_event(0)
                for b in range(2):
                    m = pe.transpose(t_ps[0:64, b * P:(b + 1) * P], ci[:, b, :], ident[:, :])
                m.then_inc(t_made, 1)
                chunks(QI, 1, 0, (2, 3))
                hold(pe, roped, l * 17 + 1)
                t_event(1)
                for b in range(5):
                    m = pe.transpose(t_ps[0:NQ[b], b * 80:b * 80 + 80], qi_raw[0:80, q_cols(b)],
                                     ident[0:80, 0:80])
                m.then_inc(t_made, 1)

                def query_tile(q, b, use, first=False):
                    chunks(QI + q, b, use, (0, 1))
                    swap(QI - 1 + q, 1 - b, swap_i[:, :], qi_raw, P)
                    chunks(QI + q, b, use, (2, 3))
                    if first:
                        hold(pe, ki_ready, l + 1)
                    scores(q - 1, first)

                query_tile(1, 0, 1, True)
                with pe.Fori(0, 3) as it:
                    query_tile(2 * it + 2, 1, it + 1)
                    query_tile(2 * it + 3, 0, it + 2)

                def recurrent_block(g, first=False):
                    chunks(LRU + 2 * g, 1, g + 4, (0, 1))
                    if first:
                        swap(QI + 7, 0, swap_i[:, :], qi_raw, P)
                    chunks(LRU + 2 * g, 1, g + 4, (2, 3))
                    if first:
                        scores(7)
                        hold(pe, idx_read, (l + 1) * 64)
                        t_event(2)
                    chunks(LRU + 1 + 2 * g, 0, g + 5, range(4))
                    hold(pe, gates_read, l * G + g)
                    hold(pe, conv_ready, l * G + g + 1)
                    hold(pe, gate_w_in, (l * G + g + 1) * 32)
                    for n, w in enumerate((w_rg, w_ig)):
                        for half in range(2):
                            m = pe.matmul(misc[:, 2 * n + half, 0:WH], w[:, :],
                                          lb[1][:, half * WH:(half + 1) * WH], start=True, stop=True)
                    m.then_inc(gates_made, 1)

                recurrent_block(0, True)
                with pe.Fori(1, G) as g:
                    recurrent_block(g)

                def head_side(h, s):
                    q, k = q_t[h % 2], k_t[h % 2]

                    def score(b):
                        if b < 2:
                            hold(pe, s_read, l * 40 + 5 * h)
                        else:
                            hold(pe, s_read, l * 40 + 5 * h + b - 1)
                        pe.matmul(s_ps[b % 2][0:NQ[b], 0:NK[b]], q[:, q_cols(b)], k[:, key_cols(b)],
                                  start=True, stop=True).then_inc(s_made, 1)

                    def turn(b, e):
                        t_event(t_no(h, e))
                        hold(pe, p_ready, l * 40 + 5 * h + b + 1)
                        for j in range(0, NK[b], P):
                            n = min(P, NK[b] - j)
                            m = pe.transpose(t_ps[0:n, j:j + NQ[b]], s_sb[b % 2][0:NQ[b], j:j + n],
                                             ident[0:NQ[b], 0:NQ[b]])
                        m.then_inc(t_made, 1)

                    def mix(b, e):
                        hold(pe, t_read, l * T_EV + t_no(h, e) + 1)
                        if b in (0, 4):
                            hold(pe, o_read_v, l * 16 + 2 * h + (b == 4))
                            hold(pe, o_read_a, l * 16 + 2 * h + (b == 4))
                        if b == 4:
                            hold(pe, cv_in, (l * 8 + h + 1) * 16)
                            vs = [cv[:, 0, :], cv[:, 1, :], v_tok[0:DEC, 4, :]]
                        else:
                            vs = [v_tok[:, j, :] for j in range(b + 1)]
                        for j, v in enumerate(vs):
                            c = (b % 4) * P
                            m = pe.matmul(o_ps[:, c:c + NQ[b]], v,
                                          p_t[b % 2][0:v.shape[0], j * P:j * P + NQ[b]],
                                          start=(j == 0), stop=(j == len(vs) - 1), skip_group_check=True)
                        m.then_inc(o_made, 1)

                    if s == 0:
                        hold(pe, evac, l * OUT + HEAD + 4 * h + 3)
                        t_event(t_no(h, 0))
                        for b in range(4):
                            m = pe.transpose(t_ps[:, b * P:(b + 1) * P], k[:, q_cols(b)], ident[:, :])
                        m.then_inc(t_made, 1)
                        score(0)
                        score(1)
                    elif s == 1:
                        t_event(t_no(h, 1))
                        for b in range(4):
                            m = pe.transpose(t_ps[:, b * P:(b + 1) * P], v_t[:, q_cols(b)], ident[:, :])
                        m.then_inc(t_made, 1)
                    elif s == 2:
                        turn(0, 2)
                        score(2)
                    elif s == 3:
                        turn(1, 3)
                        score(3)
                        mix(0, 2)
                    elif s == 4:
                        t_event(t_no(h, 4))
                        hold(pe, ck_in, (l * 8 + h + 1) * 16)
                        pe.transpose(t_ps[0:DEC, 0:P], k[:, NEW_K:KEYS], ident[:, :])
                        pe.transpose(t_ps[0:DEC, P:2 * P], v_t[:, SEQ:T], ident[:, :])
                        for b in range(2):
                            m = pe.transpose(t_ps[:, (2 + b) * P:(3 + b) * P], ck[:, b, :], ident[:, :])
                        m.then_inc(t_made, 1)
                        mix(1, 3)
                    elif s == 5:
                        turn(2, 5)
                        hold(pe, t_read, l * T_EV + t_no(h, 4) + 1)
                        score(4)
                    elif s == 6:
                        turn(3, 6)
                        mix(2, 5)
                    elif s == 7:
                        turn(4, 7)
                        mix(3, 6)
                    elif s == 8:
                        mix(4, 7)

                for h in range(9):
                    for s in range(8):
                        t, c = HEAD + 4 * h + s // 2, 2 * (s % 2)
                        if h < 8:
                            chunks(t, t % 2, t // 2, (c, c + 1))
                        if h == 6 and s < 4:
                            hold(pe, sq_used, l * SQ_U + G + HEADS)
                            t_event(t_no(5, s) - 1)
                            pe.matmul(t_ps[:, 0:HALF], ones[:, :], sqb[:, s // 2, s % 2 * HALF:][:, 0:HALF],
                                      start=True, stop=True).then_inc(t_made, 1)
                        if h > 1 and s == 0:
                            head_side(h - 2, 8)
                        if h > 0:
                            head_side(h - 1, s)
                        elif s == 6:
                            hold(pe, stat_ready, l + 1)
                            pe.transpose(t_ps[0:64, 0:P], stat[:, :, :].rearrange("p a g -> p (a g)"),
                                         ident[:, :]).then_inc(t_made, 1)
                        if HEADS <= h < 8 and s in (2, 4):
                            part = s // 2 - 1
                            src = q_t[h % 2] if part == 0 else None
                            swap(HEAD + 4 * h + part, (t - 1) % 2, swap_d[:, :], src, 32,
                                 k_t[h % 2])
                        if h == 8 and s > 1:
                            j = (s - 2) // 3
                            chunks(OUT + j, 1 - j, OUT // 2 + j, ((s - 2) % 3,), acts=None if j else KT)
                head_side(7, 8)
                hold(pe, sqc_ready, l + 1)
                sum_squares(misc[:, 0:2], sqb[:, 2, :])

                def out_tile(j, b, use):
                    chunks(OUT + j, b, use, range(4))

                chunks(OUT, 1, OUT // 2, (3,), acts=KT)
                chunks(OUT + 1, 0, OUT // 2 + 1, (3,))
                with pe.Fori(1, KT // 2) as jj:
                    out_tile(2 * jj, 1, jj + OUT // 2)
                    out_tile(2 * jj + 1, 0, jj + OUT // 2 + 1)

            pe.wait_ge(x_whole, DEPTH + 1)
            hold(pe, bank_free[0], DEPTH * USES[0])
            sum_squares(proj[0], sqx)
            pe.wait_ge(yn_made, KT)
            for b in range(5):
                n = P if b < 4 else DEC
                for k4 in range(4):
                    e = 4 * b + k4
                    if e >= 4:
                        pe.wait_ge(yt_read, e - 3)
                    for k in range(4):
                        m = pe.transpose(misc[0:n, e % 4, k * P:(k + 1) * P], xy[:, 4 * k4 + k, b * P:b * P + n],
                                         ident[:, :])
                    m.then_inc(yt_made, 1)

        @block.scalar
        def _(act):
            act.wait_ge(c_row_made, 1)
            act.activation(sq[:, 0:32], vec0[:, 0:32], ACT.Tanh, scale=0.5).then_inc(c_row_made, 1)

            def square(u, src, ready, value):
                hold(act, ready, value)
                hold(act, sq_used, u)
                act.activation(sq[:, :], src, ACT.Square).then_inc(sq_made, 1)

            act.wait_ge(rel_rows, 1)
            act.dma_start(scratch["rows"], lbf[0:8, 0:640]).then_inc(rel_out, 16)
            act.wait_ge(rel_out, 16)
            act.dma_start(scratch["windows"], bass.AP(scratch["rows"].tensor, 0, [[640, 8], [1, P], [1, 512]]))\
                .then_inc(rel_out, 16)
            act.wait_ge(rel_out, 32)
            act.dma_start(scratch["windows"][:, 0:CHUNK, 0:CHUNK], inp["blocked"]).then_inc(rel_out, 16)
            act.wait_ge(xt_read, 20)
            act.dma_start(scratch["x_keep"][0], xy[:, :, :]).then_inc(x_kept, 16)
            act.wait_ge(rel_out, 48)

            with act.Fori(0, DEPTH) as l:
                hold(act, vec_ready, l + 1)
                act.activation(sp_[:, 0, :], vec1[:, V1["lam"]:], ACT.Abs)
                act.drain()
                act.activation(sp_[:, 0, :], sp_[:, 0, :], ACT.Exp, scale=-1.0)
                act.drain().then_inc(lam_exp, 1)

                def root(r, n):
                    hold(act, ms_ready, l * 4 + n + 1)
                    act.activation(r, r, ACT.Sqrt).then_inc(r_ready, 1)

                def upper(t, cs, width=P, more=0):
                    for c in cs:
                        hold(act, raw_in[c], (l * TILES + t + 1) * 16)
                        hold(act, chunks_used, chunk_no(l, t, c) + 1 - RING + more)
                        act.activation(w_hi[:, c, :, 0:width], raw[:, c, :, 0:width], ACT.Copy)\
                            .then_inc(hi_ready, 1)

                root(r_x, 0)
                upper(KI, range(4), 80)
                for k in range(KT):
                    hold(act, norm_x, l * 2 * KT + k + 1)
                    act.activation(act_hi[:, k, :], xy[:, k, :], ACT.Copy).then_inc(h_split, 1)

                def take(t, b, pairs, free):
                    for dst, src in pairs:
                        act.activation(dst, src, ACT.Copy)
                    act.drain().then_inc(evac, 1)
                    if free:
                        act.drain().then_inc(bank_free[b], 1)

                def t_take(e, pairs):
                    hold(act, t_made, l * T_EV + e + 1)
                    for dst, src in pairs:
                        act.activation(dst, src, ACT.Copy)
                    act.drain().then_inc(t_read, 1)

                upper(QI, range(4))
                tile_made(act, l, KI)
                hold(act, zs_ready, l * 16)
                take(KI, 0, [(halves(qi_raw[0:80, :]), wide(proj[0])[0:80])], False)
                upper(QI + 1, (0, 1))
                t_take(0, [(ki_t[64 * n:64 * n + 64, SEQ:NEW_K], t_ps[0:64, 0:2 * P]) for n in range(2)])
                upper(QI + 1, (2, 3))
                hold(act, roped, l * 17 + 1)
                for n in range(2):
                    act.activation(ki_t[64 * n:64 * n + 64, 0:SEQ], qi_raw[0:64, 0:SEQ], ACT.Copy)
                    act.activation(ki_t[64 * n:64 * n + 64, NEW_K:KEYS], qi_raw[0:64, SEQ:T], ACT.Copy)
                act.drain().then_inc(ki_ready, 1)
                hold(act, ki_out, l * 32)
                t_take(1, [(kw_tok[:, 0:4, :], t_ps[:, 0:320].rearrange("p (b n) -> p b n", b=4)),
                           (kw_tok[0:DEC, 4, :], t_ps[0:DEC, 320:400])])
                act.dma_start(out["p_dsa_idx_k"][l, 0].rearrange("(b p) n -> p b n", p=P),
                              kw_tok[:, 0:4, 0:IDX_DIM]).then_inc(ki_out, 16)
                act.dma_start(out["s_dsa_idx_k"][l, 0], kw_tok[0:DEC, 4, 0:IDX_DIM]).then_inc(ki_out, 16)

                def take_query(q, b):
                    tile_made(act, l, QI + q)
                    hold(act, roped, l * 17 + q + 1)
                    take(QI + q, b, [(halves(qi_raw[:, :]), wide(proj[b]))], False)

                take_query(0, 1)

                def relus(q, first=False):
                    for e, (b, hh) in enumerate((b, hh) for b in (1, 2, 3, 4) for hh in range(2)):
                        hold(act, idx_made, l * 64 + 8 * q + e + 1)
                        hold(act, relu_used, l * 64 + (8 * q + e - 1 if not first or e > 1 else 0))
                        act.activation(s_sb[e % 2][0:NQ[b], 0:NK[b]], s_ps[e % 2][0:NQ[b], 0:NK[b]],
                                       ACT.Relu, scale=IDX_SCALE).then_inc(idx_read, 1)

                def query_tile(q, b, first=False):
                    upper(QI + 1 + q, range(4))
                    take_query(q, b)
                    relus(q - 1, first)

                query_tile(1, 0, True)
                with act.Fori(0, 3) as it:
                    query_tile(2 * it + 2, 1)
                    query_tile(2 * it + 3, 0)

                def take_input(g):
                    tile_made(act, l, LRU + 2 * g)
                    hold(act, conv_ready, l * G + g)
                    hold(act, pad_ready, l + 1)
                    take(LRU, 1, [(lb[0][:, 3:3 + HALF], proj[1][:, 0, 0:HALF]),
                                  (lb[0][:, 3 + HALF:3 + SEQ], proj[1][:, 1, 0:SEQ - HALF]),
                                  (lb[0][:, S0 + 3:S0 + 3 + DEC], proj[1][:, 1, SEQ - HALF:HALF])], True)

                def take_gate_path(t, b, n):
                    tile_made(act, l, t)
                    hold(act, zs_ready, l * 16 + n)
                    act.activation(halves(z_t[:, :]), wide(proj[b]), ACT.Tanh, scale=0.5)
                    act.drain().then_inc(evac, 1)

                def gates(g):
                    hold(act, gates_made, l * G + g + 1)
                    hold(act, hs_ready, l * G + g)
                    for n in range(2):
                        act.activation(lb[2 + n][:, 0:W].rearrange("p (a n) -> p a n", a=2),
                                       misc[:, 2 * n:2 * n + 2, 0:WH], ACT.Tanh, scale=0.5,
                                       bias=hb[:, n, bass.ds(g, 1)])
                    act.drain().then_inc(gates_read, 1)
                    act.activation(lb[4][:, 0:W], lb[2][:, 0:W], ACT.Tanh,
                                   scale=sp_[:, 4, bass.ds(g, 1)], bias=sp_[:, 4, bass.ds(g, 1)])
                    act.activation(lb[5][:, 0:W], lb[2][:, 0:W], ACT.Exp,
                                   scale=sp_[:, 5, bass.ds(g, 1)], bias=sp_[:, 5, bass.ds(g, 1)])
                    act.drain()
                    act.activation(lb[2][:, 0:W], lb[4][:, 0:W], ACT.Sqrt)
                    act.drain().then_inc(root_made, 1)

                def square_states(g):
                    hold(act, hs_ready, l * G + g + 1)
                    hold(act, sq_used, l * SQ_U + g)
                    act.activation(sq[:, 0:SEQ], lb[4][:, 0:SEQ], ACT.Square)
                    act.activation(sq[:, SEQ:T], lb[4][:, S0:S0 + DEC], ACT.Square)
                    act.drain().then_inc(sq_made, 1)

                def recurrent_block(g, first=False):
                    upper(LRU + 1 + 2 * g, (0, 1))
                    if not first:
                        gates(g - 1)
                    upper(LRU + 1 + 2 * g, (2, 3))
                    take_input(g)
                    if first:
                        relus(7)
                    upper(LRU + 2 + 2 * g, (0, 1))
                    if not first:
                        square_states(g - 1)
                    upper(LRU + 2 + 2 * g, (2, 3))
                    take_gate_path(LRU + 1 + 2 * g, 0, g)

                recurrent_block(0, True)
                with act.Fori(1, G) as g:
                    recurrent_block(g)

                def head_side(h, s):
                    q, k = q_t[h % 2], k_t[h % 2]
                    kind = "band" if h < HEADS else "dsa"

                    def exp(b):
                        hold(act, y_neg, l * 40 + 5 * h + b + 1)
                        x = s_sb[b % 2][0:NQ[b], 0:NK[b]]
                        act.activation(x, x, ACT.Exp, scale=-1.0, bias=nmx[0:NQ[b], b % 2:b % 2 + 1],
                                       accum_out=rsum[0:NQ[b], b % 2:b % 2 + 1])
                        act.drain().then_inc(exp_made, 1)

                    def take_turned(b, e):
                        hold(act, o_made, l * 40 + 5 * h + max(b - 1, 0))
                        if b < 4:
                            t_take(t_no(h, e), [(p_t[b % 2][:, 0:NK[b]], t_ps[:, 0:NK[b]])])
                        else:
                            t_take(t_no(h, e), [
                                (p_t[0][:, 0:2 * P].rearrange("p (b n) -> p b n", b=2)[:, :, 0:DEC],
                                 t_ps[:, 0:2 * P].rearrange("p (b n) -> p b n", b=2)[:, :, 0:DEC]),
                                (p_t[0][0:DEC, 2 * P:2 * P + DEC], t_ps[0:DEC, 2 * P:2 * P + DEC])])

                    def give(name, dst, tile):
                        act.dma_start(dst, tile).then_inc(tok_out, 16)

                    if s == 0:
                        hold(act, tok_out, l * TOK + 64 * h)
                        t_take(t_no(h, 0), [(k_tok[:, 0:4, :], t_ps.rearrange("p (b n) -> p b n", b=4))])
                        give("k", out[f"p_{kind}_k"][l, 0, :, h % HEADS, :]
                             .rearrange("(b p) n -> p b n", p=P), k_tok[:, 0:4, :])
                        exp(0)
                        exp(1)
                    elif s == 1:
                        t_take(t_no(h, 1), [(v_tok[:, 0:4, :], t_ps.rearrange("p (b n) -> p b n", b=4))])
                        give("v", out[f"p_{kind}_v"][l, 0, :, h % HEADS, :]
                             .rearrange("(b p) n -> p b n", p=P), v_tok[:, 0:4, :])
                    elif s == 2:
                        take_turned(0, 2)
                        exp(2)
                    elif s == 3:
                        take_turned(1, 3)
                        exp(3)
                    elif s == 4:
                        t_take(t_no(h, 4), [(k_tok[0:DEC, 4, :], t_ps[0:DEC, 0:P]),
                                        (v_tok[0:DEC, 4, :], t_ps[0:DEC, P:2 * P]),
                                        (k[:, SEQ:NEW_K], t_ps[:, 2 * P:4 * P])])
                        give("k", out[f"s_{kind}_k"][l, 0, :, h % HEADS, :], k_tok[0:DEC, 4, :])
                        give("v", out[f"s_{kind}_v"][l, 0, :, h % HEADS, :], v_tok[0:DEC, 4, :])
                    elif s == 5:
                        take_turned(2, 5)
                        exp(4)
                    elif s == 6:
                        take_turned(3, 6)
                    elif s == 7:
                        take_turned(4, 7)
                        hold(act, o_read_v, l * 16 + 2 * h + 1)
                        hold(act, sq_used, l * SQ_U + G + h)
                        act.activation(sq[:, 0:SEQ], o_ps[:, 0:SEQ], ACT.Square).then_inc(o_read_a, 1)
                    elif s == 8:
                        hold(act, o_read_v, l * 16 + 2 * h + 2)
                        act.activation(sq[:, SEQ:T], o_ps[:, 0:DEC], ACT.Square)
                        act.drain().then_inc(o_read_a, 1)
                        act.drain().then_inc(sq_made, 1)

                def take_head(h, part):
                    t = HEAD + 4 * h + part
                    b = t % 2
                    if part == 3:
                        take_gate_path(t, b, G + h)
                        return
                    tile_made(act, l, t)
                    if part == 2 and h > 0:
                        hold(act, t_made, l * T_EV + t_no(h - 1, 4) + 1)
                    if part == 1:
                        pairs = [(k_t[h % 2][:, 0:HALF], proj[b][:, 0, 0:HALF]),
                                 (k_t[h % 2][:, HALF:SEQ], proj[b][:, 1, 0:SEQ - HALF]),
                                 (k_t[h % 2][:, NEW_K:KEYS], proj[b][:, 1, SEQ - HALF:HALF])]
                    else:
                        pairs = [(halves(q_t[h % 2] if part == 0 else v_t), wide(proj[b]))]
                    take(t, b, pairs, h < HEADS or part == 2)

                def upper_y(j0, j1):
                    tile_made(act, l, OUT - 1)
                    for j in range(j0, j1):
                        hold(act, norm_x, l * 2 * KT + KT + j + 1)
                        act.activation(act_hi[:, j, :], xy[:, j, :], ACT.Copy).then_inc(h_split, 1)

                for h in range(9):
                    for s in range(8):
                        t = HEAD + 4 * h + s // 2
                        if h < 8:
                            upper(t + 1, (0, 1) if s % 2 == 0 else (2, 3))
                            if s % 2:
                                take_head(h, s // 2)
                        if h == 0 and s == 0:
                            gates(G - 1)
                        if h == 0 and s == 4:
                            square_states(G - 1)
                        if h > 1 and s == 0:
                            head_side(h - 2, 8)
                        if h > 0:
                            head_side(h - 1, s)
                        elif s == 6:
                            hold(act, stat_out, l * 64)
                            t_take(2, [(stat_r[:, :], t_ps[0:64, 0:P])])
                            for n, name in enumerate(("p_conv", "p_lru", "s_conv", "s_lru")):
                                rows = slice((0, 24, 32, 56)[n], (24, 32, 56, 64)[n])
                                dst = out[name][l]
                                dst = dst.rearrange("a (g p) -> (a g) p", p=P) if n % 2 else \
                                    dst.rearrange("a j (g p) -> (a j g) p", p=P)
                                act.dma_start(dst, stat_r[rows, :]).then_inc(stat_out, 16)
                        if h == 6 and s == 4:
                            root(r_b[0], 1)
                            root(r_b[1], 2)
                        if h == 8 and s < 3:
                            upper_y(4 * s, 4 * s + 4)
                        if h == 8 and 4 <= s < 7:
                            upper(OUT + 1, (s - 4,))
                head_side(7, 8)
                root(r_b[2], 3)
                upper_y(G + HEADS, KT)
                upper(OUT + 1, (3,), more=3)

                def out_tile(j, last=False, first=False):
                    if not last and not first:
                        upper(OUT + 1 + j, range(4))
                    square(l * SQ_U + KT + j, xy[:, j, :] if isinstance(j, int)
                           else xy[:, bass.ds(j, 1), :].rearrange("p a n -> p (a n)"),
                           x_new, l * KT + j + 1)
                    act.dma_start(scratch["x_keep"][l + 1, :, j], xy[:, j, :] if isinstance(j, int)
                                  else xy[:, bass.ds(j, 1), :].rearrange("p a n -> p (a n)"))\
                        .then_inc(x_kept, 16)

                out_tile(0, first=True)
                with act.Fori(1, KT - 1) as j:
                    out_tile(j)
                out_tile(KT - 1, True)

            act.wait_ge(ms_ready, DEPTH * 4 + 1)
            act.activation(r_x, r_x, ACT.Sqrt).then_inc(r_ready, 1)
            for b in range(5):
                n = P if b < 4 else DEC
                if b > 1:
                    act.wait_ge(y_out[b % 2], 16 * (b // 2))
                for k4 in range(4):
                    e = 4 * b + k4
                    act.wait_ge(yt_made, e + 1)
                    act.activation(y_row[b % 2][0:n, 512 * k4:512 * k4 + 512], misc[0:n, e % 4, :], ACT.Copy)\
                        .then_inc(yt_read, 1)

        @block.vector
        def _(dve):
            def tt(o, a, b, op):
                return dve.tensor_tensor(o, a, b, op)

            def stt(o, a, s, b, op0, op1):
                return dve.scalar_tensor_tensor(out=o, in0=a, scalar=s, in1=b, op0=op0, op1=op1)

            dve.memset(selm[:, 0:P], 0.0)
            dve.drain()
            dve.memset(selm[0:CHUNK, CHUNK:P], NEG)
            dve.wait_ge(const_in, CONSTS * 16)
            for n in range(2):
                dve.tensor_scalar(lbf[0:8, 384 + n * P:384 + (n + 1) * P], ones[0:8, :], lbf[0:8, 383:384],
                                  None, ALU.mult)
            dve.drain().then_inc(rel_rows, 1)
            dve.wait_ge(vec_made, 1)
            dve.tensor_copy(vec0[:, :], proj[0][:, 0, 0:48]).then_inc(c_row_made, 1)
            dve.wait_ge(c_row_made, 2)
            for a in range(2):
                c = slice(KT * a, KT * a + KT)
                stt(sc[:, :, a], sq[:, c], 1.0, vec0[:, c], ALU.add, ALU.mult)
            dve.drain()
            dve.tensor_scalar(sc[:, :, :], sc[:, :, :], 0.5, None, ALU.mult).then_inc(c_ready, 1)
            for b in range(5):
                n = P if b < 4 else DEC
                for k4 in range(4):
                    e = 4 * b + k4
                    dve.wait_ge(xt_made, e + 1)
                    dve.tensor_copy(xy[:, 4 * k4:4 * k4 + 4, b * P:b * P + n],
                                    misc[:, e % 4, :].rearrange("p (k n) -> p k n", k=4)[:, :, 0:n])\
                        .then_inc(xt_read, 1)

            def add_squares(dst, u):
                hold(dve, sq_made, u + 1)
                tt(dst, dst, sq[:, :], ALU.add)
                dve.drain().then_inc(sq_used, 1)

            def mean_square(ps, dst, n, value):
                hold(dve, ss_made, value)
                dve.tensor_scalar(halves(dst), wide(ps), 1.0 / n, EPS, ALU.mult, ALU.add)
                dve.drain()
                dve.reciprocal(dst, dst)
                dve.drain().then_inc(ms_ready, 1)

            with dve.Fori(0, DEPTH) as l:
                hold(dve, vec_made, l + 2)
                dve.tensor_copy(vec1[:, :], t_ps[:, 0:P])
                dve.tensor_copy(vec2[:, :], o_ps[:, 0:48])
                dve.drain().then_inc(vec_ready, 1)
                dve.tensor_scalar(hg[:, :], vec2[:, 0:KT], 0.5, None, ALU.mult)
                dve.tensor_scalar(hb[:, :, :], vec1[:, V1["b_rg"]:V1["lam"]]
                                  .rearrange("p (a g) -> p a g", a=2), 0.5, None, ALU.mult)

                def read_modulation(i):
                    for n in range(2):
                        hold(dve, ada_used, (l * ADA_BLOCKS + 2 * i + n + 1) * 4)
                        hold(dve, ada_turned, l * ADA_BLOCKS + 2 * i + n - 1)
                        dve.tensor_copy(ada_row[n], s_ps[n][0:2, :]).then_inc(ada_read, 1)

                with dve.Fori(0, ADA_BLOCKS // 2 - 2) as i:
                    read_modulation(i)
                e_, z_, z2, p_, m_ = (sp_[:, n, :] for n in range(5))
                hold(dve, lam_exp, l + 1)
                dve.tensor_scalar(z_, e_, 2.0, None, ALU.add)
                dve.tensor_scalar(m_, vec1[:, V1["lam"]:], -1.0, 0.0, ALU.mult, ALU.max)
                dve.drain()
                dve.reciprocal(z_, z_)
                dve.drain()
                tt(z_, z_, e_, ALU.mult)
                dve.drain()
                tt(z2, z_, z_, ALU.mult)
                dve.drain()
                dve.tensor_scalar(p_, z2, 1.0 / 17, 1.0 / 15, ALU.mult, ALU.add)
                dve.drain()
                for n in (13, 11, 9, 7, 5, 3, 1):
                    tt(p_, p_, z2, ALU.mult)
                    dve.drain()
                    dve.tensor_scalar(p_, p_, 1.0 / n, None, ALU.add)
                    dve.drain()
                stt(p_, z_, 2.0, p_, ALU.mult, ALU.mult)
                dve.drain()
                tt(p_, p_, m_, ALU.add)
                dve.drain()
                dve.tensor_scalar(sp_[:, 4, :], p_, 2.0, None, ALU.mult)
                dve.tensor_scalar(sp_[:, 5, :], p_, -4.0, None, ALU.mult)
                mean_square(proj[0], r_x, D_MODEL, l * 2 + 1)
                read_modulation(ADA_BLOCKS // 2 - 2)
                hold(dve, x_kept, 16 + l * KT * 16)
                hold(dve, r_ready, l * 4 + 1)
                for k in range(KT):
                    tt(xy[:, k, :], xy[:, k, :], r_x, ALU.mult)
                read_modulation(ADA_BLOCKS // 2 - 1)
                hold(dve, ada_turned, (l + 1) * ADA_BLOCKS)
                made = t_ps[:, 0:2 * ADA].rearrange("p (j a) -> p j a", a=2)
                for a in range(2):
                    tt(mod[:, :, a], made[:, :, a], vec1[:, 0:ADA], ALU.add)
                dve.drain()
                for a in range(2):
                    stt(mod[:, KT:2 * KT, a], mod[:, KT:2 * KT, a], 1.0,
                        vec1[:, V1["g_norm"]:V1["g_norm"] + KT], ALU.add, ALU.mult)
                dve.drain()

                def lower(k, base):
                    hold(dve, h_split, l * 2 * KT + base + k + 1)
                    tt(act_lo[:, k, :], xy[:, k, :], act_hi[:, k, :].bitcast(F32), ALU.subtract)\
                        .then_inc(h_low_v, 1)

                for k in range(KT):
                    for a, z, w in PARTS:
                        dve.tensor_scalar(xy[:, k, a:z], xy[:, k, a:z], mod[:, KT + k, w:w + 1],
                                          mod[:, k, w:w + 1], ALU.mult, ALU.add)
                    dve.drain().then_inc(norm_x, 1)
                    if k % 4 == 1 and k > 4:
                        lower(k - 2, 0)
                lower(KT - 1, 0)
                dve.drain()
                dve.memset(lb[0][:, 0:3], 0.0)
                dve.memset(lb[0][:, S0 + 3 + DEC:W + 4], 0.0)
                dve.memset(lb[0][:, S0:S0 + 3], 0.0)
                dve.drain().then_inc(pad_ready, 1)
                dve.memset(sqb[:, :, :], 0.0)
                dve.memset(acc[:, :], 0.0)

                def rotate(n, raw_parts, rot, b, table):
                    hold(dve, swapped, l * 17 + n + 1)
                    rows = rot.shape[0]
                    tt(halves(rot), wide(proj[b])[0:rows], halves(rope[0:rows, 1, :]), ALU.mult)
                    dve.drain().then_inc(bank_free[b], 1)
                    for x, a, z in raw_parts:
                        tt(x, x, rope[0:rows, 0, a:z], ALU.mult)
                    dve.drain()

                hold(dve, rope_in, (2 * l + 1) * 16)
                rotate(0, [(qi_raw[0:64, :], 0, T)], qi_rot[0:64, :], 0, 0)
                tt(qi_raw[0:64, :], qi_raw[0:64, :], qi_rot[0:64, :], ALU.add)
                dve.drain().then_inc(roped, 1)

                def query(q, b, first=False):
                    if not first:
                        hold(dve, idx_made, l * 64 + 8 * q)
                    rotate(q + 1, [(qi_raw[:, :], 0, T)], qi_rot[:, :], b, 0)
                    tt(qi_rot[:, :], qi_rot[:, :], qi_raw[:, :], ALU.add)
                    dve.drain().then_inc(roped, 1)

                def add_scores(q):
                    for e, (b, hh) in enumerate((b, hh) for b in (1, 2, 3, 4) for hh in range(2)):
                        hold(dve, idx_read, l * 64 + 8 * q + e + 1)
                        a = acc[0:NQ[b], ACC[b]:ACC[b] + NK[b]]
                        stt(a, s_sb[e % 2][0:NQ[b], 0:NK[b]],
                            kw_tok[0:NQ[b], b, bass.ds(IDX_DIM + 2 * q + hh, 1)], a, ALU.mult, ALU.add)\
                            .then_inc(relu_used, 1)
                        if hh == 0:
                            dve.drain()

                hold(dve, t_read, l * T_EV + 2)
                query(0, 1, True)
                add_scores(0)
                with dve.Fori(0, 3) as it:
                    query(2 * it + 1, 0)
                    add_scores(2 * it + 1)
                    query(2 * it + 2, 1)
                    add_scores(2 * it + 2)
                query(7, 0)
                add_scores(7)
                dve.drain()
                for b in (1, 2, 3):
                    end = ACC[b] + NK[b]
                    dve.memset(acc[0:CHUNK, end - CHUNK:end], NEG)
                dve.drain()

                def best(blocks, rows):
                    for n, b in enumerate(blocks):
                        dve.max(top8[0:rows, n, :], acc[0:rows, ACC[b]:ACC[b] + NK[b]])
                    dve.drain()
                    for n, b in enumerate(blocks):
                        a = acc[0:rows, ACC[b]:ACC[b] + NK[b]]
                        dve.match_replace(a, top8[0:rows, n, :], a, TAKEN)
                    dve.drain()

                def col(v, base, g):
                    return v[:, bass.ds(base + g, 1)]

                def convolve(g):
                    state = vec2[:, V2["state_conv"]:V2["state_conv"] + 3 * G]\
                        .rearrange("p (j g) -> p j g", g=G)
                    dve.tensor_copy(lb[0][:, S0:S0 + 3], state[:, :, bass.ds(g, 1)]
                                    .rearrange("p j a -> p (j a)"))
                    hold(dve, evac, l * OUT + LRU + 2 * g + 1)
                    dve.drain()
                    x, y = lb[0], lb[1][:, 0:W]
                    dve.tensor_copy(stat[:, 0:3, bass.ds(g, 1)].rearrange("p j a -> p (j a)"),
                                    x[:, SEQ:SEQ + 3])
                    dve.tensor_copy(stat[:, 4:7, bass.ds(g, 1)].rearrange("p j a -> p (j a)"),
                                    x[:, S0 + DEC:S0 + DEC + 3])
                    dve.tensor_scalar(y, x[:, 0:W], col(vec1, V1["conv_w"], g), col(vec1, V1["conv_b"], g),
                                      ALU.mult, ALU.add)
                    for j in range(1, CONV_W):
                        dve.drain()
                        stt(y, x[:, j:j + W], col(vec1, V1["conv_w"] + j * G, g), y, ALU.mult, ALU.add)
                    dve.drain().then_inc(conv_ready, 1)

                def gate_path(t, b, dst):
                    hold(dve, evac, l * OUT + t + 1)
                    stt(halves(dst), halves(z_t[:, :]), 1.0, wide(proj[b]), ALU.add, ALU.mult)
                    dve.drain().then_inc(bank_free[b], 1)
                    dve.drain().then_inc(zs_ready, 1)

                def tile(v, j):
                    if isinstance(j, int):
                        return v[:, j, :]
                    return v[:, bass.ds(j, 1), :].rearrange("p a n -> p (a n)")

                def recur(g):
                    hold(dve, root_made, l * G + g + 1)
                    x, s, ti, t, a = (lb[n][:, 0:W] for n in (1, 2, 3, 4, 5))
                    stt(s, a, 1.0, s, ALU.add, ALU.mult)
                    stt(t, a, 1.0, t, ALU.add, ALU.mult)
                    stt(ti, ti, 1.0, x, ALU.add, ALU.mult)
                    dve.drain()
                    dve.tensor_scalar(a, t, -1.0, 1.0, ALU.mult, ALU.add)
                    stt(s, s, 0.5, ti, ALU.mult, ALU.mult)
                    dve.drain()
                    dve.tensor_tensor_scan(t[:, 0:SEQ], a[:, 0:SEQ], s[:, 0:SEQ], 0.0, ALU.mult, ALU.add)
                    dve.tensor_tensor_scan(t[:, S0:S0 + DEC], a[:, S0:S0 + DEC], s[:, S0:S0 + DEC],
                                           col(vec2, V2["state_lru"], g), ALU.mult, ALU.add)
                    dve.drain().then_inc(hs_ready, 1)
                    dve.tensor_copy(stat[:, 3, bass.ds(g, 1)], t[:, SEQ - 1:SEQ])
                    dve.tensor_copy(stat[:, 7, bass.ds(g, 1)], t[:, S0 + DEC - 1:S0 + DEC])
                    y = tile(xy, g)
                    for a_, z_, at_ in ((0, SEQ, 0), (SEQ, T, S0)):
                        stt(y[:, a_:z_], t[:, at_:at_ + z_ - a_], col(hg, 0, g), y[:, a_:z_],
                            ALU.mult, ALU.mult)
                    add_squares(sqb[:, 0, :], l * SQ_U + g)

                def recurrent_block(g, first=False):
                    if not first:
                        recur(g - 1)
                    convolve(g)
                    for _ in range(2):
                        best((1, 2, 3), P)
                    gate_path(LRU + 1 + 2 * g, 0, tile(xy, g))

                recurrent_block(0, True)
                with dve.Fori(1, G) as g:
                    recurrent_block(g)

                def head_side(h, s):
                    def logits(b):
                        turned = t_no(h - 1, 7) if b < 2 else t_no(h, {2: 2, 3: 3, 4: 5}[b])
                        hold(dve, t_made, l * T_EV + turned + 1)
                        hold(dve, s_made, l * 40 + 5 * h + b + 1)
                        if h >= HEADS:
                            mask = selm[0:NQ[b], SEL[b]:SEL[b] + NK[b]]
                        elif b < 4:
                            mask = bias[:, 0:NK[b]][:, ::-1]
                        else:
                            mask = bias[0:DEC, CHUNK:CHUNK + NS][:, ::-1]
                        x = s_sb[b % 2][0:NQ[b], 0:NK[b]]
                        stt(x, s_ps[b % 2][0:NQ[b], 0:NK[b]], -SCALE, mask, ALU.mult, ALU.subtract)
                        dve.drain().then_inc(s_read, 1)
                        dve.tensor_reduce(nmx[0:NQ[b], b % 2:b % 2 + 1], x, AX.X, ALU.min)
                        dve.drain().then_inc(y_neg, 1)

                    def normalise(b):
                        hold(dve, exp_made, l * 40 + 5 * h + b + 1)
                        r = rinv[0:NQ[b], b % 2:b % 2 + 1]
                        dve.reciprocal(r, rsum[0:NQ[b], b % 2:b % 2 + 1])
                        dve.drain()
                        x = s_sb[b % 2][0:NQ[b], 0:NK[b]]
                        dve.tensor_scalar(x, x, r, None, ALU.mult)
                        dve.drain().then_inc(p_ready, 1)

                    if s == 0:
                        if h < HEADS:
                            hold(dve, bias_in, (l * HEADS + h + 1) * 16)
                        logits(0)
                        logits(1)
                        normalise(0)
                        normalise(1)
                    elif s in (2, 3, 5):
                        b = {2: 2, 3: 3, 5: 4}[s]
                        logits(b)
                        normalise(b)
                    elif s in (7, 8):
                        a, z = (0, SEQ) if s == 7 else (SEQ, T)
                        hold(dve, o_made, l * 40 + 5 * h + s - 3)
                        y = xy[:, G + h, a:z]
                        stt(y, o_ps[:, 0:z - a], hg[:, G + h:G + h + 1], y, ALU.mult, ALU.mult)
                        dve.drain().then_inc(o_read_v, 1)
                        if s == 8:
                            add_squares(sqb[:, 1 + h // HEADS, :], l * SQ_U + G + h)

                def norm_branches(j0, j1):
                    for j in range(j0, j1):
                        n = 0 if j < G else 1 if j < G + HEADS else 2
                        if j in (0, G, G + HEADS):
                            hold(dve, r_ready, l * 4 + 2 + n)
                        tt(xy[:, j, :], xy[:, j, :], r_b[n], ALU.mult).then_inc(norm_x, 1)

                for h in range(9):
                    for s in range(8):
                        t = HEAD + 4 * h + s // 2
                        if h == 0 and s == 1:
                            recur(G - 1)
                            dve.drain().then_inc(stat_ready, 1)
                        if h == 0 and s == 3:
                            for _ in range(TOPK_S // 8):
                                best((4,), DEC)
                            for b in (1, 2, 3, 4):
                                dve.tensor_scalar(selm[0:NQ[b], SEL[b]:SEL[b] + NK[b]],
                                                  acc[0:NQ[b], ACC[b]:ACC[b] + NK[b]],
                                                  0.5 * TAKEN, NEG, ALU.is_gt, ALU.mult)
                            dve.drain()
                        if h == 6 and s < 4:
                            hold(dve, t_made, l * T_EV + t_no(5, s))
                            r = r_b[s // 2]
                            dve.tensor_scalar(r[:, s % 2 * HALF:][:, 0:HALF], t_ps[:, 0:HALF],
                                              1.0 / (D_LRU, D_LRU // 2)[s // 2], EPS, ALU.mult, ALU.add)
                            dve.drain().then_inc(t_read, 1)
                            if s % 2:
                                dve.reciprocal(r, r)
                                dve.drain().then_inc(ms_ready, 1)
                        if HEADS <= h < 8 and s in (2, 4):
                            part = s // 2 - 1
                            x = (q_t if part == 0 else k_t)[h % 2][0:32]
                            parts = [(x, 0, T)] if part == 0 else \
                                [(x[:, 0:SEQ], 0, SEQ), (x[:, NEW_K:KEYS], SEQ, T)]
                            hold(dve, rope_in, (2 * l + 2) * 16)
                            rotate(9 + 2 * (h - HEADS) + part, parts, d_rot[0:32, 0:T], (t - 1) % 2, 1)
                            for y, a, z in parts:
                                tt(y, y, d_rot[0:32, a:z], ALU.add)
                            dve.drain().then_inc(roped, 1)
                        if h > 1 and s == 0:
                            head_side(h - 2, 8)
                        if h > 0:
                            head_side(h - 1, s)
                        if h < 8 and s == 7:
                            gate_path(t, t % 2, xy[:, G + h, :])
                        if h == 7 and s < 6:
                            norm_branches(2 * s, 2 * s + 2)
                        if h == 8 and 1 <= s < 4:
                            lower(4 * s - 1, KT)
                head_side(7, 8)
                dve.drain().then_inc(sqc_ready, 1)
                dve.memset(sqx, 0.0)
                mean_square(misc[:, 0:2], r_b[2], D_LRU // 2, l * 2 + 2)
                norm_branches(G + HEADS, KT)
                lower(KT - 1, KT)

                def out_tile(j, jj, s):
                    b = (OUT + s) % 2
                    hold(dve, chunks_used, chunk_no(l, OUT + j, 4) + (3 if isinstance(j, int) and j == 0 else 0))
                    hold(dve, old_in[s], (l * 4 + jj + 1) * 16)
                    x = tile(xy, j)
                    for half, a, z, w in ((0, 0, HALF, 0), (1, HALF, SEQ, 0), (1, SEQ, T, 1)):
                        gate = mod[:, 2 * KT + j, w:w + 1] if isinstance(j, int) else \
                            mod[:, bass.ds(2 * KT + j, 1), w:w + 1].rearrange("p a n -> p (a n)")
                        stt(x[:, a:z], proj[b][:, half, a - half * HALF:z - half * HALF], gate,
                            x_old[s][:, a:z], ALU.mult, ALU.add)
                    dve.drain().then_inc(bank_free[b], 1)
                    dve.drain().then_inc(x_new, 1)
                    add_squares(sqx, l * SQ_U + KT + j)

                for s in range(4):
                    out_tile(s, 0, s)
                with dve.Fori(1, 4) as jj:
                    for s in range(4):
                        out_tile(4 * jj + s, jj, s)
                dve.drain().then_inc(x_whole, 1)

            mean_square(proj[0], r_x, D_MODEL, DEPTH * 2 + 1)
            dve.wait_ge(x_kept, 16 + DEPTH * KT * 16)
            dve.wait_ge(r_ready, DEPTH * 4 + 1)
            for k in range(KT):
                stt(xy[:, k, :], xy[:, k, :], vec0[:, 32 + k:33 + k], r_x, ALU.mult, ALU.mult)\
                    .then_inc(yn_made, 1)


_INS = ["x_prompt", "x_sample", "c_prompt", "c_sample", "state_conv", "state_lru", "cache_band_k",
        "cache_band_v", "cache_dsa_k", "cache_dsa_v", "cache_dsa_idx_k", "g_norm", "w_ada", "b_ada",
        "w_in", "conv_w", "conv_b", "w_rg", "b_rg", "w_ig", "b_ig", "lru_lambda", "rel_bias",
        "g_branch", "w_out", "g_final"]
_OUTS = {
    "y_prompt": (1, SEQ, D_MODEL), "y_sample": (1, DEC, D_MODEL),
    "p_conv": (DEPTH, 1, CONV_W - 1, D_LRU), "p_lru": (DEPTH, 1, D_LRU),
    "p_band_k": (DEPTH, 1, SEQ, HEADS, HD), "p_band_v": (DEPTH, 1, SEQ, HEADS, HD),
    "p_dsa_k": (DEPTH, 1, SEQ, HEADS, HD), "p_dsa_v": (DEPTH, 1, SEQ, HEADS, HD),
    "p_dsa_idx_k": (DEPTH, 1, SEQ, IDX_DIM),
    "s_conv": (DEPTH, 1, CONV_W - 1, D_LRU), "s_lru": (DEPTH, 1, D_LRU),
    "s_band_k": (DEPTH, 1, DEC, HEADS, HD), "s_band_v": (DEPTH, 1, DEC, HEADS, HD),
    "s_dsa_k": (DEPTH, 1, DEC, HEADS, HD), "s_dsa_v": (DEPTH, 1, DEC, HEADS, HD),
    "s_dsa_idx_k": (DEPTH, 1, DEC, IDX_DIM),
}


def _rotary(rows, group, width):
    pos = np.concatenate([np.arange(SEQ), PAST + np.arange(DEC)]).astype(np.float32)
    half = width // 2
    inv = np.float32(ROPE_THETA) ** (-np.arange(half, dtype=np.float32) / np.float32(half))
    ang = pos[None] * inv[:, None].astype(np.float32)
    table = np.zeros((rows, 2, T), np.float32)
    table[:, 0] = 1
    for r in range(0, rows, group):
        table[r:r + half, 0] = table[r + half:r + width, 0] = np.cos(ang)
        table[r:r + half, 1] = -np.sin(ang)
        table[r + half:r + width, 1] = np.sin(ang)
    return table


def _swaps(rows, group, width):
    m = np.zeros((rows, rows), np.float32)
    for r in range(0, rows, group):
        for n in range(width):
            m[r + n, r + (n + width // 2) % width] = 1
    return m


def _constants():
    return {
        "ident": np.eye(P, dtype=np.float32), "ones": np.ones((P, P), np.float32),
        "swap_i": _swaps(P, 64, 16), "swap_d": _swaps(32, 32, 32),
        "blocked": np.full((8, CHUNK, CHUNK), NEG, np.float32),
        "rope_i": _rotary(P, 64, 16), "rope_d": _rotary(32, 32, 32),
    }


def kernel(**inputs):
    import concourse.bacc as bacc
    from concourse.bass_utils import run_bass_kernel_spmd

    nc = bacc.Bacc("TRN2", target_bir_lowering=False, num_devices=1)
    arrays, ins, outs = {}, {}, {}
    for name in _INS:
        arrays[f"in_{name}"] = np.ascontiguousarray(inputs[name])
    for name, a in _constants().items():
        arrays[f"in_{name}"] = a
    for name, a in arrays.items():
        ins[name[3:]] = nc.dram_tensor(name, a.shape, mybir.dt.from_np(a.dtype), kind="ExternalInput").ap()
    for name, shape in _OUTS.items():
        outs[name] = nc.dram_tensor(f"out_{name}", shape, F32, kind="ExternalOutput").ap()
    scratch = {
        "rows": nc.dram_tensor("rel_rows", (8, 640), F32, kind="Internal").ap(),
        "windows": nc.dram_tensor("rel_windows", (8, P, 512), F32, kind="Internal").ap(),
        "x_keep": nc.dram_tensor("x_keep", (DEPTH + 1, P, KT, T), F32, kind="Internal").ap(),
    }
    build(nc, ins, outs, scratch)
    r = run_bass_kernel_spmd(nc, [arrays], core_ids=[0])
    return tuple(r.results[0][f"out_{name}"] for name in _OUTS)
```

```python
from contextlib import ExitStack

import concourse.bass as bass
import numpy as np
from concourse import mybir

F32 = mybir.dt.float32
F32R = mybir.dt.float32r
BF16 = mybir.dt.bfloat16
ALU = mybir.AluOpType
ACT = mybir.ActivationFunctionType
AX = mybir.AxisListType

P = 128
D_MODEL, SEQ, DEC, PAST, DEPTH = 2048, 512, 64, 256, 2
KT = D_MODEL // P
T = SEQ + DEC
HALF = T // 2
D_LRU, HEADS, HD = 1024, 4, 128
G = D_LRU // P
IDX_HEADS, IDX_DIM, TOPK, TOPK_S = 16, 64, 128, 80
CHUNK, CONV_W, EPS, NEG, TAKEN = 64, 4, 1e-6, -1e30, -3e38
REL = 256
SCALE = float(HD) ** -0.5
IDX_SCALE = float(IDX_DIM) ** -0.5 * float(IDX_HEADS) ** -0.5
ROPE_THETA = 500000.0

KI = 0
QI = 1
LRU = QI + 8
HEAD = LRU + 2 * G
OUT = HEAD + 8 * 4
TILES = OUT + KT
RING = 4
KC = 4
CHUNKS = TILES * 4
USES = ((TILES + 1) // 2, TILES // 2)
COL_XA, COL_ZA, COL_HEADS = 0, D_LRU, 2 * D_LRU
COL_QI = COL_HEADS + 2 * 4 * HEADS * HD
COL_KI = COL_QI + IDX_HEADS * IDX_DIM
ADA = 3 * KT
AB = 512
ADA_BLOCKS = ADA * P // AB
GATE = 2 * D_MODEL // AB
NEW_K = SEQ + PAST
KEYS = NEW_K + DEC
NS = PAST + DEC
W = SEQ + 3 + DEC + 1
S0 = SEQ + 3
WH = W // 2
ACC = {1: 0, 2: 256, 3: 640, 4: 1152}
SEL = {0: 0, 1: 128, 2: 384, 3: 768, 4: 1280}
NK = {0: 128, 1: 256, 2: 384, 3: 512, 4: NS}
NQ = {0: P, 1: P, 2: P, 3: P, 4: DEC}

V1 = {"b_ada": 0, "g_norm": 48, "conv_w": 64, "conv_b": 96, "b_rg": 104, "b_ig": 112, "lam": 120}
V2 = {"g_branch": 0, "state_lru": 16, "state_conv": 24}


def head_col(h, part):
    return COL_HEADS + ((h // HEADS) * 4 + part) * HEADS * HD + (h % HEADS) * P


def build(nc, inp, out, scratch):
    with ExitStack() as ctx:
        def sb(name, shape, dt=F32):
            return ctx.enter_context(nc.sbuf_tensor(name, shape, dt))

        started = []
        start = {}

        def sem(name, at=0):
            start[name] = at
            s = ctx.enter_context(nc.semaphore(name))
            if at:
                started.append((s, at))
            return s

        xy = sb("xy", [P, KT, T])
        act_hi = sb("act_hi", [P, KT, T], F32R)
        act_lo = sb("act_lo", [P, KT, T], F32R)
        raw = sb("raw", [P, RING, KC, P])
        w_hi = sb("w_hi", [P, RING, KC, P], F32R)
        w_lo = sb("w_lo", [P, RING, KC, P], F32R)
        work = sb("work", [P, 8192])
        lbf = sb("lb", [P, 3 * 584])
        rope = sb("rope", [P, 2, T])
        ki_t = sb("ki_t", [P, KEYS])
        qi_raw = sb("qi_raw", [P, T])
        acc = sb("acc", [P, 1472])
        selm = sb("selm", [P, 1600], BF16)
        kw_tok = sb("kw_tok", [P, 5, 80])
        ci = sb("ci", [P, 2, IDX_DIM])
        top8 = sb("top8", [P, 3, 8])
        w_rg = sb("w_rg", [P, P])
        w_ig = sb("w_ig", [P, P])
        sq = sb("sq", [P, T])
        sqb = sb("sqb", [P, 3, T])
        sqx = sqb[:, 0, :]
        ident = sb("ident", [P, P])
        ones = sb("ones", [P, P])
        swap_i = sb("swap_i", [P, P])
        swap_d = sb("swap_d", [32, 32])
        vec1 = sb("vec1", [P, P])
        vec2 = sb("vec2", [P, 48])
        vec0 = sb("vec0", [P, 32])
        sc = sb("sc", [P, KT, 2])
        mod = sb("mod", [P, ADA, 2])
        hg = sb("hg", [P, KT])
        hb = sb("hb", [P, 2, G])
        sp_ = sb("sp", [P, 6, G])
        stat = sb("stat", [P, 8, G])
        stat_r = sb("stat_r", [64, P])
        nmx = sb("nmx", [P, 2])
        rsum = sb("rsum", [P, 2])
        rinv = sb("rinv", [P, 2])
        eps = sb("eps", [P, 1])
        r_tok = sb("r_tok", [P, 5])

        at = 0

        def cut(n):
            nonlocal at
            at += n
            return work[:, at - n:at]

        q_t = [cut(T) for _ in range(2)]
        k_t = [cut(KEYS) for _ in range(2)]
        s_sb = [cut(512) for _ in range(2)]
        relu = s_sb + q_t
        v_t = cut(T)
        qi_rot = v_t
        ck = cut(2 * P).rearrange("p (b n) -> p b n", b=2)
        cv = cut(2 * P).rearrange("p (b n) -> p b n", b=2)
        bias = cut(512)
        first = at
        p_t = [cut(512) for _ in range(2)]
        v_tok = cut(5 * P).rearrange("p (b n) -> p b n", b=5)
        k_tok = cut(5 * P).rearrange("p (b n) -> p b n", b=5)
        lb = [work[:, first + n * 584:first + (n + 1) * 584] for n in range(2)] \
            + [lbf[:, n * 584:(n + 1) * 584] for n in range(3)] \
            + [work[:, first + 2 * 584:first + 3 * 584]]
        vrow = acc[:, 0:2 * P].rearrange("p (a n) -> p a n", a=2)
        d_rot = lb[3]
        ada_w = work[:, :].rearrange("p (s k n) -> p s k n", s=4, k=KC)
        ada_row = [sqb[0:2, n, 0:AB] for n in (1, 2)]
        raw_flat = raw[:, :, :, :].rearrange("p c k n -> p (c k n)")
        XC = D_MODEL // 2
        x_row = [raw_flat[:, 0:XC], raw_flat[:, XC:2 * XC], lbf[:, 640:640 + XC],
                 rope[:, :, :].rearrange("p a n -> p (a n)")[:, 0:XC], acc[:, 2 * P:2 * P + XC]]
        g_row = work[:, 0:D_MODEL]
        y_row = [work[:, 2048 + 2048 * j:4096 + 2048 * j] for j in range(2)]
        r_x = lb[2][:, 0:T]
        r_b = [lb[n][:, 0:T] for n in (2, 4, 3)]
        z_t = qi_raw
        x_old = [lb[n][:, 0:T] for n in (2, 3, 4)] + [qi_raw[:, :]]

        proj = [ctx.enter_context(nc.psum_tensor(f"proj{b}", [P, 2, 512], F32)) for b in range(2)]
        misc = ctx.enter_context(nc.psum_tensor("misc", [P, 4, 512], F32))
        s_ps = [misc[:, 0, :], misc[:, 1, :]]
        t_ps = misc[:, 2, :]
        o_ps = misc[:, 3, :]
        idx_ps = s_ps + [o_ps, t_ps]

        c_in = sem("c_in")
        const_in = sem("const_in")
        x_in = [sem(f"x_in{s}") for s in range(5)]
        xt_made = sem("xt_made")
        xt_read = sem("xt_read")
        x_kept = sem("x_kept")
        x_whole = sem("x_whole")
        c_row_made = sem("c_row_made")
        c_ready = sem("c_ready")
        vec_in = sem("vec_in")
        vec_made = sem("vec_made")
        vec_ready = sem("vec_ready")
        ada_in = [sem(f"ada_in{s}") for s in range(4)]
        ada_used = sem("ada_used")
        ada_read = sem("ada_read", 2)
        mod_ready = sem("mod_ready")
        ada_turned = sem("ada_turned", 2)
        ss_made = sem("ss_made")
        ms_ready = sem("ms_ready")
        r_ready = sem("r_ready")
        norm_x = sem("norm_x", 1)
        pad_ready = sem("pad_ready")
        h_split = sem("h_split")
        h_low_g = sem("h_low_g")
        h_low_v = sem("h_low_v")
        raw_in = [sem(f"raw_in{s}") for s in range(RING)]
        hi_ready = sem("hi_ready")
        lo_ready = sem("lo_ready", RING)
        chunks_used = sem("chunks_used", RING)
        bank_free = [sem(f"bank_free{b}", 1) for b in range(2)]
        evac = sem("evac")
        swapped = sem("swapped")
        roped = sem("roped")
        rope_in = sem("rope_in")
        ci_in = sem("ci_in")
        ki_ready = sem("ki_ready")
        s_made = sem("s_made")
        s_read = sem("s_read", 1)
        idx_made = sem("idx_made", 1)
        idx_read = sem("idx_read", 1)
        relu_used = sem("relu_used", 1)
        t_made = sem("t_made", 1)
        t_read = sem("t_read", 1)
        exp_made = sem("exp_made")
        y_neg = sem("y_neg", 1)
        p_ready = sem("p_ready")
        o_made = sem("o_made", 1)
        o_read_a = sem("o_read_a", 1)
        o_read_v = sem("o_read_v", 1)
        zs_ready = sem("zs_ready", 1)
        gate_w_in = sem("gate_w_in")
        conv_ready = sem("conv_ready", 1)
        gates_made = sem("gates_made", 1)
        gates_read = sem("gates_read", 1)
        root_made = sem("root_made")
        hs_ready = sem("hs_ready", 1)
        sq_made = sem("sq_made")
        sq_used = sem("sq_used", 1)
        bias_in = sem("bias_in")
        ck_in = sem("ck_in")
        cv_in = sem("cv_in")
        ki_out = sem("ki_out", 16)
        tok_out = sem("tok_out", 16)
        stat_ready = sem("stat_ready")
        stat_out = sem("stat_out", 16)
        old_in = [sem(f"old_in{s}") for s in range(4)]
        rel_rows = sem("rel_rows")
        rel_out = sem("rel_out")
        lam_exp = sem("lam_exp")
        x_new = sem("x_new", 1)
        g_in = sem("g_in")
        yt_made = sem("yt_made")
        yt_read = sem("yt_read")
        y_out = [sem(f"y_out{s}") for s in range(2)]
        ticks = sem("ticks")

        def hold(eng, s, value):
            eng.wait_ge(s, value + start[s.name])
            eng.sem_inc(ticks, 1)

        def chunk_no(l, t, c):
            return l * CHUNKS + t * 4 + c

        def t_no(h, e):
            return 3 + 8 * h + e + (0 if h < 5 else min(e + 1, 4) if h == 5 else 4)

        def tile_made(eng, l, t):
            hold(eng, chunks_used, chunk_no(l, t, 4))

        block = ctx.enter_context(nc.Block())

        def wide(ps, n=HALF):
            return ps[:, :, 0:n]

        def halves(ap):
            return ap.rearrange("p (a n) -> p a n", a=2)

        def q_cols(b):
            return slice(b * P, b * P + NQ[b])

        def key_cols(b):
            return slice(0, NK[b]) if b < 4 else slice(SEQ, KEYS)

        PARTS = ((0, SEQ, 0), (SEQ, T, 1))
        T_EV = 3 + 8 * 8 + 4
        SQ_U = 33
        TOK = 32 * 16
        CONSTS = 4

        @block.sync
        def _(sp):
            for s, n in started:
                sp.sem_inc(s, n)
            for dst, src in (
                (ident[:, :], inp["ident"]),
                (vrow[0:16, 0, :], inp["c_prompt"].rearrange("a (r p) -> (a r) p", p=P)),
                (vrow[16:32, 0, :], inp["c_sample"].rearrange("a (r p) -> (a r) p", p=P)),
            ):
                sp.dma_start(dst, src).then_inc(c_in, 16)
            for i in range(10):
                b, slot, cols = i // 2, i % 5, slice(i % 2 * XC, (i % 2 + 1) * XC)
                if i >= 5:
                    sp.wait_ge(xt_read, 2 * (i - 4))
                src = inp["x_prompt"][0, b * P:(b + 1) * P, cols] if b < 4 else inp["x_sample"][0][:, cols]
                sp.dma_start(x_row[slot][0:src.shape[0], :], src).then_inc(x_in[slot], 16)
            for dst, src in (
                (ones[:, :], inp["ones"]), (swap_i[:, :], inp["swap_i"]), (swap_d[:, :], inp["swap_d"]),
                (lbf[0:8, 0:384], inp["rel_bias"].rearrange("l h n -> (l h) n")[:, REL - P + 1:]),
            ):
                sp.dma_start(dst, src).then_inc(const_in, 16)

            with sp.Fori(0, DEPTH) as l:
                hold(sp, vec_made, l + 1)
                hold(sp, norm_x, l * 2 * KT)
                for n, (name, row, rows) in enumerate((
                    ("b_ada", V1["b_ada"], ADA), ("g_norm", V1["g_norm"], KT),
                    ("conv_w", V1["conv_w"], 4 * G), ("conv_b", V1["conv_b"], G),
                    ("b_rg", V1["b_rg"], G), ("b_ig", V1["b_ig"], G), ("lru_lambda", V1["lam"], G),
                    ("g_branch", V2["g_branch"], KT), ("state_lru", V2["state_lru"], G),
                    ("state_conv", V2["state_conv"], 3 * G),
                )):
                    src = inp[name][l]
                    src = {1: lambda a: a.rearrange("(r p) -> r p", p=P),
                           2: lambda a: a.rearrange("a (r p) -> (a r) p", p=P),
                           3: lambda a: a.rearrange("a b (r p) -> (a b r) p", p=P)}[len(src.shape)](src)
                    sp.dma_start(vrow[row:row + rows, int(n > 6), :], src).then_inc(vec_in, 16)
                hold(sp, o_made, l * 40)
                hold(sp, tok_out, l * TOK)
                w_ada = inp["w_ada"][l].rearrange("(k p) n -> p k n", p=P)

                def load_ada(s, col):
                    sp.dma_start(ada_w[:, s], w_ada[:, s * KC:(s + 1) * KC, bass.ds(col, AB)])\
                        .then_inc(ada_in[s], 16)

                for s in range(4):
                    load_ada(s, 0)
                with sp.Fori(1, ADA_BLOCKS) as j:
                    for s in range(4):
                        hold(sp, ada_used, (l * ADA_BLOCKS + j) * 4 + (s - 3))
                        load_ada(s, j * AB)
                sp.dma_start(rope[:, :, :], inp["rope_i"]).then_inc(rope_in, 16)
                sp.dma_start(ci[:, :, :], inp["cache_dsa_idx_k"][l, 0].rearrange("(b p) n -> p b n", p=P))\
                    .then_inc(ci_in, 16)

                w_in = inp["w_in"][l].rearrange("(k p) n -> p k n", p=P)
                w_out = inp["w_out"][l].rearrange("(k p) n -> p k n", p=P)

                def load(w, t, col, width=P, cs=range(4)):
                    for c in cs:
                        hold(sp, lo_ready, chunk_no(l, t, c) + 1 - RING)
                        sp.dma_start(raw[:, c, :, 0:width],
                                     w[:, c * KC:(c + 1) * KC, bass.ds(col, width)]).then_inc(raw_in[c], 16)

                load(w_in, KI, COL_KI, 80)
                with sp.Fori(0, 8) as q:
                    load(w_in, QI + q, COL_QI + q * P)
                with sp.Fori(0, G) as g:
                    load(w_in, LRU + 2 * g, COL_XA + g * P)
                    load(w_in, LRU + 1 + 2 * g, COL_ZA + g * P)
                    hold(sp, gates_made, l * G + g)
                    sp.dma_start(w_rg[:, :], inp["w_rg"][l, g]).then_inc(gate_w_in, 16)
                    sp.dma_start(w_ig[:, :], inp["w_ig"][l, g]).then_inc(gate_w_in, 16)

                def load_head_extras(h, values):
                    kind = "band" if h < HEADS else "dsa"
                    if values:
                        hold(sp, o_made, (l * 8 + h) * 5)
                    else:
                        hold(sp, y_neg, (l * 8 + h) * 5)
                        if h < HEADS:
                            sp.dma_start(bias, scratch["windows"][l * HEADS + h]).then_inc(bias_in, 16)
                    src = inp[f"cache_{kind}_{'v' if values else 'k'}"][l, 0, :, h % HEADS, :]
                    sp.dma_start(cv if values else ck, src.rearrange("(b p) n -> p b n", p=P))\
                        .then_inc(cv_in if values else ck_in, 16)

                for h in range(8):
                    load(w_in, HEAD + 4 * h, head_col(h, 0))
                    if h > 0:
                        load_head_extras(h - 1, False)
                    if h == HEADS - 1:
                        sp.dma_start(rope[0:32, :, :], inp["rope_d"]).then_inc(rope_in, 16)
                    load(w_in, HEAD + 4 * h + 1, head_col(h, 1))
                    load(w_in, HEAD + 4 * h + 2, head_col(h, 2))
                    if h > 0:
                        load_head_extras(h - 1, True)
                    load(w_in, HEAD + 4 * h + 3, head_col(h, 3))
                load_head_extras(7, False)
                load(w_out, OUT, 0)
                load_head_extras(7, True)
                load(w_out, OUT + 1, P)
                load(w_out, OUT + 2, 2 * P, cs=(0, 1, 2))
                hold(sp, norm_x, (l + 1) * 2 * KT)
                for s in range(4):
                    sp.dma_start(x_old[s], scratch["x_keep"][l, :, s]).then_inc(old_in[s], 16)
                load(w_out, OUT + 2, 2 * P, cs=(3,))
                load(w_out, OUT + 3, 3 * P)
                with sp.Fori(1, 4) as jj:
                    for s in range(4):
                        hold(sp, x_new, l * KT + 4 * jj + (s - 3))
                        sp.dma_start(x_old[s], scratch["x_keep"][l, :, 4 * jj + s]).then_inc(old_in[s], 16)
                        load(w_out, OUT + s + 4 * jj, jj * 512 + s * P)

            hold(sp, o_made, DEPTH * 40)
            sp.dma_start(g_row, bass.AP(inp["g_final"].tensor, 0, [[0, P], [1, D_MODEL]])).then_inc(g_in, 16)
            for b in range(5):
                sp.wait_ge(yt_read, 4 * (b + 1))
                n = P if b < 4 else DEC
                dst = out["y_prompt"][0, b * P:(b + 1) * P, :] if b < 4 else out["y_sample"][0]
                sp.dma_start(dst, y_row[b % 2][0:n, :]).then_inc(y_out[b % 2], 16)
            sp.wait_ge(y_out[0], 48)
            sp.wait_ge(y_out[1], 32)
            hold(sp, tok_out, DEPTH * TOK)
            hold(sp, ki_out, DEPTH * 32)
            hold(sp, stat_out, DEPTH * 64)
            sp.wait_ge(x_kept, 64 + DEPTH * KT * 16)

        @block.gpsimd
        def _(pool):
            pool.wait_ge(c_ready, 1)
            pool.wait_ge(xt_read, 20)
            pool.tensor_tensor(sqx, xy[:, 0, :], xy[:, 0, :], ALU.mult)
            for k in range(1, KT):
                pool.tensor_tensor(sq[:, :], xy[:, k, :], xy[:, k, :], ALU.mult)
                pool.drain()
                pool.tensor_tensor(sqx, sqx, sq[:, :], ALU.add)
                pool.drain()
            pool.drain().then_inc(x_whole, 1)

            def lower(l, base, k0=0, k1=KT):
                for k in range(k0, k1):
                    if k % 2 == 0:
                        pool.wait_ge(h_split, l * 2 * KT + base + k + 1)
                        pool.tensor_tensor(act_lo[:, k, :], xy[:, k, :], act_hi[:, k, :].bitcast(F32),
                                           ALU.subtract).then_inc(h_low_g, 1)

            def split(l, t, width=P, cs=range(4)):
                for c in cs:
                    pool.wait_ge(hi_ready, chunk_no(l, t, c) + 1)
                    pool.tensor_tensor(w_lo[:, c, :, 0:width], raw[:, c, :, 0:width],
                                       w_hi[:, c, :, 0:width].bitcast(F32), ALU.subtract)\
                        .then_inc(lo_ready, 1)

            with pool.Fori(0, DEPTH) as l:
                lower(l, 0)
                split(l, KI, 80)
                with pool.Fori(1, OUT + 1) as t:
                    split(l, t)
                lower(l, KT, 0, G + HEADS)
                split(l, OUT + 1, cs=(0, 1, 2))
                lower(l, KT, G + HEADS, KT)
                split(l, OUT + 1, cs=(3,))
                with pool.Fori(OUT + 2, TILES) as t:
                    split(l, t)

        @block.tensor
        def _(pe):
            pe.wait_ge(c_in, 48)
            pe.transpose(proj[0][:, 0, 0:32], vrow[0:32, 0, :], ident[0:32, 0:32]).then_inc(vec_made, 1)
            for b in range(5):
                n = P if b < 4 else DEC
                for k4 in range(4):
                    e = 4 * b + k4
                    slot = e // 2 % 5
                    pe.wait_ge(x_in[slot], 16 * (e // 10 + 1))
                    if e >= 4:
                        pe.wait_ge(xt_read, e - 3)
                    for k in range(4):
                        c = (e % 2 * 4 + k) * P
                        m = pe.transpose(misc[:, e % 4, k * P:k * P + n], x_row[slot][0:n, c:c + P],
                                         ident[0:n, 0:n])
                    m.then_inc(xt_made, 1)

            def sum_squares(ps, src):
                for half in range(2):
                    m = pe.matmul(ps[:, half, 0:HALF], ones[:, :], src[:, half * HALF:(half + 1) * HALF],
                                  start=True, stop=True)
                m.then_inc(ss_made, 1)

            pe.wait_ge(xt_read, 20)
            pe.wait_ge(c_ready, 1)

            with pe.Fori(0, DEPTH) as l:

                def modulate(j, n):
                    hold(pe, ada_read, l * ADA_BLOCKS + j - 1)
                    for s in range(4):
                        hold(pe, ada_in[s], (l * ADA_BLOCKS + j + 1) * 16)
                        for kk in range(KC):
                            k = s * KC + kk
                            m = pe.matmul(s_ps[n][0:2, :], sc[:, k, :], ada_w[:, s, kk, :],
                                          start=(k == 0), stop=(k == KT - 1))
                        m.then_inc(ada_used, 1)

                def turn_modulation(j, n):
                    hold(pe, ada_read, l * ADA_BLOCKS + j + 1)
                    for i in range(AB // P):
                        m = pe.matmul(t_ps[:, bass.ds(j * 8 + 2 * i, 2)], ada_row[n][:, i * P:(i + 1) * P],
                                      ident[0:2, 0:2], start=True, stop=True)
                    m.then_inc(ada_turned, 1)

                modulate(0, 0)
                hold(pe, vec_in, (l + 1) * 160)
                pe.transpose(t_ps[:, 0:P], vrow[:, 0, :], ident[:, :])
                pe.transpose(o_ps[:, 0:48], vrow[0:48, 1, :], ident[0:48, 0:48]).then_inc(vec_made, 1)
                hold(pe, vec_ready, l + 1)

                def two_blocks(i):
                    modulate(2 * i + 1, 1)
                    turn_modulation(2 * i, 0)
                    modulate(2 * i + 2, 0)
                    turn_modulation(2 * i + 1, 1)

                with pe.Fori(0, 2) as i:
                    two_blocks(i)
                hold(pe, x_whole, l + 1)
                hold(pe, bank_free[0], l * USES[0])
                sum_squares(proj[0], sqx)
                with pe.Fori(2, GATE // 2) as i:
                    two_blocks(i)
                modulate(GATE + 1, 1)
                hold(pe, mod_ready, 2 * l + 1)
                for j in range(GATE, ADA_BLOCKS):
                    turn_modulation(j, j % 2)
                    if j + 2 < ADA_BLOCKS:
                        modulate(j + 2, j % 2)

                def chunks(t, b, use, cs, width=P, acts=None):
                    for c in cs:
                        if c == 0:
                            pe.wait_ge(bank_free[b], l * USES[b] + use + 1)
                        if acts is not None:
                            pe.wait_ge(h_low_g, (l * 2 * KT + acts + (c + 1) * KC) // 2)
                            pe.wait_ge(h_low_v, (l * 2 * KT + acts + (c + 1) * KC) // 2)
                        pe.wait_ge(lo_ready, chunk_no(l, t, c) + 1 + RING)
                        for kk in range(KC):
                            k = c * KC + kk
                            for half in range(2):
                                cols = slice(half * HALF, (half + 1) * HALF)
                                dst = proj[b][0:width, half, 0:HALF]
                                pe.matmul(dst, w_hi[:, c, kk, 0:width], act_hi[:, k, cols],
                                          start=(k == 0), stop=False)
                                pe.matmul(dst, w_hi[:, c, kk, 0:width], act_lo[:, k, cols],
                                          start=False, stop=False)
                            for half in range(2):
                                cols = slice(half * HALF, (half + 1) * HALF)
                                m = pe.matmul(proj[b][0:width, half, 0:HALF], w_lo[:, c, kk, 0:width],
                                              act_hi[:, k, cols], start=False, stop=(k == KT - 1))
                        m.then_inc(chunks_used, 1)

                def swap(t_evac, b, perm, src, n, keys=False):
                    hold(pe, evac, l * OUT + t_evac + 1)
                    parts = ((0, 0, 0, HALF), (1, 0, HALF, T)) if not keys else \
                        ((0, 0, 0, HALF), (1, 0, HALF, SEQ), (1, SEQ - HALF, NEW_K, KEYS))
                    for half, at_, a, z in parts:
                        m = pe.matmul(proj[b][0:n, half, at_:at_ + z - a], perm, src[0:n, a:z],
                                      start=True, stop=True, skip_group_check=at_ > 0)
                    m.then_inc(swapped, 1)

                def t_event(e):
                    hold(pe, t_read, l * T_EV + e)

                def scores(q, first=False):
                    hold(pe, roped, l * 17 + q + 2)
                    for e, (b, hh) in enumerate((b, hh) for b in (1, 2, 3, 4) for hh in range(2)):
                        hold(pe, idx_read, l * 64 + (8 * q + e - 3 if not first or e > 3 else 0))
                        rows = slice(64 * hh, 64 * hh + 64)
                        pe.matmul(idx_ps[e % 4][0:NQ[b], 0:NK[b]], qi_rot[rows, q_cols(b)],
                                  ki_t[rows, key_cols(b)], start=True, stop=True).then_inc(idx_made, 1)

                chunks(KI, 0, 0, range(4), 80, acts=0)
                chunks(QI, 1, 0, (0, 1))
                swap(KI, 0, swap_i[0:64, 0:64], qi_raw, 64)
                hold(pe, ci_in, (l + 1) * 16)
                hold(pe, mod_ready, 2 * l + 2)
                t_event(0)
                for b in range(2):
                    m = pe.transpose(t_ps[0:64, b * P:(b + 1) * P], ci[:, b, :], ident[:, :])
                m.then_inc(t_made, 1)
                chunks(QI, 1, 0, (2, 3))
                hold(pe, roped, l * 17 + 1)
                t_event(1)
                for b in range(5):
                    m = pe.transpose(t_ps[0:NQ[b], b * 80:b * 80 + 80], qi_raw[0:80, q_cols(b)],
                                     ident[0:80, 0:80])
                m.then_inc(t_made, 1)

                def query_tile(q, b, use, first=False):
                    chunks(QI + q, b, use, (0, 1))
                    swap(QI - 1 + q, 1 - b, swap_i[:, :], qi_raw, P)
                    chunks(QI + q, b, use, (2, 3))
                    if first:
                        hold(pe, ki_ready, l + 1)
                        hold(pe, t_read, l * T_EV + 2)
                    scores(q - 1, first)

                query_tile(1, 0, 1, True)
                with pe.Fori(0, 3) as it:
                    query_tile(2 * it + 2, 1, it + 1)
                    query_tile(2 * it + 3, 0, it + 2)

                def gates(g):
                    hold(pe, gates_read, l * G + g)
                    hold(pe, conv_ready, l * G + g + 1)
                    hold(pe, gate_w_in, (l * G + g + 1) * 32)
                    for n, w in enumerate((w_rg, w_ig)):
                        for half in range(2):
                            m = pe.matmul(misc[:, 2 * n + half, 0:WH], w[:, :],
                                          lb[1][:, half * WH:(half + 1) * WH], start=True, stop=True)
                    m.then_inc(gates_made, 1)

                def recurrent_block(g, first=False):
                    chunks(LRU + 2 * g, 1, g + 4, (0,))
                    if not first:
                        gates(g - 1)
                    chunks(LRU + 2 * g, 1, g + 4, (1,))
                    if first:
                        swap(QI + 7, 0, swap_i[:, :], qi_raw, P)
                    chunks(LRU + 2 * g, 1, g + 4, (2, 3))
                    if first:
                        scores(7)
                        hold(pe, idx_read, (l + 1) * 64)
                        t_event(2)
                    chunks(LRU + 1 + 2 * g, 0, g + 5, range(4))

                recurrent_block(0, True)
                with pe.Fori(1, G) as g:
                    recurrent_block(g)

                def head_side(h, s):
                    q, k = q_t[h % 2], k_t[h % 2]

                    def score(b):
                        if b < 2:
                            hold(pe, s_read, l * 40 + 5 * h)
                        else:
                            hold(pe, s_read, l * 40 + 5 * h + b - 1)
                        pe.matmul(s_ps[b % 2][0:NQ[b], 0:NK[b]], q[:, q_cols(b)], k[:, key_cols(b)],
                                  start=True, stop=True).then_inc(s_made, 1)

                    def turn(b, e):
                        t_event(t_no(h, e))
                        hold(pe, p_ready, l * 40 + 5 * h + b + 1)
                        for j in range(0, NK[b], P):
                            n = min(P, NK[b] - j)
                            m = pe.transpose(t_ps[0:n, j:j + NQ[b]], s_sb[b % 2][0:NQ[b], j:j + n],
                                             ident[0:NQ[b], 0:NQ[b]])
                        m.then_inc(t_made, 1)

                    def mix(b, e):
                        hold(pe, t_read, l * T_EV + t_no(h, e) + 1)
                        if b in (0, 4):
                            hold(pe, o_read_v, l * 16 + 2 * h + (b == 4))
                            hold(pe, o_read_a, l * 16 + 2 * h + (b == 4))
                        if b == 4:
                            hold(pe, cv_in, (l * 8 + h + 1) * 16)
                            vs = [cv[:, 0, :], cv[:, 1, :], v_tok[0:DEC, 4, :]]
                        else:
                            vs = [v_tok[:, j, :] for j in range(b + 1)]
                        for j, v in enumerate(vs):
                            c = (b % 4) * P
                            m = pe.matmul(o_ps[:, c:c + NQ[b]], v,
                                          p_t[b % 2][0:v.shape[0], j * P:j * P + NQ[b]],
                                          start=(j == 0), stop=(j == len(vs) - 1), skip_group_check=True)
                        m.then_inc(o_made, 1)

                    if s == 0:
                        hold(pe, evac, l * OUT + HEAD + 4 * h + 3)
                        t_event(t_no(h, 0))
                        for b in range(4):
                            m = pe.transpose(t_ps[:, b * P:(b + 1) * P], k[:, q_cols(b)], ident[:, :])
                        m.then_inc(t_made, 1)
                        score(0)
                        score(1)
                    elif s == 1:
                        t_event(t_no(h, 1))
                        for b in range(4):
                            m = pe.transpose(t_ps[:, b * P:(b + 1) * P], v_t[:, q_cols(b)], ident[:, :])
                        m.then_inc(t_made, 1)
                    elif s == 2:
                        turn(0, 2)
                        score(2)
                    elif s == 3:
                        turn(1, 3)
                        score(3)
                        mix(0, 2)
                    elif s == 4:
                        t_event(t_no(h, 4))
                        hold(pe, ck_in, (l * 8 + h + 1) * 16)
                        pe.transpose(t_ps[0:DEC, 0:P], k[:, NEW_K:KEYS], ident[:, :])
                        pe.transpose(t_ps[0:DEC, P:2 * P], v_t[:, SEQ:T], ident[:, :])
                        for b in range(2):
                            m = pe.transpose(t_ps[:, (2 + b) * P:(3 + b) * P], ck[:, b, :], ident[:, :])
                        m.then_inc(t_made, 1)
                        mix(1, 3)
                    elif s == 5:
                        turn(2, 5)
                        hold(pe, t_read, l * T_EV + t_no(h, 4) + 1)
                        score(4)
                    elif s == 6:
                        turn(3, 6)
                        mix(2, 5)
                    elif s == 7:
                        turn(4, 7)
                        mix(3, 6)
                    elif s == 8:
                        mix(4, 7)

                for h in range(9):
                    for s in range(8):
                        t, c = HEAD + 4 * h + s // 2, 2 * (s % 2)
                        if h < 8:
                            chunks(t, t % 2, t // 2, (c, c + 1))
                        if h == 0 and s == 0:
                            gates(G - 1)
                        if h == 6 and s < 4:
                            hold(pe, sq_used, l * SQ_U + G + HEADS)
                            t_event(t_no(5, s) - 1)
                            pe.matmul(t_ps[:, 0:HALF], ones[:, :], sqb[:, s // 2, s % 2 * HALF:][:, 0:HALF],
                                      start=True, stop=True).then_inc(t_made, 1)
                        if h > 1 and s == 0:
                            head_side(h - 2, 8)
                        if h > 0:
                            head_side(h - 1, s)
                        elif s == 6:
                            hold(pe, stat_ready, l + 1)
                            pe.transpose(t_ps[0:64, 0:P], stat[:, :, :].rearrange("p a g -> p (a g)"),
                                         ident[:, :]).then_inc(t_made, 1)
                        if HEADS <= h < 8 and s in (2, 4):
                            part = s // 2 - 1
                            src = (q_t if part == 0 else k_t)[h % 2]
                            swap(HEAD + 4 * h + part, (t - 1) % 2, swap_d[:, :], src, 32, part == 1)
                        if h == 8 and s < 6:
                            j = s // 3
                            chunks(OUT + j, 1 - j, OUT // 2 + j, (s % 3,), acts=None if j else KT)
                for half in range(2):
                    hold(pe, sq_used, l * SQ_U + KT + half)
                    pe.matmul(misc[:, half, 0:HALF], ones[:, :], sqb[:, 2, half * HALF:(half + 1) * HALF],
                              start=True, stop=True).then_inc(ss_made, 1)
                    if half == 0:
                        head_side(7, 8)

                def out_tile(j, b, use):
                    chunks(OUT + j, b, use, range(4))

                chunks(OUT, 1, OUT // 2, (3,), acts=KT)
                chunks(OUT + 1, 0, OUT // 2 + 1, (3,))
                with pe.Fori(1, KT // 2) as jj:
                    out_tile(2 * jj, 1, jj + OUT // 2)
                    out_tile(2 * jj + 1, 0, jj + OUT // 2 + 1)

            hold(pe, x_new, DEPTH * KT)
            for b in range(5):
                n = P if b < 4 else DEC
                for k4 in range(4):
                    e = 4 * b + k4
                    if e >= 4:
                        pe.wait_ge(yt_read, e - 3)
                    for k in range(4):
                        m = pe.transpose(misc[0:n, e % 4, k * P:(k + 1) * P], xy[:, 4 * k4 + k, b * P:b * P + n],
                                         ident[:, :])
                    m.then_inc(yt_made, 1)
                if b == 0:
                    pe.wait_ge(x_whole, DEPTH + 1)
                    hold(pe, bank_free[0], DEPTH * USES[0])
                    for c in range(5):
                        m = pe.matmul(proj[0][0:(P if c < 4 else DEC), 0, c:c + 1],
                                      sqx[:, c * P:min(c * P + P, T)], ones[:, 0:1], start=True, stop=True)
                    m.then_inc(ss_made, 1)

        @block.scalar
        def _(act):
            act.wait_ge(c_row_made, 1)
            act.activation(sq[:, 0:32], vec0[:, 0:32], ACT.Tanh, scale=0.5).then_inc(c_row_made, 1)

            def square(u, src, ready, value):
                hold(act, ready, value)
                hold(act, sq_used, u)
                act.activation(sq[:, :], src, ACT.Square).then_inc(sq_made, 1)

            act.wait_ge(rel_rows, 1)
            act.wait_ge(ada_used, 8)
            act.dma_start(scratch["rows"], lbf[0:8, 0:640]).then_inc(rel_out, 16)
            act.wait_ge(rel_out, 16)
            act.dma_start(scratch["windows"], bass.AP(scratch["rows"].tensor, 0, [[640, 8], [1, P], [1, 512]]))\
                .then_inc(rel_out, 16)
            act.wait_ge(rel_out, 32)
            act.dma_start(scratch["windows"][:, 0:CHUNK, 0:CHUNK], inp["blocked"]).then_inc(rel_out, 16)
            act.wait_ge(xt_read, 20)
            for c in range(4):
                act.wait_ge(ada_used, 8 + 4 * c)
                act.dma_start(scratch["x_keep"][0][:, c * KC:(c + 1) * KC], xy[:, c * KC:(c + 1) * KC, :])\
                    .then_inc(x_kept, 16)
            act.wait_ge(rel_out, 48)

            with act.Fori(0, DEPTH) as l:
                hold(act, vec_ready, l + 1)
                act.activation(sp_[:, 0, :], vec1[:, V1["lam"]:], ACT.Abs)
                act.drain()
                act.activation(sp_[:, 0, :], sp_[:, 0, :], ACT.Exp, scale=-1.0)
                act.drain().then_inc(lam_exp, 1)

                def root(r, n):
                    hold(act, ms_ready, l * 3 + n + 1)
                    act.activation(r, r, ACT.Sqrt).then_inc(r_ready, 1)

                def upper(t, cs, width=P, more=0):
                    for c in cs:
                        hold(act, raw_in[c], (l * TILES + t + 1) * 16)
                        hold(act, chunks_used, chunk_no(l, t, c) + 1 - RING + more)
                        act.activation(w_hi[:, c, :, 0:width], raw[:, c, :, 0:width], ACT.Copy)\
                            .then_inc(hi_ready, 1)

                root(r_x, 0)
                for k in range(KT):
                    hold(act, norm_x, l * 2 * KT + k + 1)
                    act.activation(act_hi[:, k, :], xy[:, k, :], ACT.Copy).then_inc(h_split, 1)

                def take(t, b, pairs, free):
                    for dst, src in pairs:
                        act.activation(dst, src, ACT.Copy)
                    act.drain().then_inc(evac, 1)
                    if free:
                        act.drain().then_inc(bank_free[b], 1)

                def t_take(e, pairs):
                    hold(act, t_made, l * T_EV + e + 1)
                    for dst, src in pairs:
                        act.activation(dst, src, ACT.Copy)
                    act.drain().then_inc(t_read, 1)

                upper(KI, range(4), 80)
                upper(QI, range(4))
                tile_made(act, l, KI)
                hold(act, zs_ready, l * 16)
                take(KI, 0, [(halves(qi_raw[0:80, :]), wide(proj[0])[0:80])], False)
                upper(QI + 1, (0, 1))
                t_take(0, [(ki_t[64 * n:64 * n + 64, SEQ:NEW_K], t_ps[0:64, 0:2 * P]) for n in range(2)])
                upper(QI + 1, (2, 3))
                hold(act, roped, l * 17 + 1)
                for n in range(2):
                    act.activation(ki_t[64 * n:64 * n + 64, 0:SEQ], qi_raw[0:64, 0:SEQ], ACT.Copy)
                    act.activation(ki_t[64 * n:64 * n + 64, NEW_K:KEYS], qi_raw[0:64, SEQ:T], ACT.Copy)
                act.drain().then_inc(ki_ready, 1)
                hold(act, ki_out, l * 32)
                t_take(1, [(kw_tok[:, 0:4, :], t_ps[:, 0:320].rearrange("p (b n) -> p b n", b=4)),
                           (kw_tok[0:DEC, 4, :], t_ps[0:DEC, 320:400])])
                act.dma_start(out["p_dsa_idx_k"][l, 0].rearrange("(b p) n -> p b n", p=P),
                              kw_tok[:, 0:4, 0:IDX_DIM]).then_inc(ki_out, 16)
                act.dma_start(out["s_dsa_idx_k"][l, 0], kw_tok[0:DEC, 4, 0:IDX_DIM]).then_inc(ki_out, 16)

                def take_query(q, b):
                    tile_made(act, l, QI + q)
                    hold(act, roped, l * 17 + q + 1)
                    take(QI + q, b, [(halves(qi_raw[:, :]), wide(proj[b]))], False)

                take_query(0, 1)

                def relus(q, first=False):
                    for e, (b, hh) in enumerate((b, hh) for b in (1, 2, 3, 4) for hh in range(2)):
                        hold(act, idx_made, l * 64 + 8 * q + e + 1)
                        hold(act, relu_used, l * 64 + (8 * q + e - 3 if not first or e > 3 else 0))
                        act.activation(relu[e % 4][0:NQ[b], 0:NK[b]], idx_ps[e % 4][0:NQ[b], 0:NK[b]],
                                       ACT.Relu, scale=IDX_SCALE).then_inc(idx_read, 1)

                def query_tile(q, b, first=False):
                    upper(QI + 1 + q, range(4))
                    take_query(q, b)
                    relus(q - 1, first)

                query_tile(1, 0, True)
                with act.Fori(0, 3) as it:
                    query_tile(2 * it + 2, 1)
                    query_tile(2 * it + 3, 0)

                def take_input(g):
                    tile_made(act, l, LRU + 2 * g)
                    hold(act, conv_ready, l * G + g)
                    hold(act, pad_ready, l + 1)
                    take(LRU, 1, [(lb[0][:, 3:3 + HALF], proj[1][:, 0, 0:HALF]),
                                  (lb[0][:, 3 + HALF:3 + SEQ], proj[1][:, 1, 0:SEQ - HALF]),
                                  (lb[0][:, S0 + 3:S0 + 3 + DEC], proj[1][:, 1, SEQ - HALF:HALF])], True)

                def take_gate_path(t, b, n):
                    tile_made(act, l, t)
                    hold(act, zs_ready, l * 16 + n)
                    act.activation(halves(z_t[:, :]), wide(proj[b]), ACT.Tanh, scale=0.5)
                    act.drain().then_inc(evac, 1)

                def gates(g):
                    hold(act, gates_made, l * G + g + 1)
                    hold(act, hs_ready, l * G + g)
                    for n in range(2):
                        act.activation(lb[2 + n][:, 0:W].rearrange("p (a n) -> p a n", a=2),
                                       misc[:, 2 * n:2 * n + 2, 0:WH], ACT.Tanh, scale=0.5,
                                       bias=hb[:, n, bass.ds(g, 1)])
                    act.drain().then_inc(gates_read, 1)
                    act.activation(lb[4][:, 0:W], lb[2][:, 0:W], ACT.Tanh,
                                   scale=sp_[:, 4, bass.ds(g, 1)], bias=sp_[:, 4, bass.ds(g, 1)])
                    act.activation(lb[5][:, 0:W], lb[2][:, 0:W], ACT.Exp,
                                   scale=sp_[:, 5, bass.ds(g, 1)], bias=sp_[:, 5, bass.ds(g, 1)])
                    act.drain()
                    act.activation(lb[2][:, 0:W], lb[4][:, 0:W], ACT.Sqrt)
                    act.drain().then_inc(root_made, 1)

                def square_states(g):
                    hold(act, hs_ready, l * G + g + 1)
                    hold(act, sq_used, l * SQ_U + g)
                    act.activation(sq[:, 0:SEQ], lb[4][:, 0:SEQ], ACT.Square)
                    act.activation(sq[:, SEQ:T], lb[4][:, S0:S0 + DEC], ACT.Square)
                    act.drain().then_inc(sq_made, 1)

                def recurrent_block(g, first=False):
                    upper(LRU + 1 + 2 * g, (0, 1))
                    if not first:
                        gates(g - 1)
                    upper(LRU + 1 + 2 * g, (2, 3))
                    take_input(g)
                    if first:
                        relus(7)
                    upper(LRU + 2 + 2 * g, (0, 1))
                    if not first:
                        square_states(g - 1)
                    upper(LRU + 2 + 2 * g, (2, 3))
                    take_gate_path(LRU + 1 + 2 * g, 0, g)

                recurrent_block(0, True)
                with act.Fori(1, G) as g:
                    recurrent_block(g)

                def head_side(h, s):
                    q, k = q_t[h % 2], k_t[h % 2]
                    kind = "band" if h < HEADS else "dsa"

                    def exp(b):
                        hold(act, y_neg, l * 40 + 5 * h + b + 1)
                        x = s_sb[b % 2][0:NQ[b], 0:NK[b]]
                        act.activation(x, x, ACT.Exp, scale=-1.0, bias=nmx[0:NQ[b], b % 2:b % 2 + 1],
                                       accum_out=rsum[0:NQ[b], b % 2:b % 2 + 1])
                        act.drain().then_inc(exp_made, 1)

                    def take_turned(b, e):
                        hold(act, o_made, l * 40 + 5 * h + max(b - 1, 0))
                        if b < 4:
                            t_take(t_no(h, e), [(p_t[b % 2][:, 0:NK[b]], t_ps[:, 0:NK[b]])])
                        else:
                            t_take(t_no(h, e), [
                                (p_t[0][:, 0:2 * P].rearrange("p (b n) -> p b n", b=2)[:, :, 0:DEC],
                                 t_ps[:, 0:2 * P].rearrange("p (b n) -> p b n", b=2)[:, :, 0:DEC]),
                                (p_t[0][0:DEC, 2 * P:2 * P + DEC], t_ps[0:DEC, 2 * P:2 * P + DEC])])

                    def give(name, dst, tile):
                        act.dma_start(dst, tile).then_inc(tok_out, 16)

                    if s == 0:
                        hold(act, tok_out, l * TOK + 64 * h)
                        t_take(t_no(h, 0), [(k_tok[:, 0:4, :], t_ps.rearrange("p (b n) -> p b n", b=4))])
                        give("k", out[f"p_{kind}_k"][l, 0, :, h % HEADS, :]
                             .rearrange("(b p) n -> p b n", p=P), k_tok[:, 0:4, :])
                        exp(0)
                        exp(1)
                    elif s == 1:
                        t_take(t_no(h, 1), [(v_tok[:, 0:4, :], t_ps.rearrange("p (b n) -> p b n", b=4))])
                        give("v", out[f"p_{kind}_v"][l, 0, :, h % HEADS, :]
                             .rearrange("(b p) n -> p b n", p=P), v_tok[:, 0:4, :])
                    elif s == 2:
                        take_turned(0, 2)
                        exp(2)
                    elif s == 3:
                        take_turned(1, 3)
                        exp(3)
                    elif s == 4:
                        t_take(t_no(h, 4), [(k_tok[0:DEC, 4, :], t_ps[0:DEC, 0:P]),
                                        (v_tok[0:DEC, 4, :], t_ps[0:DEC, P:2 * P]),
                                        (k[:, SEQ:NEW_K], t_ps[:, 2 * P:4 * P])])
                        give("k", out[f"s_{kind}_k"][l, 0, :, h % HEADS, :], k_tok[0:DEC, 4, :])
                        give("v", out[f"s_{kind}_v"][l, 0, :, h % HEADS, :], v_tok[0:DEC, 4, :])
                    elif s == 5:
                        take_turned(2, 5)
                        exp(4)
                    elif s == 6:
                        take_turned(3, 6)
                    elif s == 7:
                        take_turned(4, 7)
                        hold(act, o_read_v, l * 16 + 2 * h + 1)
                        hold(act, sq_used, l * SQ_U + G + h)
                        act.activation(sq[:, 0:SEQ], o_ps[:, 0:SEQ], ACT.Square).then_inc(o_read_a, 1)
                        if h == 7:
                            act.drain().then_inc(sq_made, 1)
                    elif s == 8:
                        hold(act, o_read_v, l * 16 + 2 * h + 2)
                        act.activation(sq[:, SEQ:T], o_ps[:, 0:DEC], ACT.Square)
                        act.drain().then_inc(o_read_a, 1)
                        act.drain().then_inc(sq_made, 1)

                def take_head(h, part):
                    t = HEAD + 4 * h + part
                    b = t % 2
                    if part == 3:
                        take_gate_path(t, b, G + h)
                        return
                    tile_made(act, l, t)
                    if part == 2 and h > 0:
                        hold(act, t_made, l * T_EV + t_no(h - 1, 4) + 1)
                    if part == 1:
                        pairs = [(k_t[h % 2][:, 0:HALF], proj[b][:, 0, 0:HALF]),
                                 (k_t[h % 2][:, HALF:SEQ], proj[b][:, 1, 0:SEQ - HALF]),
                                 (k_t[h % 2][:, NEW_K:KEYS], proj[b][:, 1, SEQ - HALF:HALF])]
                    else:
                        pairs = [(halves(q_t[h % 2] if part == 0 else v_t), wide(proj[b]))]
                    take(t, b, pairs, h < HEADS or part == 2)

                def upper_y(j0, j1):
                    for j in range(j0, j1):
                        if j % KC == 0:
                            hold(act, chunks_used, chunk_no(l, OUT - 1, j // KC + 1))
                        hold(act, norm_x, l * 2 * KT + KT + j + 1)
                        act.activation(act_hi[:, j, :], xy[:, j, :], ACT.Copy).then_inc(h_split, 1)

                for h in range(9):
                    for s in range(8):
                        t = HEAD + 4 * h + s // 2
                        if h == 7 and s == 7:
                            upper_y(0, 2 * KC)
                        if h < 8:
                            upper(t + 1, (0, 1) if s % 2 == 0 else (2, 3))
                            if s % 2:
                                take_head(h, s // 2)
                        if h == 0 and s == 0:
                            gates(G - 1)
                        if h == 0 and s == 4:
                            square_states(G - 1)
                        if h > 1 and s == 0:
                            head_side(h - 2, 8)
                        if h > 0:
                            head_side(h - 1, s)
                        elif s == 6:
                            hold(act, stat_out, l * 64)
                            t_take(2, [(stat_r[:, :], t_ps[0:64, 0:P])])
                            for n, name in enumerate(("p_conv", "p_lru", "s_conv", "s_lru")):
                                rows = slice((0, 24, 32, 56)[n], (24, 32, 56, 64)[n])
                                dst = out[name][l]
                                dst = dst.rearrange("a (g p) -> (a g) p", p=P) if n % 2 else \
                                    dst.rearrange("a j (g p) -> (a j g) p", p=P)
                                act.dma_start(dst, stat_r[rows, :]).then_inc(stat_out, 16)
                        if h == 6 and s == 4:
                            root(r_b[0], 1)
                            root(r_b[1], 2)
                        if h == 8 and s == 0:
                            upper_y(2 * KC, 3 * KC)
                        if h == 8 and 2 <= s < 5:
                            upper(OUT + 1, (s - 2,))
                def root_third(half):
                    hold(act, ss_made, l * 3 + 2 + half)
                    act.activation(r_b[2][:, half * HALF:(half + 1) * HALF], misc[:, half, 0:HALF], ACT.Sqrt,
                                   scale=2.0 / D_LRU, bias=eps[:, :]).then_inc(r_ready, 1)

                root_third(0)
                head_side(7, 8)
                root_third(1)
                upper_y(G + HEADS, KT)
                upper(OUT + 1, (3,), more=3)

                def out_tile(j, last=False, first=False):
                    if not last and not first:
                        upper(OUT + 1 + j, range(4))
                    square(l * SQ_U + KT + 1 + j, xy[:, j, :] if isinstance(j, int)
                           else xy[:, bass.ds(j, 1), :].rearrange("p a n -> p (a n)"),
                           x_new, l * KT + j + 1)
                    act.dma_start(scratch["x_keep"][l + 1, :, j], xy[:, j, :] if isinstance(j, int)
                                  else xy[:, bass.ds(j, 1), :].rearrange("p a n -> p (a n)"))\
                        .then_inc(x_kept, 16)

                out_tile(0, first=True)
                with act.Fori(1, KT - 1) as j:
                    out_tile(j)
                out_tile(KT - 1, True)

            act.wait_ge(ms_ready, DEPTH * 3 + 1)
            act.activation(r_tok[:, 0:4], r_tok[:, 0:4], ACT.Sqrt)
            act.activation(r_tok[0:DEC, 4:5], r_tok[0:DEC, 4:5], ACT.Sqrt)
            act.drain().then_inc(r_ready, 1)

        @block.vector
        def _(dve):
            def tt(o, a, b, op):
                return dve.tensor_tensor(o, a, b, op)

            def stt(o, a, s, b, op0, op1):
                return dve.scalar_tensor_tensor(out=o, in0=a, scalar=s, in1=b, op0=op0, op1=op1)

            dve.memset(eps[:, :], EPS)
            dve.memset(selm[:, 0:P], 0.0)
            dve.drain()
            dve.memset(selm[0:CHUNK, CHUNK:P], NEG)
            dve.wait_ge(vec_made, 1)
            dve.tensor_copy(vec0[:, :], proj[0][:, 0, 0:32]).then_inc(c_row_made, 1)
            dve.wait_ge(c_row_made, 2)
            for a in range(2):
                c = slice(KT * a, KT * a + KT)
                stt(sc[:, :, a], sq[:, c], 1.0, vec0[:, c], ALU.add, ALU.mult)
            dve.drain()
            dve.tensor_scalar(sc[:, :, :], sc[:, :, :], 0.5, None, ALU.mult).then_inc(c_ready, 1)
            for b in range(5):
                n = P if b < 4 else DEC
                for k4 in range(4):
                    e = 4 * b + k4
                    dve.wait_ge(xt_made, e + 1)
                    dve.tensor_copy(xy[:, 4 * k4:4 * k4 + 4, b * P:b * P + n],
                                    misc[:, e % 4, :].rearrange("p (k n) -> p k n", k=4)[:, :, 0:n])\
                        .then_inc(xt_read, 1)
            dve.wait_ge(const_in, CONSTS * 16)
            for n in range(2):
                dve.tensor_scalar(lbf[0:8, 384 + n * P:384 + (n + 1) * P], ones[0:8, :], lbf[0:8, 383:384],
                                  None, ALU.mult)
            dve.drain().then_inc(rel_rows, 1)

            def add_squares(dst, u, a=0, z=T):
                hold(dve, sq_made, u + 1)
                tt(dst[:, a:z], dst[:, a:z], sq[:, a:z], ALU.add)
                dve.drain().then_inc(sq_used, 1)

            def mean_square(ps, dst, n, value):
                hold(dve, ss_made, value)
                dve.tensor_scalar(halves(dst), wide(ps), 1.0 / n, EPS, ALU.mult, ALU.add)
                dve.drain()
                dve.reciprocal(dst, dst)
                dve.drain().then_inc(ms_ready, 1)

            with dve.Fori(0, DEPTH) as l:
                hold(dve, vec_made, l + 2)
                dve.tensor_copy(vec1[:, :], t_ps[:, 0:P])
                dve.tensor_copy(vec2[:, :], o_ps[:, 0:48])
                dve.drain().then_inc(vec_ready, 1)
                dve.tensor_scalar(hg[:, :], vec2[:, 0:KT], 0.5, None, ALU.mult)
                dve.tensor_scalar(hb[:, :, :], vec1[:, V1["b_rg"]:V1["lam"]]
                                  .rearrange("p (a g) -> p a g", a=2), 0.5, None, ALU.mult)

                def read_modulation(j, n):
                    hold(dve, ada_used, (l * ADA_BLOCKS + j + 1) * 4)
                    hold(dve, ada_turned, l * ADA_BLOCKS + j - 1)
                    dve.tensor_copy(ada_row[n], s_ps[n][0:2, :]).then_inc(ada_read, 1)

                with dve.Fori(0, 2) as i:
                    for n in range(2):
                        read_modulation(2 * i + n, n)
                e_, z_, z2, p_, m_ = (sp_[:, n, :] for n in range(5))
                hold(dve, lam_exp, l + 1)
                dve.tensor_scalar(z_, e_, 2.0, None, ALU.add)
                dve.tensor_scalar(m_, vec1[:, V1["lam"]:], -1.0, 0.0, ALU.mult, ALU.max)
                dve.drain()
                dve.reciprocal(z_, z_)
                dve.drain()
                tt(z_, z_, e_, ALU.mult)
                dve.drain()
                tt(z2, z_, z_, ALU.mult)
                dve.drain()
                dve.tensor_scalar(p_, z2, 1.0 / 17, 1.0 / 15, ALU.mult, ALU.add)
                dve.drain()
                for n in (13, 11, 9, 7, 5, 3, 1):
                    tt(p_, p_, z2, ALU.mult)
                    dve.drain()
                    dve.tensor_scalar(p_, p_, 1.0 / n, None, ALU.add)
                    dve.drain()
                stt(p_, z_, 2.0, p_, ALU.mult, ALU.mult)
                dve.drain()
                tt(p_, p_, m_, ALU.add)
                dve.drain()
                dve.tensor_scalar(sp_[:, 4, :], p_, 2.0, None, ALU.mult)
                dve.tensor_scalar(sp_[:, 5, :], p_, -4.0, None, ALU.mult)
                mean_square(proj[0], r_x, D_MODEL, l * 3 + 1)
                for j in range(4, 6):
                    read_modulation(j, j % 2)
                hold(dve, x_kept, 64 + l * KT * 16)
                hold(dve, r_ready, l * 5 + 1)
                for k in range(KT):
                    tt(xy[:, k, :], xy[:, k, :], r_x, ALU.mult)
                for j in range(6, GATE):
                    read_modulation(j, j % 2)

                made = t_ps[:, 0:2 * ADA].rearrange("p (j a) -> p j a", a=2)

                def add_bias(j0, j1):
                    hold(dve, ada_turned, l * ADA_BLOCKS + j1 * P // AB)
                    for a in range(2):
                        tt(mod[:, j0:j1, a], made[:, j0:j1, a], vec1[:, j0:j1], ALU.add)
                    dve.drain().then_inc(mod_ready, 1)

                add_bias(0, 2 * KT)
                for a in range(2):
                    stt(mod[:, KT:2 * KT, a], mod[:, KT:2 * KT, a], 1.0,
                        vec1[:, V1["g_norm"]:V1["g_norm"] + KT], ALU.add, ALU.mult)
                dve.drain()
                read_modulation(GATE, 0)

                def lower(k, base):
                    hold(dve, h_split, l * 2 * KT + base + k + 1)
                    tt(act_lo[:, k, :], xy[:, k, :], act_hi[:, k, :].bitcast(F32), ALU.subtract)\
                        .then_inc(h_low_v, 1)

                for k in range(KT):
                    for a, z, w in PARTS:
                        dve.tensor_scalar(xy[:, k, a:z], xy[:, k, a:z], mod[:, KT + k, w:w + 1],
                                          mod[:, k, w:w + 1], ALU.mult, ALU.add)
                    dve.drain().then_inc(norm_x, 1)
                    if k % 2 and k > 1:
                        lower(k - 2, 0)
                lower(KT - 1, 0)
                for j in range(GATE + 1, ADA_BLOCKS):
                    read_modulation(j, j % 2)
                add_bias(2 * KT, ADA)
                dve.drain()
                dve.memset(lb[0][:, 0:3], 0.0)
                dve.memset(lb[0][:, S0 + 3 + DEC:W + 4], 0.0)
                dve.memset(lb[0][:, S0:S0 + 3], 0.0)
                dve.drain().then_inc(pad_ready, 1)
                dve.memset(sqb[:, :, :], 0.0)
                dve.memset(acc[:, :], 0.0)

                def rotate(n, raw_parts, rot, b):
                    hold(dve, swapped, l * 17 + n + 1)
                    rows = rot.shape[0]
                    tt(halves(rot), wide(proj[b])[0:rows], halves(rope[0:rows, 1, :]), ALU.mult)
                    dve.drain().then_inc(bank_free[b], 1)
                    for x, a, z in raw_parts:
                        tt(x, x, rope[0:rows, 0, a:z], ALU.mult)
                    dve.drain()

                hold(dve, rope_in, (2 * l + 1) * 16)
                rotate(0, [(qi_raw[0:64, :], 0, T)], qi_rot[0:64, :], 0)
                tt(qi_raw[0:64, :], qi_raw[0:64, :], qi_rot[0:64, :], ALU.add)
                dve.drain().then_inc(roped, 1)

                def query(q, b, first=False):
                    if not first:
                        hold(dve, idx_made, l * 64 + 8 * q)
                    rotate(q + 1, [(qi_raw[:, :], 0, T)], qi_rot[:, :], b)
                    tt(qi_rot[:, :], qi_rot[:, :], qi_raw[:, :], ALU.add)
                    dve.drain().then_inc(roped, 1)

                def add_scores(q):
                    for e, (b, hh) in enumerate((b, hh) for b in (1, 2, 3, 4) for hh in range(2)):
                        hold(dve, idx_read, l * 64 + 8 * q + e + 1)
                        a = acc[0:NQ[b], ACC[b]:ACC[b] + NK[b]]
                        stt(a, relu[e % 4][0:NQ[b], 0:NK[b]],
                            kw_tok[0:NQ[b], b, bass.ds(IDX_DIM + 2 * q + hh, 1)], a, ALU.mult, ALU.add)\
                            .then_inc(relu_used, 1)
                        if hh == 0:
                            dve.drain()

                hold(dve, t_read, l * T_EV + 2)
                query(0, 1, True)
                add_scores(0)
                with dve.Fori(0, 3) as it:
                    query(2 * it + 1, 0)
                    add_scores(2 * it + 1)
                    query(2 * it + 2, 1)
                    add_scores(2 * it + 2)
                query(7, 0)
                add_scores(7)
                dve.drain()
                for b in (1, 2, 3):
                    end = ACC[b] + NK[b]
                    dve.memset(acc[0:CHUNK, end - CHUNK:end], NEG)
                dve.drain()

                def best(blocks, rows):
                    for n, b in enumerate(blocks):
                        dve.max(top8[0:rows, n, :], acc[0:rows, ACC[b]:ACC[b] + NK[b]])
                    dve.drain()
                    for n, b in enumerate(blocks):
                        a = acc[0:rows, ACC[b]:ACC[b] + NK[b]]
                        dve.match_replace(a, top8[0:rows, n, :], a, TAKEN)
                    dve.drain()

                def col(v, base, g):
                    return v[:, bass.ds(base + g, 1)]

                def convolve(g):
                    state = vec2[:, V2["state_conv"]:V2["state_conv"] + 3 * G]\
                        .rearrange("p (j g) -> p j g", g=G)
                    dve.tensor_copy(lb[0][:, S0:S0 + 3], state[:, :, bass.ds(g, 1)]
                                    .rearrange("p j a -> p (j a)"))
                    hold(dve, evac, l * OUT + LRU + 2 * g + 1)
                    dve.drain()
                    x, y = lb[0], lb[1][:, 0:W]
                    dve.tensor_copy(stat[:, 0:3, bass.ds(g, 1)].rearrange("p j a -> p (j a)"),
                                    x[:, SEQ:SEQ + 3])
                    dve.tensor_copy(stat[:, 4:7, bass.ds(g, 1)].rearrange("p j a -> p (j a)"),
                                    x[:, S0 + DEC:S0 + DEC + 3])
                    dve.tensor_scalar(y, x[:, 0:W], col(vec1, V1["conv_w"], g), col(vec1, V1["conv_b"], g),
                                      ALU.mult, ALU.add)
                    for j in range(1, CONV_W):
                        dve.drain()
                        stt(y, x[:, j:j + W], col(vec1, V1["conv_w"] + j * G, g), y, ALU.mult, ALU.add)
                    dve.drain().then_inc(conv_ready, 1)

                def gate_path(t, b, dst):
                    hold(dve, evac, l * OUT + t + 1)
                    stt(halves(dst), halves(z_t[:, :]), 1.0, wide(proj[b]), ALU.add, ALU.mult)
                    dve.drain().then_inc(bank_free[b], 1)
                    dve.drain().then_inc(zs_ready, 1)

                def tile(v, j):
                    if isinstance(j, int):
                        return v[:, j, :]
                    return v[:, bass.ds(j, 1), :].rearrange("p a n -> p (a n)")

                def recur(g):
                    hold(dve, root_made, l * G + g + 1)
                    x, s, ti, t, a = (lb[n][:, 0:W] for n in (1, 2, 3, 4, 5))
                    stt(s, a, 1.0, s, ALU.add, ALU.mult)
                    stt(t, a, 1.0, t, ALU.add, ALU.mult)
                    stt(ti, ti, 1.0, x, ALU.add, ALU.mult)
                    dve.drain()
                    dve.tensor_scalar(a, t, -1.0, 1.0, ALU.mult, ALU.add)
                    stt(s, s, 0.5, ti, ALU.mult, ALU.mult)
                    dve.drain()
                    dve.tensor_tensor_scan(t[:, 0:SEQ], a[:, 0:SEQ], s[:, 0:SEQ], 0.0, ALU.mult, ALU.add)
                    dve.tensor_tensor_scan(t[:, S0:S0 + DEC], a[:, S0:S0 + DEC], s[:, S0:S0 + DEC],
                                           col(vec2, V2["state_lru"], g), ALU.mult, ALU.add)
                    dve.drain().then_inc(hs_ready, 1)
                    dve.tensor_copy(stat[:, 3, bass.ds(g, 1)], t[:, SEQ - 1:SEQ])
                    dve.tensor_copy(stat[:, 7, bass.ds(g, 1)], t[:, S0 + DEC - 1:S0 + DEC])
                    y = tile(xy, g)
                    for a_, z_, at_ in ((0, SEQ, 0), (SEQ, T, S0)):
                        stt(y[:, a_:z_], t[:, at_:at_ + z_ - a_], col(hg, 0, g), y[:, a_:z_],
                            ALU.mult, ALU.mult)
                    add_squares(sqb[:, 0, :], l * SQ_U + g)

                def recurrent_block(g, first=False):
                    if not first:
                        recur(g - 1)
                    convolve(g)
                    for _ in range(2):
                        best((1, 2, 3), P)
                    gate_path(LRU + 1 + 2 * g, 0, tile(xy, g))

                recurrent_block(0, True)
                with dve.Fori(1, G) as g:
                    recurrent_block(g)

                def head_side(h, s):
                    def logits(b):
                        turned = t_no(h - 1, 7) if b < 2 else t_no(h, {2: 2, 3: 3, 4: 5}[b])
                        hold(dve, t_made, l * T_EV + turned + 1)
                        hold(dve, s_made, l * 40 + 5 * h + b + 1)
                        if h >= HEADS:
                            mask = selm[0:NQ[b], SEL[b]:SEL[b] + NK[b]]
                        elif b < 4:
                            mask = bias[:, 0:NK[b]][:, ::-1]
                        else:
                            mask = bias[0:DEC, CHUNK:CHUNK + NS][:, ::-1]
                        x = s_sb[b % 2][0:NQ[b], 0:NK[b]]
                        stt(x, s_ps[b % 2][0:NQ[b], 0:NK[b]], -SCALE, mask, ALU.mult, ALU.subtract)
                        dve.drain().then_inc(s_read, 1)
                        dve.tensor_reduce(nmx[0:NQ[b], b % 2:b % 2 + 1], x, AX.X, ALU.min)
                        dve.drain().then_inc(y_neg, 1)

                    def normalise(b):
                        hold(dve, exp_made, l * 40 + 5 * h + b + 1)
                        r = rinv[0:NQ[b], b % 2:b % 2 + 1]
                        dve.reciprocal(r, rsum[0:NQ[b], b % 2:b % 2 + 1])
                        dve.drain()
                        x = s_sb[b % 2][0:NQ[b], 0:NK[b]]
                        dve.tensor_scalar(x, x, r, None, ALU.mult)
                        dve.drain().then_inc(p_ready, 1)

                    if s == 0:
                        if h < HEADS:
                            hold(dve, bias_in, (l * HEADS + h + 1) * 16)
                        logits(0)
                        logits(1)
                        normalise(0)
                        normalise(1)
                    elif s in (2, 3, 5):
                        b = {2: 2, 3: 3, 5: 4}[s]
                        logits(b)
                        normalise(b)
                    elif s in (7, 8):
                        a, z = (0, SEQ) if s == 7 else (SEQ, T)
                        hold(dve, o_made, l * 40 + 5 * h + s - 3)
                        y = xy[:, G + h, a:z]
                        stt(y, o_ps[:, 0:z - a], hg[:, G + h:G + h + 1], y, ALU.mult, ALU.mult)
                        dve.drain().then_inc(o_read_v, 1)
                        if h == 7:
                            add_squares(sqb[:, 2, :], l * SQ_U + G + s, a, z)
                        elif s == 8:
                            add_squares(sqb[:, 1 + h // HEADS, :], l * SQ_U + G + h)

                def invert_rms(half):
                    hold(dve, r_ready, l * 5 + 4 + half)
                    r = r_b[2][:, half * HALF:(half + 1) * HALF]
                    dve.reciprocal(r, r)
                    dve.drain()

                def norm_branches(j0, j1):
                    for j in range(j0, j1):
                        n = 0 if j < G else 1 if j < G + HEADS else 2
                        if j in (0, G):
                            hold(dve, r_ready, l * 5 + 2 + n)
                        tt(xy[:, j, :], xy[:, j, :], r_b[n], ALU.mult).then_inc(norm_x, 1)

                for h in range(9):
                    for s in range(8):
                        t = HEAD + 4 * h + s // 2
                        if h == 0 and s == 1:
                            recur(G - 1)
                            dve.drain().then_inc(stat_ready, 1)
                        if h == 0 and s == 3:
                            for _ in range(TOPK_S // 8):
                                best((4,), DEC)
                            for b in (1, 2, 3, 4):
                                dve.tensor_scalar(selm[0:NQ[b], SEL[b]:SEL[b] + NK[b]],
                                                  acc[0:NQ[b], ACC[b]:ACC[b] + NK[b]],
                                                  0.5 * TAKEN, NEG, ALU.is_gt, ALU.mult)
                            dve.drain()
                        if h == 6 and s < 4:
                            hold(dve, t_made, l * T_EV + t_no(5, s))
                            r = r_b[s // 2]
                            dve.tensor_scalar(r[:, s % 2 * HALF:][:, 0:HALF], t_ps[:, 0:HALF],
                                              1.0 / (D_LRU, D_LRU // 2)[s // 2], EPS, ALU.mult, ALU.add)
                            dve.drain().then_inc(t_read, 1)
                            if s % 2:
                                dve.reciprocal(r, r)
                                dve.drain().then_inc(ms_ready, 1)
                        if HEADS <= h < 8 and s in (2, 4):
                            part = s // 2 - 1
                            x = (q_t if part == 0 else k_t)[h % 2][0:32]
                            parts = [(x, 0, T)] if part == 0 else \
                                [(x[:, 0:SEQ], 0, SEQ), (x[:, NEW_K:KEYS], SEQ, T)]
                            hold(dve, rope_in, (2 * l + 2) * 16)
                            rotate(9 + 2 * (h - HEADS) + part, parts, d_rot[0:32, 0:T], (t - 1) % 2)
                            for y, a, z in parts:
                                tt(y, y, d_rot[0:32, a:z], ALU.add)
                            dve.drain().then_inc(roped, 1)
                        if h > 1 and s == 0:
                            head_side(h - 2, 8)
                        if h > 0:
                            head_side(h - 1, s)
                        if h == 7 and s == 7:
                            for j in range(1, 2 * KC, 2):
                                lower(j, KT)
                        if h < 8 and s == 7:
                            gate_path(t, t % 2, xy[:, G + h, :])
                        if h == 7 and s < 6:
                            norm_branches(2 * s, 2 * s + 2)
                        if h == 8 and s == 1:
                            for j in range(2 * KC + 1, 3 * KC, 2):
                                lower(j, KT)
                head_side(7, 8)
                invert_rms(0)
                invert_rms(1)
                norm_branches(G + HEADS, KT)
                lower(KT - 3, KT)
                lower(KT - 1, KT)
                dve.memset(sqx, 0.0)

                def out_tile(j, jj, s, first=False):
                    b = (OUT + s) % 2
                    hold(dve, chunks_used, chunk_no(l, OUT + j, 4) + (3 if first else 0))
                    hold(dve, old_in[s], (l * 4 + jj + 1) * 16)
                    x = tile(xy, j)
                    for half, a, z, w in ((0, 0, HALF, 0), (1, HALF, SEQ, 0), (1, SEQ, T, 1)):
                        gate = mod[:, 2 * KT + j, w:w + 1] if isinstance(j, int) else \
                            mod[:, bass.ds(2 * KT + j, 1), w:w + 1].rearrange("p a n -> p (a n)")
                        stt(x[:, a:z], proj[b][:, half, a - half * HALF:z - half * HALF], gate,
                            x_old[s][:, a:z], ALU.mult, ALU.add)
                    dve.drain().then_inc(bank_free[b], 1)
                    dve.drain().then_inc(x_new, 1)
                    add_squares(sqx, l * SQ_U + KT + 1 + j)

                for s in range(4):
                    out_tile(s, 0, s, first=s == 0)
                with dve.Fori(1, 4) as jj:
                    for s in range(4):
                        out_tile(4 * jj + s, jj, s)
                dve.drain().then_inc(x_whole, 1)

            dve.wait_ge(ss_made, DEPTH * 3 + 1)
            tokens = ((slice(0, P), slice(0, 4)), (slice(0, DEC), slice(4, 5)))
            for p, c in tokens:
                dve.tensor_scalar(r_tok[p, c], proj[0][p, 0, c], 1.0 / D_MODEL, EPS, ALU.mult, ALU.add)
            dve.drain()
            for p, c in tokens:
                dve.reciprocal(r_tok[p, c], r_tok[p, c])
            dve.drain().then_inc(ms_ready, 1)
            dve.wait_ge(g_in, 16)
            dve.wait_ge(r_ready, DEPTH * 5 + 1)
            for b in range(5):
                n = P if b < 4 else DEC
                if b > 1:
                    dve.wait_ge(y_out[b % 2], 16 * (b // 2))
                for k4 in range(4):
                    e, cols = 4 * b + k4, slice(512 * k4, 512 * k4 + 512)
                    dve.wait_ge(yt_made, e + 1)
                    stt(y_row[b % 2][0:n, cols], misc[0:n, e % 4, :], r_tok[0:n, b:b + 1], g_row[0:n, cols],
                        ALU.mult, ALU.mult).then_inc(yt_read, 1)


_INS = ["x_prompt", "x_sample", "c_prompt", "c_sample", "state_conv", "state_lru", "cache_band_k",
        "cache_band_v", "cache_dsa_k", "cache_dsa_v", "cache_dsa_idx_k", "g_norm", "w_ada", "b_ada",
        "w_in", "conv_w", "conv_b", "w_rg", "b_rg", "w_ig", "b_ig", "lru_lambda", "rel_bias",
        "g_branch", "w_out", "g_final"]
_OUTS = {
    "y_prompt": (1, SEQ, D_MODEL), "y_sample": (1, DEC, D_MODEL),
    "p_conv": (DEPTH, 1, CONV_W - 1, D_LRU), "p_lru": (DEPTH, 1, D_LRU),
    "p_band_k": (DEPTH, 1, SEQ, HEADS, HD), "p_band_v": (DEPTH, 1, SEQ, HEADS, HD),
    "p_dsa_k": (DEPTH, 1, SEQ, HEADS, HD), "p_dsa_v": (DEPTH, 1, SEQ, HEADS, HD),
    "p_dsa_idx_k": (DEPTH, 1, SEQ, IDX_DIM),
    "s_conv": (DEPTH, 1, CONV_W - 1, D_LRU), "s_lru": (DEPTH, 1, D_LRU),
    "s_band_k": (DEPTH, 1, DEC, HEADS, HD), "s_band_v": (DEPTH, 1, DEC, HEADS, HD),
    "s_dsa_k": (DEPTH, 1, DEC, HEADS, HD), "s_dsa_v": (DEPTH, 1, DEC, HEADS, HD),
    "s_dsa_idx_k": (DEPTH, 1, DEC, IDX_DIM),
}


def _rotary(rows, group, width):
    pos = np.concatenate([np.arange(SEQ), PAST + np.arange(DEC)]).astype(np.float32)
    half = width // 2
    inv = np.float32(ROPE_THETA) ** (-np.arange(half, dtype=np.float32) / np.float32(half))
    ang = pos[None] * inv[:, None].astype(np.float32)
    table = np.zeros((rows, 2, T), np.float32)
    table[:, 0] = 1
    for r in range(0, rows, group):
        table[r:r + half, 0] = table[r + half:r + width, 0] = np.cos(ang)
        table[r:r + half, 1] = -np.sin(ang)
        table[r + half:r + width, 1] = np.sin(ang)
    return table


def _swaps(rows, group, width):
    m = np.zeros((rows, rows), np.float32)
    for r in range(0, rows, group):
        for n in range(width):
            m[r + n, r + (n + width // 2) % width] = 1
    return m


def _constants():
    return {
        "ident": np.eye(P, dtype=np.float32), "ones": np.ones((P, P), np.float32),
        "swap_i": _swaps(P, 64, 16), "swap_d": _swaps(32, 32, 32),
        "blocked": np.full((8, CHUNK, CHUNK), NEG, np.float32),
        "rope_i": _rotary(P, 64, 16), "rope_d": _rotary(32, 32, 32),
    }


def kernel(**inputs):
    import concourse.bacc as bacc
    from concourse.bass_utils import run_bass_kernel_spmd

    nc = bacc.Bacc("TRN2", target_bir_lowering=False, num_devices=1)
    arrays, ins, outs = {}, {}, {}
    for name in _INS:
        arrays[f"in_{name}"] = np.ascontiguousarray(inputs[name])
    for name, a in _constants().items():
        arrays[f"in_{name}"] = a
    for name, a in arrays.items():
        ins[name[3:]] = nc.dram_tensor(name, a.shape, mybir.dt.from_np(a.dtype), kind="ExternalInput").ap()
    for name, shape in _OUTS.items():
        outs[name] = nc.dram_tensor(f"out_{name}", shape, F32, kind="ExternalOutput").ap()
    scratch = {
        "rows": nc.dram_tensor("rel_rows", (8, 640), F32, kind="Internal").ap(),
        "windows": nc.dram_tensor("rel_windows", (8, P, 512), F32, kind="Internal").ap(),
        "x_keep": nc.dram_tensor("x_keep", (DEPTH + 1, P, KT, T), F32, kind="Internal").ap(),
    }
    build(nc, ins, outs, scratch)
    r = run_bass_kernel_spmd(nc, [arrays], core_ids=[0])
    return tuple(r.results[0][f"out_{name}"] for name in _OUTS)
```
